# Optimizing a Trainium2 kernel written in Bass

```python
import math
import jax
import jax.numpy as jnp
from jax import lax
import numpy as np

D_MODEL = 1024
BATCH = 1
SEQ = 512
DEPTH = 2

GRID_W = 64
CTX_LEN = 256
ROPE_THETA = 10000.0
Q_BLOCK = 128
EPS = 1e-6

CHUNK = 128
A_GROUPS = 4
A_GROUP_DIM = D_MODEL // 8
D_A = A_GROUPS * A_GROUP_DIM
B_HEADS = 8
B_KV_HEADS = 2
B_HEAD_DIM = 128
EV_A_END = 2 * D_A
EV_Q_END = EV_A_END + B_HEADS * B_HEAD_DIM
EV_K_END = EV_Q_END + B_KV_HEADS * B_HEAD_DIM
EV_IN = EV_K_END + B_KV_HEADS * B_HEAD_DIM
EV_OUT = D_A + B_HEADS * B_HEAD_DIM

D_C = D_MODEL // 2
CONV_W = 31
MLA_HEADS = 8
MLA_NOPE = 128
MLA_ROPE = 64
MLA_V = 128
Q_LORA = D_MODEL // 2
KV_LORA = D_MODEL // 4
OD_C_END = 2 * D_C
OD_Q_END = OD_C_END + Q_LORA
OD_IN = OD_Q_END + KV_LORA + MLA_ROPE
OD_OUT = D_C + MLA_HEADS * MLA_V

D_FF = 2816
FFN_CONV_W = 3

kernel_name = "hybrid_gmlp_gqa_conformer_mla_convffn_dit"

def rmsnorm(x, g):
    xf = x.astype(jnp.float32)
    y = xf * lax.rsqrt(jnp.mean(xf * xf, axis=-1, keepdims=True) + EPS)
    return (y * g.astype(jnp.float32)).astype(x.dtype)

def layernorm(x, g, b):
    xf = x.astype(jnp.float32)
    mu = jnp.mean(xf, axis=-1, keepdims=True)
    xc = xf - mu
    y = xc * lax.rsqrt(jnp.mean(xc * xc, axis=-1, keepdims=True) + EPS)
    return (y * g.astype(jnp.float32) + b.astype(jnp.float32)).astype(x.dtype)

def dwconv(x, w, b):
    k = w.shape[0]
    y = lax.conv_general_dilated(
        x, w[:, None, :].astype(x.dtype), window_strides=(1,),
        padding=[(k // 2, k // 2)], dimension_numbers=('NWC', 'WIO', 'NWC'),
        feature_group_count=x.shape[-1])
    return y + b.astype(x.dtype)

def axial_rope_tables(row, col, d_rot):
    n_freq = d_rot // 4
    freq = ROPE_THETA ** (-jnp.arange(n_freq, dtype=jnp.float32) / n_freq)
    ang = jnp.concatenate([row[:, None] * freq, col[:, None] * freq], axis=-1)
    return jnp.cos(ang), jnp.sin(ang)

def apply_rope(x, cos, sin):
    b, n, h, d = x.shape
    xp = x.reshape(b, n, h, d // 2, 2)
    x0, x1 = xp[..., 0], xp[..., 1]
    cs = cos[None, :, None, :].astype(x.dtype)
    sn = sin[None, :, None, :].astype(x.dtype)
    return jnp.stack([x0 * cs - x1 * sn, x0 * sn + x1 * cs], axis=-1).reshape(b, n, h, d)

def block_attention(q, k, v, scale):
    b, n, g, r, dq = q.shape
    nb = n // Q_BLOCK
    qb = jnp.moveaxis(q.reshape(b, nb, Q_BLOCK, g, r, dq), 1, 0)

    def one_block(q_blk):
        s = jnp.einsum('bqgrd,bkgd->bgrqk', q_blk, k, preferred_element_type=jnp.float32) * scale
        p = jax.nn.softmax(s, axis=-1).astype(v.dtype)
        return jnp.einsum('bgrqk,bkgd->bqgrd', p, v)

    o = lax.map(one_block, qb)
    return jnp.moveaxis(o, 0, 1).reshape(b, n, g * r * v.shape[-1])

def spatial_gating(z, ln_g, ln_b, w_s, b_s):
    z = jax.nn.gelu(z)
    u, v = jnp.split(z, 2, axis=-1)
    v = layernorm(v, ln_g, ln_b)
    b, n, _ = v.shape
    vb = v.reshape(b, n // CHUNK, CHUNK, A_GROUPS, A_GROUP_DIM)
    s = jnp.einsum('gpq,bnqgd->bnpgd', w_s, vb) + b_s.T[:, :, None]
    return u * s.reshape(b, n, D_A)

def conformer_conv(z, conv_w, conv_b, ln_g, ln_b):
    a, gt = jnp.split(z, 2, axis=-1)
    h = dwconv(a * jax.nn.sigmoid(gt), conv_w, conv_b)
    return jax.nn.silu(layernorm(h, ln_g, ln_b))

def mla_q(z_q, g_cq, w_uq, cos, sin):
    b, n, _ = z_q.shape
    q = (rmsnorm(z_q, g_cq) @ w_uq).reshape(b, n, MLA_HEADS, MLA_NOPE + MLA_ROPE)
    if cos is None:
        return q
    return jnp.concatenate([q[..., :MLA_NOPE], apply_rope(q[..., MLA_NOPE:], cos, sin)], axis=-1)

def mla_kv(z_kv, g_ckv, w_ukv, cos, sin):
    b, n, _ = z_kv.shape
    kv = (rmsnorm(z_kv[..., :KV_LORA], g_ckv) @ w_ukv).reshape(b, n, MLA_HEADS, MLA_NOPE + MLA_V)
    k_rope = z_kv[..., KV_LORA:].reshape(b, n, 1, MLA_ROPE)
    if cos is not None:
        k_rope = apply_rope(k_rope, cos, sin)
    k = jnp.concatenate([kv[..., :MLA_NOPE], jnp.broadcast_to(k_rope, (b, n, MLA_HEADS, MLA_ROPE))], axis=-1)
    return k, kv[..., MLA_NOPE:]

def even_mixer(h_lat, h_ctx, w_in, a_ln, w_s, b_s, qk_g, w_out, cos, sin, with_ctx_out):
    b, n, _ = h_lat.shape
    l = h_ctx.shape[1]
    rep = B_HEADS // B_KV_HEADS
    scale = B_HEAD_DIM ** -0.5
    kvw = B_KV_HEADS * B_HEAD_DIM
    zc_kv = h_ctx @ w_in[:, EV_Q_END:]
    k_ctx = rmsnorm(zc_kv[..., :kvw].reshape(b, l, B_KV_HEADS, B_HEAD_DIM), qk_g[1])
    v_ctx = zc_kv[..., kvw:].reshape(b, l, B_KV_HEADS, B_HEAD_DIM)
    z = h_lat @ w_in
    a_lat = spatial_gating(z[..., :EV_A_END], a_ln[0], a_ln[1], w_s, b_s)
    q = apply_rope(rmsnorm(z[..., EV_A_END:EV_Q_END].reshape(b, n, B_HEADS, B_HEAD_DIM), qk_g[0]), cos, sin)
    k = apply_rope(rmsnorm(z[..., EV_Q_END:EV_K_END].reshape(b, n, B_KV_HEADS, B_HEAD_DIM), qk_g[1]), cos, sin)
    v = z[..., EV_K_END:].reshape(b, n, B_KV_HEADS, B_HEAD_DIM)
    att = block_attention(q.reshape(b, n, B_KV_HEADS, rep, B_HEAD_DIM),
                          jnp.concatenate([k_ctx, k], axis=1), jnp.concatenate([v_ctx, v], axis=1), scale)
    o_lat = jnp.concatenate([a_lat, att], axis=-1) @ w_out
    if not with_ctx_out:
        return o_lat, None
    zc = h_ctx @ w_in[:, :EV_Q_END]
    a_ctx = spatial_gating(zc[..., :EV_A_END], a_ln[0], a_ln[1], w_s, b_s)
    q_ctx = rmsnorm(zc[..., EV_A_END:].reshape(b, l, B_HEADS, B_HEAD_DIM), qk_g[0])
    att_ctx = block_attention(q_ctx.reshape(b, l, B_KV_HEADS, rep, B_HEAD_DIM), k_ctx, v_ctx, scale)
    o_ctx = jnp.concatenate([a_ctx, att_ctx], axis=-1) @ w_out
    return o_lat, o_ctx

def odd_mixer(h_lat, h_ctx, w_in, conv_w, conv_b, c_ln, g_cq, g_ckv, w_uq, w_ukv, w_out, cos, sin, with_ctx_out):
    scale = (MLA_NOPE + MLA_ROPE) ** -0.5
    k_ctx, v_ctx = mla_kv(h_ctx @ w_in[:, OD_Q_END:], g_ckv, w_ukv, None, None)
    z = h_lat @ w_in
    c_lat = conformer_conv(z[..., :OD_C_END], conv_w, conv_b, c_ln[0], c_ln[1])
    q = mla_q(z[..., OD_C_END:OD_Q_END], g_cq, w_uq, cos, sin)
    k, v = mla_kv(z[..., OD_Q_END:], g_ckv, w_ukv, cos, sin)
    att = block_attention(q[:, :, :, None, :], jnp.concatenate([k_ctx, k], axis=1),
                          jnp.concatenate([v_ctx, v], axis=1), scale)
    o_lat = jnp.concatenate([c_lat, att], axis=-1) @ w_out
    if not with_ctx_out:
        return o_lat, None
    zc = h_ctx @ w_in[:, :OD_Q_END]
    c_ctx_o = conformer_conv(zc[..., :OD_C_END], conv_w, conv_b, c_ln[0], c_ln[1])
    q_ctx = mla_q(zc[..., OD_C_END:], g_cq, w_uq, None, None)
    att_ctx = block_attention(q_ctx[:, :, :, None, :], k_ctx, v_ctx, scale)
    o_ctx = jnp.concatenate([c_ctx_o, att_ctx], axis=-1) @ w_out
    return o_lat, o_ctx

def conv_ffn(h, w_in, conv_w, conv_b, w_out):
    z = h @ w_in
    g = dwconv(z[..., :D_FF], conv_w, conv_b)
    return (jax.nn.silu(g) * z[..., D_FF:]) @ w_out

def setup_inputs(seed: int = 0) -> dict:
    key = jax.random.key(seed)
    ks = iter(jax.random.split(key, 40))
    ne, no = (DEPTH + 1) // 2, DEPTH // 2

    def nrm(shape, scale):
        return jax.random.normal(next(ks), shape, jnp.float32) * scale

    def gain(shape):
        return 1.0 + nrm(shape, 0.05)

    return dict(
        x=nrm((BATCH, SEQ, D_MODEL), 1.0),
        c=nrm((BATCH, D_MODEL), 1.0),
        ctx=nrm((BATCH, CTX_LEN, D_MODEL), 1.0),
        c_ctx=nrm((D_MODEL,), 1.0),
        mod_w=nrm((DEPTH, D_MODEL, 6 * D_MODEL), 0.5 * D_MODEL ** -0.5),
        mod_b=nrm((DEPTH, 6 * D_MODEL), 0.02),
        norm_g=gain((DEPTH, 4, D_MODEL)),
        ffn_w_in=nrm((DEPTH, D_MODEL, 2 * D_FF), D_MODEL ** -0.5),
        ffn_conv_w=nrm((DEPTH, FFN_CONV_W, D_FF), FFN_CONV_W ** -0.5),
        ffn_conv_b=nrm((DEPTH, D_FF), 0.02),
        ffn_w_out=nrm((DEPTH, D_FF, D_MODEL), D_FF ** -0.5),
        ev_w_in=nrm((ne, D_MODEL, EV_IN), D_MODEL ** -0.5),
        ev_a_ln=jnp.stack([gain((ne, D_A)), nrm((ne, D_A), 0.02)], axis=1),
        ev_w_s=nrm((ne, A_GROUPS, CHUNK, CHUNK), CHUNK ** -0.5),
        ev_b_s=1.0 + nrm((ne, A_GROUPS, CHUNK), 0.1),
        ev_qk_g=gain((ne, 2, B_HEAD_DIM)),
        ev_w_out=nrm((ne, EV_OUT, D_MODEL), EV_OUT ** -0.5),
        od_w_in=nrm((no, D_MODEL, OD_IN), D_MODEL ** -0.5),
        od_conv_w=nrm((no, CONV_W, D_C), CONV_W ** -0.5),
        od_conv_b=nrm((no, D_C), 0.02),
        od_c_ln=jnp.stack([gain((no, D_C)), nrm((no, D_C), 0.02)], axis=1),
        od_g_cq=gain((no, Q_LORA)),
        od_g_ckv=gain((no, KV_LORA)),
        od_w_uq=nrm((no, Q_LORA, MLA_HEADS * (MLA_NOPE + MLA_ROPE)), Q_LORA ** -0.5),
        od_w_ukv=nrm((no, KV_LORA, MLA_HEADS * (MLA_NOPE + MLA_V)), KV_LORA ** -0.5),
        od_w_out=nrm((no, OD_OUT, D_MODEL), OD_OUT ** -0.5),
    )

def reference(x, c, ctx, c_ctx, mod_w, mod_b, norm_g, ffn_w_in, ffn_conv_w, ffn_conv_b, ffn_w_out,
              ev_w_in, ev_a_ln, ev_w_s, ev_b_s, ev_qk_g, ev_w_out,
              od_w_in, od_conv_w, od_conv_b, od_c_ln, od_g_cq, od_g_ckv, od_w_uq, od_w_ukv, od_w_out):
    n = x.shape[1]
    rows = n // GRID_W
    row = jnp.repeat(jnp.arange(rows, dtype=jnp.float32), GRID_W)
    col = jnp.tile(jnp.arange(GRID_W, dtype=jnp.float32), rows)
    cos_b, sin_b = axial_rope_tables(row, col, B_HEAD_DIM)
    cos_d, sin_d = axial_rope_tables(row, col, MLA_ROPE)
    s_c = jax.nn.silu(c)
    s_cc = jax.nn.silu(c_ctx)
    x_lat, x_ctx = x, ctx
    for layer in range(DEPTH):
        more = layer < DEPTH - 1
        m_lat = jnp.split((s_c @ mod_w[layer] + mod_b[layer])[:, None, :], 6, axis=-1)
        m_ctx = jnp.split(s_cc @ mod_w[layer] + mod_b[layer], 6, axis=-1)
        g_pre1, g_post1, g_pre2, g_post2 = norm_g[layer]
        h_lat = rmsnorm(x_lat, g_pre1) * (1 + m_lat[1]) + m_lat[0]
        h_ctx = rmsnorm(x_ctx, g_pre1) * (1 + m_ctx[1]) + m_ctx[0]
        i = layer // 2
        if layer % 2 == 0:
            o_lat, o_ctx = even_mixer(h_lat, h_ctx, ev_w_in[i], ev_a_ln[i], ev_w_s[i], ev_b_s[i],
                                      ev_qk_g[i], ev_w_out[i], cos_b, sin_b, more)
        else:
            o_lat, o_ctx = odd_mixer(h_lat, h_ctx, od_w_in[i], od_conv_w[i], od_conv_b[i], od_c_ln[i],
                                     od_g_cq[i], od_g_ckv[i], od_w_uq[i], od_w_ukv[i], od_w_out[i],
                                     cos_d, sin_d, more)
        x_lat = x_lat + m_lat[2] * rmsnorm(o_lat, g_post1)
        f_lat = conv_ffn(rmsnorm(x_lat, g_pre2) * (1 + m_lat[4]) + m_lat[3],
                         ffn_w_in[layer], ffn_conv_w[layer], ffn_conv_b[layer], ffn_w_out[layer])
        x_lat = x_lat + m_lat[5] * rmsnorm(f_lat, g_post2)
        if more:
            x_ctx = x_ctx + m_ctx[2] * rmsnorm(o_ctx, g_post1)
            f_ctx = conv_ffn(rmsnorm(x_ctx, g_pre2) * (1 + m_ctx[4]) + m_ctx[3],
                             ffn_w_in[layer], ffn_conv_w[layer], ffn_conv_b[layer], ffn_w_out[layer])
            x_ctx = x_ctx + m_ctx[5] * rmsnorm(f_ctx, g_post2)
    return x_lat


_drawn_inputs = setup_inputs


def setup_inputs(seed=0):
    import zlib

    import numpy as np

    out = dict(_drawn_inputs(seed))
    spreads = {}
    factors = {'ffn_conv_b': 7.616,
     'ev_b_s': 2.799,
     'ev_qk_g': 8.0,
     'od_conv_b': 56.976,
     'od_g_cq': 8.0,
     'od_g_ckv': 6.766,
     'od_conv_w': 3.437,
     'od_c_ln': 4.201}
    for name, (base, spread) in spreads.items():
        noise = np.random.default_rng([zlib.crc32(name.encode()), seed]).standard_normal(out[name].shape)
        drawn = base * np.exp(spread * noise) if base else spread * noise
        out[name] = jnp.asarray(drawn.astype(out[name].dtype))
    for name, factor in factors.items():
        out[name] = (out[name] * factor).astype(out[name].dtype)
    return out
```

```python
from contextlib import ExitStack

import numpy as np

import concourse.bass as bass
from concourse import mybir

P = 128
F32 = mybir.dt.float32
F32R = mybir.dt.float32r
ALU = mybir.AluOpType
ACT = mybir.ActivationFunctionType
AX_X = mybir.AxisListType.X

D = 1024
KD = D // P
LAT, CTX = 512, 256
TOK = LAT + CTX
LT, NT = LAT // P, TOK // P
FF = 2816
JF = FF // P
HEADS = 8
SLOT = 2048
EPS = 1e-6
KIB = 1024

N_EVZ, N_OUT, N_FF1, N_FF2, N_ODZ, N_UQ, N_UKV = 10, 6, JF, 12, 8, 3, 2
EV0 = 0
EVO0 = EV0 + N_EVZ
F10 = EVO0 + N_OUT
F20 = F10 + N_FF1
OD0 = F20 + N_FF2
UQ0 = OD0 + N_ODZ
UKV0 = UQ0 + N_UQ
ODO0 = UKV0 + N_UKV
F11 = ODO0 + N_OUT
F21 = F11 + N_FF1
NSLOT = F21 + N_FF2 + ((F21 + N_FF2) % 2)
MODT = 6 * D // P


def build(nc, x, ctx, cvec, wpack, modw, modb, normg, ffcw, rope_ev, rope_od, qkg, aln, wsT, bs,
          odcw, odcln, gcq, gckv, out):
    es = ExitStack()
    with es:
        base = [16 * KIB + 128]
        uid = [0]

        def at(name, off, shape, dt=F32):
            return nc.alloc_sbuf_tensor_at(name, shape, dt, offset=base[0] + off)

        def sem(name):
            return es.enter_context(nc.semaphore(name))

        R_X, R_HT, R_A = 0, 24 * KIB, 72 * KIB
        R_RAW, R_WH, R_WL, R_MOD, R_GM, R_C = (138 * KIB, 154 * KIB, 170 * KIB, 186 * KIB, 194 * KIB, 202 * KIB)
        X = at("X", R_X, [P, NT, D])
        HTh = at("HTh", R_HT, [P, KD, TOK], F32R)
        HTl = at("HTl", R_HT + 24 * KIB, [P, KD, TOK], F32R)
        w_raw = [at(f"w_raw{i}", R_RAW + i * 8 * KIB, [P, SLOT]) for i in range(2)]
        w_hi = [at(f"w_hi{i}", R_WH + i * 8 * KIB, [P, SLOT], F32R) for i in range(2)]
        w_lo = [at(f"w_lo{i}", R_WL + i * 8 * KIB, [P, SLOT], F32R) for i in range(2)]
        mod_raw = [at(f"mod_raw{i}", R_MOD + i * 4 * KIB, [P, KD, P]) for i in range(2)]
        gmB = at("gmB", R_GM, [P, 2, D])
        c_off = [R_C]

        def const(name, shape, dt=F32):
            n = 4
            for s in shape[1:]:
                n *= s
            t = at(name, c_off[0], shape, dt)
            c_off[0] += (n + 31) // 32 * 32
            assert base[0] + c_off[0] <= nc.sbuf_usable_end, name
            return t

        ident = const("ident", [P, P])
        ones = const("ones", [P, P])
        modc = const("modc", [P, 2, MODT, 2])
        modb_sb = const("modb_sb", [P, 2, MODT])
        ng = const("ng", [P, 2, 4, KD])
        cw = const("cw", [P, 2, JF, 4])
        sT = const("sT", [P, KD, 2])
        prescale = const("prescale", [P, KD, 2])
        gmcol = const("gmcol", [P, KD, 2])
        ssq = const("ssq", [P, 64])
        rstd = const("rstd", [P, 64])
        halfneg = const("halfneg", [P, 64])
        cws = [const(f"cws{i}", [P, 4]) for i in range(2)]
        lnst = at("lnst", R_HT + 44 * KIB, [P, NT, 6])
        lnmv = at("lnmv", R_HT + 45 * KIB, [P, NT, 2])
        rmax = const("rmax", [P, 2, 2])
        rsum = const("rsum", [P, 2, 2])

        xn = at("xn", R_A, [P, NT, D])
        pre_tmp = [at(f"pre_tmp{i}", R_A + (24 + 3 * i) * KIB, [P, TOK]) for i in range(2)]
        junk = at("junk", R_A + 32 * KIB, [P, D])
        A_ff = at("A_ff", R_A, [P, JF, TOK])
        A_ff_lat = at("A_ff_lat", R_A, [P, JF, LAT])
        cat_ev = at("cat_ev", R_A, [P, 12, TOK])
        cat_od = at("cat_od", R_A, [P, 12, LAT])
        a_hi = [at(f"a_hi{i}", R_HT + 3 * i * KIB, [P, TOK], F32R) for i in range(2)]
        a_lo = [at(f"a_lo{i}", R_HT + (6 + 3 * i) * KIB, [P, TOK], F32R) for i in range(2)]
        O = at("O", R_HT + 12 * KIB, [P, NT, D])
        diag = at("diag", R_HT + 36 * KIB, [P, 4, P])
        junk2 = at("junk2", R_HT + 40 * KIB, [P, D])
        yb = [at(f"yb{i}", R_GM + 3 * i * KIB, [P, TOK]) for i in range(2)]
        Zv = at("Zv", R_A + 12 * KIB, [P, NT, 512])
        V32 = at("V32", R_A + 24 * KIB, [P, NT, 256])
        sA = at("sA", R_A + 30 * KIB, [P, 512])
        sB = at("sB", R_A + 32 * KIB, [P, 512])
        csn = at("csn", R_A + 34 * KIB, [P, 2, LT, 64])
        Zq = at("Zq", R_A + 36 * KIB, [P, NT, D])
        Kt = at("Kt", R_A + 60 * KIB, [P, NT, 256])
        alnb = at("alnb", R_GM, [P, 2, 512])
        qkgb = at("qkgb", R_GM + 4 * KIB, [P, 2, P])
        bsb = at("bsb", R_GM + 5 * KIB, [P, 512])
        ws_sb = at("ws_sb", R_MOD, [P, 512])
        KT = at("KT", R_HT, [P, 2, TOK])
        Vev = at("Vev", R_HT + 6 * KIB, [P, NT, 256])
        PTe = [at(f"PTe{i}", R_HT + (12 + 6 * i) * KIB, [P, NT, 256]) for i in range(2)]
        Pe = [at(f"Pe{i}", R_HT + (24 + 6 * i) * KIB, [P, 2, TOK]) for i in range(2)]
        qTe = [at(f"qTe{i}", R_HT + (36 + i) * KIB, [P, 256]) for i in range(2)]
        sptmp = [at(f"sptmp{i}", R_HT + (40 + 2 * i) * KIB, [P, 4, P]) for i in range(2)]
        HALO = 15
        G = at("G", R_A + 24 * KIB, [P, 4, LAT + 2 * HALO])
        sg = [at(f"sg{i}", R_A + (57 + 2 * i) * KIB, [P, LAT]) for i in range(2)]
        cqh = at("cqh", R_A + 33 * KIB, [P, 4, LAT], F32R)
        cql = at("cql", R_A + 41 * KIB, [P, 4, LAT], F32R)
        zq = at("zq", R_GM, [P, LT, 512])
        zkv = at("zkv", R_MOD, [P, NT, 320])
        ckh = at("ckh", R_GM, [P, 2, TOK], F32R)
        ckl = at("ckl", R_A + 57 * KIB, [P, 2, TOK], F32R)
        KRT = at("KRT", R_A + 63 * KIB, [P, TOK])
        Vod = at("Vod", R_A + 33 * KIB, [P, NT, 1024])
        QTn = at("QTn", R_HT, [P, HEADS, LAT])
        QRT = at("QRT", R_HT + 16 * KIB, [P, 4, LAT])
        KTn = at("KTn", R_HT + 24 * KIB, [P, HEADS, TOK])
        QR = at("QR", R_MOD, [P, LT, 512])
        Pod = at("Pod", R_MOD, [P, 2, TOK])
        PTo = [at("PTo0", R_GM, [P, NT, 256]), at("PTo1", R_A + 57 * KIB, [P, NT, 256])]
        ccw = const("ccw", [P, 4, 32])
        ccln = const("ccln", [P, 4, 2])
        gq = const("gq", [P, 4])
        gkv = const("gkv", [P, 2])
        nrm_t = at("nrm_t", R_HT, [P, LT, 512])
        nrm_k = at("nrm_k", R_HT + 8 * KIB, [P, NT, 256])
        kr2 = at("kr2", R_HT + 16 * KIB, [P, NT, P])
        ev_t = [at(f"ev_t{i}", R_HT + (20 + 3 * i) * KIB, [P, TOK]) for i in range(2)]
        csd = at("csd", R_HT + 28 * KIB, [P, 2, LT, 32])
        rA = at("rA", R_HT + 30 * KIB, [P, 256])
        rB = at("rB", R_HT + 31 * KIB, [P, 256])
        csd2 = at("csd2", R_HT + 40 * KIB, [P, 2, LT, 32])
        rA2 = at("rA2", R_HT + 42 * KIB, [P, 256])
        rB2 = at("rB2", R_HT + 43 * KIB, [P, 256])
        mu = at("mu", R_HT + 0, [P, LAT])
        sqs = at("sqs", R_HT + 4 * KIB, [P, 4, LAT])
        rs_b = at("rs_b", R_HT + 2 * KIB, [P, LAT])
        nh_b = at("nh_b", R_HT + 12 * KIB, [P, LAT])

        PS = es.enter_context(nc.psum_tensor("PS", [P, 8, 512], F32))
        MODBANK = 6

        def ps2(b, n):
            return PS[:, b:b + 2, :].rearrange("p a b -> p (a b)")[:, 0:n]

        landed = [sem(f"landed{i}") for i in range(2)]
        wh_ready, wl_ready, w_used = sem("wh_ready"), sem("wl_ready"), sem("w_used")
        mod_landed = [sem(f"mod_landed{i}") for i in range(2)]
        mod_used, mod_evac = sem("mod_used"), sem("mod_evac")
        arrived = sem("arrived")
        consts, stored = sem("consts"), sem("stored")
        const_count = [0]
        phase = {}
        sems = {}

        def S(stage, what):
            return sems.setdefault((stage, what), sem(f"{stage}_{what}")) if (stage, what) not in sems else sems[(stage, what)]

        def barrier(eng, drains=True):
            k = phase.get(id(eng), 0) + 1
            phase[id(eng)] = k
            eng.drain().then_inc(arrived, 1)
            eng.wait_ge(arrived, 4 * k)

        def load_const(eng, dst, src):
            const_count[0] += 16
            eng.dma_start(dst, src).then_inc(consts, 16)

        def round_hi(act, n, u=0, i=None):
            r, more = n % 2, (0 if i is None else i)
            act.wait_ge(landed[r], (more + (n // 2 + 1)) * 16)
            if n >= 2:
                act.wait_ge(w_used, more * 2 + (n - 1))
            nc.scalar.activation(w_hi[r][:, :], w_raw[r][:, :], ACT.Copy).then_inc(wh_ready, 1)

        def take_lo(dve, n, i=None):
            r, more = n % 2, (0 if i is None else i)
            dve.wait_ge(wh_ready, more * 2 + (n + 1))
            nc.vector.tensor_tensor(w_lo[r][:, :], w_raw[r][:, :], w_hi[r][:, :].bitcast(F32),
                                    ALU.subtract).then_inc(wl_ready, 1)

        def weights(pe, n, i=None):
            pe.wait_ge(wl_ready, (0 if i is None else i) * 2 + (n + 1))

        def split_mm(outs, wh, wl, xs, start, stop):
            last = None
            for o, (xh, _) in zip(outs, xs):
                nc.tensor.matmul(o, wh, xh, start=start, stop=False)
            for o, (_, xl) in zip(outs, xs):
                nc.tensor.matmul(o, wh, xl, start=False, stop=False)
            for o, (xh, _) in zip(outs, xs):
                last = nc.tensor.matmul(o, wl, xh, start=False, stop=stop)
            return last

        def feature_slot(ns, n, tok, ncols, pair=2):
            b, r = 3 * (ns % 2), n % 2
            last = None
            for mt in range(pair):
                for k in range(KD):
                    cols = slice(k * 256 + mt * P, k * 256 + mt * P + P)
                    outs = [PS[:, b + mt, :]]
                    xs = [(HTh[:, k, 0:LAT], HTl[:, k, 0:LAT])]
                    if tok > LAT:
                        outs.append(PS[:, b + 2, mt * 256:mt * 256 + 256])
                        xs.append((HTh[:, k, LAT:TOK], HTl[:, k, LAT:TOK]))
                    last = split_mm(outs, w_hi[r][:, cols], w_lo[r][:, cols], xs, k == 0, k == KD - 1)
            return last

        def token_slot(ns, n, tiles, width):
            b, r = 3 * (ns % 2), n % 2
            last = None
            for t in range(tiles):
                o = PS[:, b + t // 2, (t % 2) * 256:(t % 2) * 256 + width]
                for k in range(KD):
                    wc = slice(k * 256, k * 256 + width)
                    xh, xl = HTh[:, k, t * P:(t + 1) * P], HTl[:, k, t * P:(t + 1) * P]
                    nc.tensor.matmul(o, xh, w_hi[r][:, wc], start=k == 0, stop=False)
                    nc.tensor.matmul(o, xh, w_lo[r][:, wc], start=False, stop=False)
                    last = nc.tensor.matmul(o, xl, w_hi[r][:, wc], start=False, stop=k == KD - 1)
            return last

        def mod_tile(pe, m, i=None, step=2, col=None):
            r = m % 2
            more = 0 if i is None else i * (step // 2)
            pe.wait_ge(mod_landed[r], (more + (m // 2 + 1)) * 16)
            for k in range(KD):
                last = nc.tensor.matmul(col, mod_raw[r][:, k, :], sT[:, k, :], start=k == 0, stop=k == KD - 1)
            last.then_inc(mod_used, 1)

        def mod_col(c):
            return PS[:, MODBANK, 2 * c:2 * c + 2]

        def mod_load(pool, m0, m1):
            a = m0
            if m0 == 0:
                for r in range(2):
                    pool.dma_start(mod_raw[r][:, :, :], modw[r]).then_inc(mod_landed[r], 16)
                a = 2
            with pool.Fori(a // 2, m1 // 2) as i:
                for r in range(2):
                    pool.wait_ge(mod_used, i * 2 + (r - 1))
                    pool.dma_start(mod_raw[r][:, :, :],
                                   modw[bass.ds(i * 2 + r, 1)].rearrange("a p k c -> (a p) k c"))\
                        .then_inc(mod_landed[r], 16)

        def mod_evacuate(dve, layer, c0, n, used):
            dve.wait_ge(mod_used, used)
            nc.vector.tensor_tensor(
                modc[:, layer, c0:c0 + n, :],
                PS[:, MODBANK, 0:2 * n].rearrange("p (m s) -> p m s", s=2),
                modb_sb[:, layer, c0:c0 + n].unsqueeze(2).to_broadcast([P, n, 2]), ALU.add).then_inc(mod_evac, 1)

        def prenorm_dve(dve, st, layer, which):
            o = 3 * which
            nc.vector.scalar_tensor_tensor(
                out=prescale[:, :, :], in0=modc[:, layer, (o + 1) * KD:(o + 2) * KD, :], scalar=1.0,
                in1=ng[:, layer, 2 * which, :].unsqueeze(2).to_broadcast([P, KD, 2]), op0=ALU.add, op1=ALU.mult)
            dve.wait_ge(S(st, "ssq"), NT)
            nc.vector.tensor_scalar(rstd[:, 0:NT], ssq[:, 0:NT], 1.0 / D, EPS, ALU.mult, ALU.add)\
                .then_inc(S(st, "mean"), 1)
            dve.wait_ge(S(st, "rstd"), 1)
            for t in range(NT):
                nc.vector.tensor_scalar(xn[:, t, :], X[:, t, :], rstd[:, t:t + 1], None, ALU.mult)\
                    .then_inc(S(st, "xn"), 1)
            for k in range(KD):
                dve.wait_ge(S(st, "tr"), k + 1)
                if k >= 2:
                    dve.wait_ge(S(st, "hi"), k - 1)
                src, tmp = ps2(2 * (k % 2), TOK), pre_tmp[k % 2]
                for s, (a, b) in enumerate(((0, LAT), (LAT, TOK))):
                    last = nc.vector.tensor_scalar(tmp[:, a:b], src[:, a:b], prescale[:, k, s:s + 1],
                                                   modc[:, layer, o * KD + k, s:s + 1], ALU.mult, ALU.add)
                last.then_inc(S(st, "aff"), 1)
                dve.wait_ge(S(st, "hi"), k + 1)
                nc.vector.tensor_tensor(HTl[:, k, :], tmp[:, :], HTh[:, k, :].bitcast(F32), ALU.subtract)
                dve.drain()

        def prenorm_act(act, st):
            for t in range(NT):
                nc.scalar.activation(junk[:, :], X[:, t, :], ACT.Square, accum_out=ssq[:, t:t + 1])\
                    .then_inc(S(st, "ssq"), 1)
                act.drain()
            for k in range(KD):
                act.wait_ge(S(st, "aff"), k + 1)
                nc.scalar.activation(HTh[:, k, :], pre_tmp[k % 2][:, :], ACT.Copy).then_inc(S(st, "hi"), 1)

        def power(pool, st, n, what="mean", done="rstd", count=1):
            pool.wait_ge(S(st, what), count)
            nc.gpsimd.tensor_tensor(rstd[:, 0:n], rstd[:, 0:n], halfneg[:, 0:n], ALU.pow)\
                .then_inc(S(st, done), 1)

        def prenorm_pe(pe, st):
            pe.wait_ge(S(st, "xn"), NT)
            for k in range(KD):
                if k >= 2:
                    pe.wait_ge(S(st, "aff"), k - 1)
                for t in range(NT):
                    last = nc.tensor.transpose(ps2(2 * (k % 2), TOK)[:, t * P:(t + 1) * P],
                                               xn[:, t, k * P:(k + 1) * P], ident[:, :])
                last.then_inc(S(st, "tr"), 1)

        def out_ktiles(kt):
            per = (kt + 3) // 4
            return [(h * per + k // 4, k % 4, h, k) for h in range(2) for k in range(kt)]

        def out_pe(pe, st, n0, kt, tiles):
            for c in range(2 * 2):
                pe.wait_ge(S(st, "diag"), c + 1)
                nc.tensor.matmul(PS[:, 6 + c % 2, :], ones[:, :], diag[:, :, :].rearrange("p a b -> p (a b)"),
                                 start=True, stop=True).then_inc(S(st, "row"), 1)
            for q, (s, j, h, k) in enumerate(out_ktiles(kt)):
                n = n0 + s
                if j == 0:
                    weights(pe, n)
                pe.wait_ge(S(st, "a_lo"), q + 1)
                for t in range(tiles):
                    if h == 1 and k == 0:
                        pe.wait_ge(S(st, "o_copy"), t + 1)
                    tc = slice(t * P, (t + 1) * P)
                    wc = slice(j * 512, j * 512 + 512)
                    ah, al = a_hi[q % 2][:, tc], a_lo[q % 2][:, tc]
                    nc.tensor.matmul(PS[:, t, :], ah, w_hi[n % 2][:, wc], start=k == 0, stop=False)
                    nc.tensor.matmul(PS[:, t, :], ah, w_lo[n % 2][:, wc], start=False, stop=False)
                    last = nc.tensor.matmul(PS[:, t, :], al, w_hi[n % 2][:, wc], start=False, stop=k == kt - 1)
                last.then_inc(S(st, "a_used"), 1)
                if j == 3 or k == kt - 1:
                    pe.drain().then_inc(w_used, 1)

        def out_act(act, st, n0, kt, tiles, A):
            w = tiles * P
            for q, (s, j, h, k) in enumerate(out_ktiles(kt)):
                if j == 0:
                    if h == 0 and k == 0:
                        round_hi(act, n0)
                    if n0 + s + 1 < n0 + 2 * ((kt + 3) // 4):
                        round_hi(act, n0 + s + 1) if False else None
                if q >= 2:
                    act.wait_ge(S(st, "a_used"), q - 1)
                nc.scalar.activation(a_hi[q % 2][:, 0:w], A[:, k, :], ACT.Copy).then_inc(S(st, "a_hi"), 1)
                if (j == 2 or (k == kt - 1 and j < 2)) and s + 1 < 2 * ((kt + 3) // 4):
                    round_hi(act, n0 + s + 1)
            for h in range(2):
                for t in range(tiles):
                    act.wait_ge(S(st, "o_copy"), h * tiles + t + 1)
                    nc.scalar.activation(junk2[:, 0:512], O[:, t, h * 512:h * 512 + 512], ACT.Square,
                                         accum_out=ssq[:, 2 * t + h:2 * t + h + 1]).then_inc(S(st, "ssq"), 1)
                    act.drain()

        def out_dve(dve, st, n0, kt, tiles, A, layer, which):
            w = tiles * P
            gate = 3 * which + 2
            nc.vector.tensor_tensor(gmcol[:, :, :], modc[:, layer, gate * KD:(gate + 1) * KD, :],
                                    ng[:, layer, 2 * which + 1, :].unsqueeze(2).to_broadcast([P, KD, 2]), ALU.mult)
            for c in range(4):
                s, half = divmod(c, 2)
                dve.drain()
                nc.vector.tensor_tensor(
                    diag[:, :, :], ident[:, :].unsqueeze(1).to_broadcast([P, 4, P]),
                    gmcol[:, 4 * half:4 * half + 4, s:s + 1].to_broadcast([P, 4, P]), ALU.mult)\
                    .then_inc(S(st, "diag"), 1)
                dve.wait_ge(S(st, "row"), c + 1)
                nc.vector.tensor_copy(gmB[:, s, half * 512:half * 512 + 512], PS[:, 6 + c % 2, :])
            order = out_ktiles(kt)
            for q, (s, j, h, k) in enumerate(order):
                if h == 0 and k == 0:
                    take_lo(dve, n0)
                dve.wait_ge(S(st, "a_hi"), q + 1)
                nc.vector.tensor_tensor(a_lo[q % 2][:, 0:w], A[:, k, :], a_hi[q % 2][:, 0:w].bitcast(F32),
                                        ALU.subtract).then_inc(S(st, "a_lo"), 1)
                if (j == 2 or (k == kt - 1 and j < 2)) and s + 1 < 2 * ((kt + 3) // 4):
                    take_lo(dve, n0 + s + 1)
                if h == 1 and k == 0 or k == kt - 1 and h == 1:
                    pass
                if k == kt - 1:
                    dve.wait_ge(S(st, "a_used"), q + 1)
                    for t in range(tiles):
                        nc.vector.tensor_copy(O[:, t, h * 512:h * 512 + 512], PS[:, t, :])\
                            .then_inc(S(st, "o_copy"), 1)
            dve.wait_ge(S(st, "ssq"), 2 * tiles)
            pairs = ssq[:, 0:2 * tiles].rearrange("p (t h) -> p t h", h=2)
            nc.vector.tensor_tensor(rstd[:, 0:tiles], pairs[:, :, 0], pairs[:, :, 1], ALU.add)
            dve.drain()
            nc.vector.tensor_scalar(rstd[:, 0:tiles], rstd[:, 0:tiles], 1.0 / D, EPS, ALU.mult, ALU.add)\
                .then_inc(S(st, "mean"), 1)
            dve.wait_ge(S(st, "rstd"), 1)
            for t in range(tiles):
                s = 0 if t < LT else 1
                nc.vector.scalar_tensor_tensor(out=O[:, t, :], in0=O[:, t, :], scalar=rstd[:, t:t + 1],
                                               in1=gmB[:, s, :], op0=ALU.mult, op1=ALU.mult)
            dve.drain()
            for t in range(tiles):
                nc.vector.tensor_tensor(X[:, t, :], X[:, t, :], O[:, t, :], ALU.add)

        def ffn_pe(pe, st, n0, tok, mods):
            def slot(ns, i=None):
                n = n0 + ns
                weights(pe, n, i)
                if ns >= 2 or i is not None:
                    pe.wait_ge(S(st, "evac"), (0 if i is None else i * 2) + (ns - 1))
                feature_slot(ns, n, tok, 256).then_inc(w_used, 1)
                if mods is not None:
                    for m in range(2):
                        c = 2 * ns + m
                        if i is None:
                            mod_tile(pe, mods + c, col=mod_col(c))
                        else:
                            mod_tile(pe, mods + c, i, 4, col=PS[:, MODBANK, bass.ds(i * 8 + 2 * c, 2)])
            slot(0)
            slot(1)
            with pe.Fori(1, JF // 2) as i:
                for u in range(2):
                    slot(u, i)
            if mods is not None:
                for c in range(2 * JF, MODT):
                    mod_tile(pe, mods + c, col=mod_col(c))

        def ffn_act(act, st, layer, n0, tok):
            def slot(u, i, more):
                y, b = yb[u], 3 * u
                if more:
                    round_hi(act, n0 + u + 1, i=i)
                act.wait_ge(S(st, "tap"), i * 2 + (u + 1))
                act.wait_ge(w_used, i * 2 + (n0 + u + 1))
                nc.scalar.activation(y[:, 0:LAT], PS[:, b, :], ACT.Identity, bias=cws[u][:, 3:4], scale=cws[u][:, 1:2])
                if tok > LAT:
                    nc.scalar.activation(y[:, LAT:TOK], PS[:, b + 2, 0:256], ACT.Identity, bias=cws[u][:, 3:4],
                                         scale=cws[u][:, 1:2])
                act.drain().then_inc(S(st, "mid"), 1)
                act.wait_ge(S(st, "conv"), i * 2 + (u + 1))
                nc.scalar.activation(y[:, 0:tok], y[:, 0:tok], ACT.Silu).then_inc(S(st, "silu"), 1)
            round_hi(act, n0)
            with act.Fori(0, JF // 2 - 1) as i:
                slot(0, i, True)
                slot(1, i, True)
            slot(0, JF // 2 - 1, True)
            slot(1, JF // 2 - 1, False)

        def ffn_dve(dve, st, layer, n0, tok, A):
            def slot(u, i, more):
                y, b = yb[u], 3 * u
                if more:
                    take_lo(dve, n0 + u + 1, i)
                nc.vector.tensor_copy(cws[u][:, :], cw[:, layer, bass.ds(i * 2 + u, 1), :].rearrange("p a b -> p (a b)"))\
                    .then_inc(S(st, "tap"), 1)
                dve.wait_ge(S(st, "mid"), i * 2 + (u + 1))
                streams = ((0, LAT, PS[:, b, :]),) + (((LAT, TOK, PS[:, b + 2, 0:256]),) if tok > LAT else ())
                for w, dst, src in ((0, 1, 0), (2, 0, 1)):
                    for a, e, g in streams:
                        n = e - a - 1
                        last = nc.vector.scalar_tensor_tensor(
                            out=y[:, a + dst:a + dst + n], in0=g[:, src:src + n], scalar=cws[u][:, w:w + 1],
                            in1=y[:, a + dst:a + dst + n], op0=ALU.mult, op1=ALU.add)
                    if w == 0:
                        dve.drain()
                last.then_inc(S(st, "conv"), 1)
                dve.wait_ge(S(st, "silu"), i * 2 + (u + 1))
                parts = ((0, LAT, PS[:, b + 1, :]),) + (((LAT, TOK, PS[:, b + 2, 256:512]),) if tok > LAT else ())
                for a, e, z in parts:
                    last = nc.vector.tensor_tensor(
                        A[:, bass.ds(i * 2 + u, 1), a:e].rearrange("p a b -> p (a b)"), y[:, a:e], z, ALU.mult)
                last.then_inc(S(st, "evac"), 1)
            take_lo(dve, n0)
            with dve.Fori(0, JF // 2 - 1) as i:
                slot(0, i, True)
                slot(1, i, True)
            slot(0, JF // 2 - 1, True)
            slot(1, JF // 2 - 1, False)

        def units(odd):
            lat = [(h, 256 * q, NT, 0) for h in range(HEADS) for q in range(2)]
            return lat if odd else lat + [(h, LAT, 2, LT) for h in range(HEADS)]

        def attn_pe(pe, st, odd):
            U = units(odd)
            PT = PTo if odd else PTe
            Pb = [Pod, Pod] if odd else Pe
            V = Vod if odd else Vev

            def q_transpose(u):
                h, q0, nk, k0 = U[u]
                if u >= 1:
                    pe.wait_ge(S(st, "qT"), u)
                for t in range(2):
                    last = nc.tensor.transpose(PS[:, 6, t * P:(t + 1) * P], Zq[:, q0 // P + t, h * P:(h + 1) * P],
                                               ident[:, :])
                last.then_inc(S(st, "qtr"), 1)

            def scores(u):
                h, q0, nk, k0 = U[u]
                if not odd:
                    pe.wait_ge(S(st, "qT"), u + 1)
                if u >= 1:
                    pe.wait_ge(S(st, "exp"), 2 * u)
                for t in range(2):
                    for a, e in (((0, 512), (512, 768)) if nk == NT else ((0, 256),)):
                        ks = slice(k0 * P + a, k0 * P + e)
                        o = PS[:, 2 * t + a // 512, a % 512:a % 512 + e - a]
                        if odd:
                            qs = slice(q0 + t * P, q0 + (t + 1) * P)
                            r = slice(64 * (h % 2), 64 * (h % 2) + 64)
                            nc.tensor.matmul(o, QTn[:, h, qs], KTn[:, h, ks], start=True, stop=False)
                            last = nc.tensor.matmul(o, QRT[r, h // 2, qs], KRT[r, ks], start=False, stop=True)
                        else:
                            last = nc.tensor.matmul(o, qTe[u % 2][:, t * P:(t + 1) * P], KT[:, h // 4, ks],
                                                    start=True, stop=True)
                last.then_inc(S(st, "s"), 1)

            rounds = 0
            if not odd:
                q_transpose(0)
            scores(0)
            for u in range(len(U)):
                h, q0, nk, k0 = U[u]
                if u + 1 < len(U):
                    if not odd:
                        q_transpose(u + 1)
                    scores(u + 1)
                pe.wait_ge(S(st, "p"), 2 * (u + 1))
                for g in range(nk // 2):
                    bank = 4 + rounds % 2
                    if rounds >= 2:
                        pe.wait_ge(S(st, "pT"), rounds - 1)
                    for kk in range(2):
                        for t in range(2):
                            last = nc.tensor.transpose(
                                PS[:, bank, kk * 256 + t * P:kk * 256 + (t + 1) * P],
                                Pb[u % 2][:, t, (2 * g + kk) * P:(2 * g + kk + 1) * P], ident[:, :])
                    last.then_inc(S(st, "ptr"), 1)
                    rounds += 1
                pe.wait_ge(S(st, "pT"), rounds)
                if u >= 1:
                    pe.wait_ge(S(st, "ocopy"), u)
                for j in range(nk):
                    vh = V[:, k0 + j, (h * P if odd else (h // 4) * P):(h * P if odd else (h // 4) * P) + P]
                    last = nc.tensor.matmul(PS[:, 7, 0:256], vh, PT[u % 2][:, j, :], start=j == 0, stop=j == nk - 1)
                last.then_inc(S(st, "o"), 1)

        def attn_act(act, st, odd, scale):
            U = units(odd)
            PT = PTo if odd else PTe
            Pb = [Pod, Pod] if odd else Pe

            def q_copy(u):
                act.wait_ge(S(st, "qtr"), u + 1)
                if u >= 2:
                    act.wait_ge(S(st, "s"), u - 1)
                nc.scalar.activation(qTe[u % 2][:, :], PS[:, 6, 0:256], ACT.Copy).then_inc(S(st, "qT"), 1)

            def exps(u):
                h, q0, nk, k0 = U[u]
                if odd and u >= 1:
                    act.wait_ge(S(st, "ptr"), u * nk // 2)
                if not odd and u >= 2:
                    act.wait_ge(S(st, "o"), u - 1)
                for t in range(2):
                    act.wait_ge(S(st, "max"), 2 * u + t + 1)
                    nc.scalar.activation(Pb[u % 2][:, t, 0:nk * P], ps2(2 * t, nk * P), ACT.Exp,
                                         bias=rmax[:, u % 2, t:t + 1], scale=scale,
                                         accum_out=rsum[:, u % 2, t:t + 1]).then_inc(S(st, "exp"), 1)
            rounds = 0
            if not odd:
                q_copy(0)
            exps(0)
            for u in range(len(U)):
                h, q0, nk, k0 = U[u]
                if u + 1 < len(U):
                    if not odd:
                        q_copy(u + 1)
                        exps(u + 1)
                if u >= 2:
                    act.wait_ge(S(st, "o"), u - 1)
                for g in range(nk // 2):
                    act.wait_ge(S(st, "ptr"), rounds + 1)
                    nc.scalar.activation(PT[u % 2][:, 2 * g:2 * g + 2, :].rearrange("p a b -> p (a b)"),
                                         PS[:, 4 + rounds % 2, :], ACT.Copy).then_inc(S(st, "pT"), 1)
                    rounds += 1
                if odd and u + 1 < len(U):
                    exps(u + 1)

        def attn_dve(dve, st, odd, scale, cat, extra):
            U = units(odd)
            Pb = [Pod, Pod] if odd else Pe

            def maxima(u):
                h, q0, nk, k0 = U[u]
                dve.wait_ge(S(st, "s"), u + 1)
                if u >= 2:
                    dve.wait_ge(S(st, "exp"), 2 * (u - 1))
                for t in range(2):
                    nc.vector.reduce_max(rmax[:, u % 2, t:t + 1], ps2(2 * t, nk * P), AX_X)
                dve.drain()
                for t in range(2):
                    nc.vector.tensor_scalar(rmax[:, u % 2, t:t + 1], rmax[:, u % 2, t:t + 1], -scale, None,
                                            ALU.mult).then_inc(S(st, "max"), 1)

            maxima(0)
            for u in range(len(U)):
                h, q0, nk, k0 = U[u]
                dve.wait_ge(S(st, "exp"), 2 * (u + 1))
                nc.vector.reciprocal(rsum[:, u % 2, :], rsum[:, u % 2, :])
                dve.drain()
                for t in range(2):
                    nc.vector.tensor_scalar(Pb[u % 2][:, t, 0:nk * P], Pb[u % 2][:, t, 0:nk * P],
                                            rsum[:, u % 2, t:t + 1], None, ALU.mult).then_inc(S(st, "p"), 1)
                if u + 1 < len(U):
                    maxima(u + 1)
                extra(u)
                dve.wait_ge(S(st, "o"), u + 1)
                nc.vector.tensor_copy(cat[:, 4 + h, q0:q0 + 256], PS[:, 7, 0:256]).then_inc(S(st, "ocopy"), 1)

        def rotate(dve, x0, x1, cs, sn, tA, tB):
            nc.vector.tensor_tensor(tA, x1, sn, ALU.mult)
            nc.vector.tensor_tensor(tB, x0, sn, ALU.mult)
            nc.vector.tensor_tensor(x0, x0, cs, ALU.mult)
            nc.vector.tensor_tensor(x1, x1, cs, ALU.mult)
            dve.drain()
            nc.vector.tensor_tensor(x0, x0, tA, ALU.subtract)
            nc.vector.tensor_tensor(x1, x1, tB, ALU.add)
            dve.drain()

        block = es.enter_context(nc.Block())

        @block.sync
        def _(sp):
            for n in range(2):
                sp.dma_start(w_raw[n][:, :], wpack[n]).then_inc(landed[n], 16)
            with sp.Fori(1, NSLOT // 2) as i:
                for r in range(2):
                    sp.wait_ge(wl_ready, i * 2 + (r - 1))
                    sp.dma_start(w_raw[r][:, :], wpack[bass.ds(i * 2 + r, 1)].rearrange("a p c -> (a p) c"))\
                        .then_inc(landed[r], 16)
            sp.wait_ge(S("end", "x"), 1)
            sp.dma_start(out.rearrange("(t p) d -> p t d", p=P), X[:, 0:LT, :]).then_inc(stored, 16)
            sp.wait_ge(stored, 16)

        @block.gpsimd
        def _(pool):
            nc.gpsimd.memset(ident[:, :], 0.0)
            nc.gpsimd.memset(ones[:, :], 1.0)
            nc.gpsimd.memset(halfneg[:, :], -0.5)
            pool.drain()
            nc.gpsimd.affine_select(out=ident[:, :], in_=ident[:, :], compare_op=ALU.not_equal, fill=1.0,
                                    base=0, pattern=[[-1, P]], channel_multiplier=1)
            mod_load(pool, 0, 16)
            barrier(pool)
            power(pool, "pre0", NT)
            barrier(pool)
            mod_load(pool, 16, MODT)
            power(pool, "evz", 60)
            barrier(pool)
            power(pool, "gate", NT)
            barrier(pool)
            barrier(pool)
            power(pool, "evo", NT)
            barrier(pool)
            power(pool, "pre1", NT)
            barrier(pool)
            mod_load(pool, MODT, 2 * MODT)
            barrier(pool)
            power(pool, "ffo0", NT)
            barrier(pool)
            power(pool, "pre2", NT)
            barrier(pool)
            barrier(pool)
            power(pool, "odn", LT + NT)
            barrier(pool)
            barrier(pool)
            barrier(pool)
            barrier(pool)
            pool.wait_ge(S("cln", "var"), 1)
            nc.gpsimd.tensor_tensor(rs_b[:, :], rs_b[:, :], nh_b[:, :], ALU.pow).then_inc(S("cln", "rstd"), 1)
            barrier(pool)
            power(pool, "odo", LT)
            barrier(pool)
            power(pool, "pre3", NT)
            barrier(pool)
            barrier(pool)
            power(pool, "ffo1", LT)

        @block.scalar
        def _(act):
            load_const(act, sT[:, :, :], cvec)
            load_const(act, modb_sb[:, :, :], modb)
            load_const(act, ng[:, :, :, :], normg)
            load_const(act, cw[:, :, :, :], ffcw)
            load_const(act, ccw[:, :, :], odcw)
            load_const(act, ccln[:, :, :], odcln)
            load_const(act, gq[:, :], gcq)
            load_const(act, gkv[:, :], gckv)
            load_const(act, X[:, 0:LT, :], x.rearrange("(t p) d -> p t d", p=P))
            load_const(act, X[:, LT:NT, :], ctx.rearrange("(t p) d -> p t d", p=P))
            act.wait_ge(consts, const_count[0])
            nc.scalar.activation(sT[:, :, :], sT[:, :, :], ACT.Silu).then_inc(S("init", "silu"), 1)
            barrier(act)
            prenorm_act(act, "pre0")
            barrier(act)
            load_const(act, csn[:, :, :, :], rope_ev)
            load_const(act, alnb[:, :, :], aln)
            load_const(act, qkgb[:, :, :], qkg)
            load_const(act, bsb[:, :], bs)
            round_hi(act, EV0)
            for s in range(N_EVZ):
                if s + 1 < N_EVZ:
                    round_hi(act, EV0 + s + 1)
                b = 3 * (s % 2)
                if s in (0, 2, 3, 4, 5):
                    act.wait_ge(S("evz", "copy"), s + 1)
                    for t in range(NT):
                        for hh in range(2):
                            src = Kt[:, t, hh * P:hh * P + P] if s == 0 else \
                                Zq[:, t, (s - 2) * 256 + hh * P:(s - 2) * 256 + hh * P + P]
                            c = t * 10 + (8 + hh if s == 0 else 2 * (s - 2) + hh)
                            j4 = (2 * t + hh) % 4
                            nc.scalar.activation(sA[:, j4 * P:(j4 + 1) * P], src, ACT.Square, accum_out=ssq[:, c:c + 1])
                        if t % 2:
                            act.drain()
                    act.drain().then_inc(S("evz", "ssq"), 1)
                if s in (6, 7):
                    act.wait_ge(w_used, EV0 + s + 1)
                    for i in range(3):
                        nc.scalar.activation(Zv[:, 2 * i:2 * i + 2, (s - 6) * 256:(s - 6) * 256 + 256],
                                             PS[:, b + i, :].rearrange("p (a b) -> p a b", a=2), ACT.Gelu_apprx_tanh)
                    act.drain().then_inc(S("evz", "gelu"), 1)
                if s in (8, 9):
                    act.wait_ge(w_used, EV0 + s + 1)
                    for mt in range(2):
                        g = 2 * (s - 8) + mt
                        nc.scalar.activation(cat_ev[:, g, 0:LAT], PS[:, b + mt, :], ACT.Gelu_apprx_tanh)
                        nc.scalar.activation(cat_ev[:, g, LAT:TOK], PS[:, b + 2, mt * 256:mt * 256 + 256],
                                             ACT.Gelu_apprx_tanh)
            barrier(act)
            load_const(act, ws_sb[:, :], wsT)
            for g in range(2):
                act.wait_ge(S("gate", "ktr"), g + 1)
                nc.scalar.activation(KT[:, g, :], ps2(6, TOK), ACT.Copy).then_inc(S("gate", "kT"), 1)
            barrier(act)
            attn_act(act, "eva", False, P ** -0.5)
            barrier(act)
            out_act(act, "evo", EVO0, 12, NT, cat_ev)
            barrier(act)
            prenorm_act(act, "pre1")
            barrier(act)
            ffn_act(act, "ff0", 0, F10, TOK)
            barrier(act)
            out_act(act, "ffo0", F20, JF, NT, A_ff)
            barrier(act)
            prenorm_act(act, "pre2")
            barrier(act)
            round_hi(act, OD0)
            for s in range(N_ODZ):
                if s + 1 < N_ODZ:
                    round_hi(act, OD0 + s + 1)
                if s < 4:
                    act.wait_ge(w_used, OD0 + s + 1)
                    if s >= 2:
                        act.wait_ge(S("odz", "evac"), s - 1)
                    nc.scalar.activation(sg[s % 2][:, :], PS[:, 3 * (s % 2) + 1, :], ACT.Sigmoid)\
                        .then_inc(S("odz", "sg"), 1)
            barrier(act)
            load_const(act, csd[:, :, :, :], rope_od)
            for t in range(LT):
                nc.scalar.activation(ev_t[0][:, 0:512], zq[:, t, :], ACT.Square, accum_out=ssq[:, t:t + 1])
                act.drain()
            for t in range(NT):
                nc.scalar.activation(ev_t[0][:, 0:256], zkv[:, t, 0:256], ACT.Square,
                                     accum_out=ssq[:, LT + t:LT + t + 1])
                act.drain()
            act.drain().then_inc(S("odn", "ssq"), 1)
            for k in range(6):
                act.wait_ge(S("odn", "aff"), k + 1)
                if k < 4:
                    nc.scalar.activation(cqh[:, k, :], ev_t[k % 2][:, 0:LAT], ACT.Copy).then_inc(S("odn", "hi"), 1)
                else:
                    nc.scalar.activation(ckh[:, k - 4, :], ev_t[k % 2][:, :], ACT.Copy).then_inc(S("odn", "hi"), 1)
            barrier(act)
            load_const(act, csd2[:, :, :, :], rope_od)
            for n in range(UQ0, UQ0 + 3):
                round_hi(act, n)
            barrier(act)
            for n in range(UKV0, UKV0 + 2):
                round_hi(act, n)
            barrier(act)
            attn_act(act, "oda", True, 192 ** -0.5)
            barrier(act)
            for j in range(4):
                act.wait_ge(S("cln", "cent"), j + 1)
                nc.scalar.activation(sqs[:, j, :], cat_od[:, j, :], ACT.Square).then_inc(S("cln", "sq"), 1)
            for j in range(4):
                act.wait_ge(S("cln", "nrm"), j + 1)
                nc.scalar.activation(cat_od[:, j, :], cat_od[:, j, :], ACT.Silu, bias=ccln[:, j, 1:2],
                                     scale=ccln[:, j, 0:1])
            barrier(act)
            out_act(act, "odo", ODO0, 12, LT, cat_od)
            barrier(act)
            prenorm_act(act, "pre3")
            barrier(act)
            ffn_act(act, "ff1", 1, F11, LAT)
            barrier(act)
            out_act(act, "ffo1", F21, JF, LT, A_ff_lat)



        @block.tensor
        def _(pe):
            pe.wait_ge(S("init", "silu"), 1)
            for m in range(16):
                mod_tile(pe, m, col=mod_col(m))
            barrier(pe)
            prenorm_pe(pe, "pre0")
            barrier(pe)
            done = 16
            for s in range(N_EVZ):
                n = EV0 + s
                weights(pe, n)
                if s >= 2:
                    if s - 2 < 6:
                        pe.wait_ge(S("evz", "copy"), s - 1)
                    else:
                        pe.wait_ge(S("evz", "gelu"), s - 7)
                (feature_slot(s, n, TOK, 256) if s >= 8 else token_slot(s, n, NT, 256)).then_inc(w_used, 1)
                for m in range(done, min(done + 6, MODT)):
                    mod_tile(pe, m, col=mod_col(m - 16))
                done = min(done + 6, MODT)
            barrier(pe)
            for g in range(2):
                if g:
                    pe.wait_ge(S("gate", "kT"), g)
                for t in range(NT):
                    last = nc.tensor.transpose(ps2(6, TOK)[:, t * P:(t + 1) * P], Kt[:, t, g * P:(g + 1) * P],
                                               ident[:, :])
                last.then_inc(S("gate", "ktr"), 1)
            pe.wait_ge(S("gate", "ws"), 1)
            for c in range(NT):
                pe.wait_ge(S("gate", "vn"), c + 1)
                for g in range(4):
                    last = nc.tensor.matmul(PS[:, c, g * P:(g + 1) * P], Zv[:, c, g * P:(g + 1) * P],
                                            ws_sb[:, g * P:(g + 1) * P], start=True, stop=True)
                last.then_inc(S("gate", "sp"), 1)
            barrier(pe)
            attn_pe(pe, "eva", False)
            barrier(pe)
            out_pe(pe, "evo", EVO0, 12, NT)
            barrier(pe)
            prenorm_pe(pe, "pre1")
            barrier(pe)
            ffn_pe(pe, "ff0", F10, TOK, MODT)
            barrier(pe)
            out_pe(pe, "ffo0", F20, JF, NT)
            barrier(pe)
            prenorm_pe(pe, "pre2")
            barrier(pe)
            for s in range(N_ODZ):
                n = OD0 + s
                weights(pe, n)
                if s >= 2:
                    pe.wait_ge(S("odz", "evac"), s - 1)
                if s < 4:
                    last = feature_slot(s, n, LAT, 256)
                elif s < 6:
                    last = token_slot(s, n, LT, 256)
                else:
                    last = token_slot(s, n, NT, 160)
                last.then_inc(w_used, 1)
            barrier(pe)
            pe.wait_ge(S("odn", "xn"), 1)
            for k in range(7):
                if k >= 2:
                    pe.wait_ge(S("odn", "aff"), k - 1)
                b = 2 * (k % 2)
                for t in range(LT if k < 4 else NT):
                    src = nrm_t[:, t, k * P:(k + 1) * P] if k < 4 else \
                        (nrm_k[:, t, (k - 4) * P:(k - 3) * P] if k < 6 else kr2[:, t, :])
                    last = nc.tensor.transpose(ps2(b, TOK)[:, t * P:(t + 1) * P], src, ident[:, :])
                last.then_inc(S("odn", "tr"), 1)
            barrier(pe)
            for s in range(2):
                n = UQ0 + s
                weights(pe, n)
                for hh in range(4):
                    h = 4 * s + hh
                    if h >= 4:
                        pe.wait_ge(S("odu", "q"), h - 3)
                    for k in range(4):
                        cols = slice(k * 512 + hh * P, k * 512 + (hh + 1) * P)
                        last = split_mm([PS[:, h % 4, :]], w_hi[n % 2][:, cols], w_lo[n % 2][:, cols],
                                        [(cqh[:, k, :], cql[:, k, :])], k == 0, k == 3)
                    last.then_inc(S("odu", "qmm"), 1)
                pe.drain().then_inc(w_used, 1)
            n = UQ0 + 2
            weights(pe, n)
            for t in range(LT):
                for k in range(4):
                    wc, tc = slice(k * 512, k * 512 + 512), slice(t * P, (t + 1) * P)
                    nc.tensor.matmul(PS[:, 4 + t, :], cqh[:, k, tc], w_hi[n % 2][:, wc], start=k == 0, stop=False)
                    nc.tensor.matmul(PS[:, 4 + t, :], cqh[:, k, tc], w_lo[n % 2][:, wc], start=False, stop=False)
                    last = nc.tensor.matmul(PS[:, 4 + t, :], cql[:, k, tc], w_hi[n % 2][:, wc], start=False, stop=k == 3)
                last.then_inc(S("odu", "rmm"), 1)
            pe.drain().then_inc(w_used, 1)
            pe.wait_ge(S("odu", "rope"), LT)
            for p in range(4):
                if p >= 0:
                    pe.wait_ge(S("odu", "q"), 8 if p < 4 else 8)
                for t in range(LT):
                    last = nc.tensor.transpose(PS[:, p, t * P:(t + 1) * P], QR[:, t, p * P:(p + 1) * P], ident[:, :])
                last.then_inc(S("odu", "rtr"), 1)
            barrier(pe)
            for s in range(2):
                n = UKV0 + s
                weights(pe, n)
                for hh in range(4):
                    q = 4 * s + hh
                    if q >= 2:
                        pe.wait_ge(S("odk", "k"), q - 1)
                    b = 2 * (q % 2)
                    for k in range(2):
                        cols = slice(k * 1024 + hh * P, k * 1024 + (hh + 1) * P)
                        last = split_mm([PS[:, b, :], PS[:, b + 1, 0:256]], w_hi[n % 2][:, cols], w_lo[n % 2][:, cols],
                                        [(ckh[:, k, 0:LAT], ckl[:, k, 0:LAT]), (ckh[:, k, LAT:TOK], ckl[:, k, LAT:TOK])],
                                        k == 0, k == 1)
                    last.then_inc(S("odk", "kmm"), 1)
                for t in range(NT):
                    q = NT * s + t
                    if q >= 4:
                        pe.wait_ge(S("odk", "v"), q - 3)
                    o = PS[:, 4 + q % 4, :]
                    for k in range(2):
                        wc, tc = slice(k * 1024 + 512, k * 1024 + 1024), slice(t * P, (t + 1) * P)
                        nc.tensor.matmul(o, ckh[:, k, tc], w_hi[n % 2][:, wc], start=k == 0, stop=False)
                        nc.tensor.matmul(o, ckh[:, k, tc], w_lo[n % 2][:, wc], start=False, stop=False)
                        last = nc.tensor.matmul(o, ckl[:, k, tc], w_hi[n % 2][:, wc], start=False, stop=k == 1)
                    last.then_inc(S("odk", "vmm"), 1)
                pe.drain().then_inc(w_used, 1)
            barrier(pe)
            attn_pe(pe, "oda", True)
            barrier(pe)
            for j in range(4):
                last = nc.tensor.matmul(PS[:, 0, :], ones[:, :], cat_od[:, j, :], start=j == 0, stop=j == 3)
            last.then_inc(S("cln", "sum"), 1)
            for j in range(4):
                pe.wait_ge(S("cln", "sq"), j + 1)
                last = nc.tensor.matmul(PS[:, 1, :], ones[:, :], sqs[:, j, :], start=j == 0, stop=j == 3)
            last.then_inc(S("cln", "sum2"), 1)
            barrier(pe)
            out_pe(pe, "odo", ODO0, 12, LT)
            barrier(pe)
            prenorm_pe(pe, "pre3")
            barrier(pe)
            ffn_pe(pe, "ff1", F11, LAT, None)
            barrier(pe)
            out_pe(pe, "ffo1", F21, JF, LT)

        @block.vector
        def _(dve):
            dve.wait_ge(consts, 16 * 10)
            mod_evacuate(dve, 0, 0, 16, 16)
            barrier(dve)
            prenorm_dve(dve, "pre0", 0, 0)
            barrier(dve)
            take_lo(dve, EV0)
            for s in range(N_EVZ):
                if s + 1 < N_EVZ:
                    take_lo(dve, EV0 + s + 1)
                b = 3 * (s % 2)
                if s < 6:
                    dve.wait_ge(w_used, EV0 + s + 1)
                    for i in range(3):
                        dst = (Kt if s == 0 else V32)[:, 2 * i:2 * i + 2, :] if s < 2 else \
                            Zq[:, 2 * i:2 * i + 2, (s - 2) * 256:(s - 1) * 256]
                        last = nc.vector.tensor_copy(dst, PS[:, b + i, :].rearrange("p (a b) -> p a b", a=2))
                    last.then_inc(S("evz", "copy"), 1)
                if s == 6:
                    mod_evacuate(dve, 0, 16, 32, MODT)
                if s == 7:
                    dve.wait_ge(S("evz", "ssq"), 5)
                    nc.vector.tensor_scalar(rstd[:, 0:60], ssq[:, 0:60], 1.0 / P, EPS, ALU.mult, ALU.add)\
                        .then_inc(S("evz", "mean"), 1)
            dve.wait_ge(S("evz", "rstd"), 1)
            dve.wait_ge(consts, 16 * 14)
            for t in range(NT):
                q3 = Zq[:, t, :].rearrange("p (h d) -> p h d", d=P)
                k3 = Kt[:, t, :].rearrange("p (h d) -> p h d", d=P)
                nc.vector.tensor_tensor(q3, q3, rstd[:, 10 * t:10 * t + 8].unsqueeze(2).to_broadcast([P, 8, P]), ALU.mult)
                nc.vector.tensor_tensor(k3, k3, rstd[:, 10 * t + 8:10 * t + 10].unsqueeze(2).to_broadcast([P, 2, P]),
                                        ALU.mult)
                dve.drain()
                nc.vector.tensor_tensor(q3, q3, qkgb[:, 0, :].unsqueeze(1).to_broadcast([P, 8, P]), ALU.mult)
                nc.vector.tensor_tensor(k3, k3, qkgb[:, 1, :].unsqueeze(1).to_broadcast([P, 2, P]), ALU.mult)
                dve.drain()
                if t < LT:
                    for z, nh in ((Zq, 8), (Kt, 2)):
                        zz = z[:, t, :].rearrange("p (h i two) -> p h i two", i=64, two=2)
                        cs = csn[:, 0, t, :].unsqueeze(1).to_broadcast([P, nh, 64])
                        sn = csn[:, 1, t, :].unsqueeze(1).to_broadcast([P, nh, 64])
                        tA = sA[:, 0:nh * 64].rearrange("p (h i) -> p h i", i=64)
                        tB = sB[:, 0:nh * 64].rearrange("p (h i) -> p h i", i=64)
                        rotate(dve, zz[:, :, :, 0], zz[:, :, :, 1], cs, sn, tA, tB)
            barrier(dve)
            nc.vector.tensor_copy(Vev[:, :, :], V32[:, :, :])
            dve.wait_ge(consts, 16 * 15)
            nc.vector.tensor_copy(ws_sb[:, 0:1], ws_sb[:, 0:1]).then_inc(S("gate", "ws"), 1)
            for t in range(NT):
                nc.vector.bn_stats(lnst[:, t, :], Zv[:, t, :])
            dve.drain()
            for t in range(NT):
                nc.vector.bn_aggr(lnmv[:, t, :], lnst[:, t, :])
            dve.drain()
            nc.vector.tensor_scalar(rstd[:, 0:NT], lnmv[:, :, 1], 1.0, EPS, ALU.mult, ALU.add)\
                .then_inc(S("gate", "mean"), 1)
            dve.wait_ge(S("gate", "rstd"), 1)
            for t in range(NT):
                nc.vector.tensor_scalar(Zv[:, t, :], Zv[:, t, :], lnmv[:, t, 0:1], rstd[:, t:t + 1],
                                        ALU.subtract, ALU.mult)
                dve.drain()
                nc.vector.tensor_tensor(Zv[:, t, :], Zv[:, t, :], alnb[:, 0, :], ALU.mult)
                dve.drain()
                nc.vector.tensor_tensor(Zv[:, t, :], Zv[:, t, :], alnb[:, 1, :], ALU.add).then_inc(S("gate", "vn"), 1)
            for c in range(NT):
                dve.wait_ge(S("gate", "sp"), c + 1)
                tmp = sptmp[c % 2]
                nc.vector.tensor_tensor(tmp[:, :, :], PS[:, c, :].rearrange("p (g q) -> p g q", q=P),
                                        bsb[:, :].rearrange("p (g q) -> p g q", q=P), ALU.add)
                dve.drain()
                cc = cat_ev[:, 0:4, c * P:(c + 1) * P]
                nc.vector.tensor_tensor(cc, cc, tmp[:, :, :], ALU.mult)
            barrier(dve)
            attn_dve(dve, "eva", False, P ** -0.5, cat_ev, lambda u: None)
            barrier(dve)
            out_dve(dve, "evo", EVO0, 12, NT, cat_ev, 0, 0)
            barrier(dve)
            prenorm_dve(dve, "pre1", 0, 1)
            barrier(dve)
            ffn_dve(dve, "ff0", 0, F10, TOK, A_ff)
            mod_evacuate(dve, 1, 0, MODT, 2 * MODT)
            barrier(dve)
            out_dve(dve, "ffo0", F20, JF, NT, A_ff, 0, 1)
            barrier(dve)
            prenorm_dve(dve, "pre2", 1, 0)
            barrier(dve)
            nc.vector.memset(G[:, :, 0:HALO], 0.0)
            nc.vector.memset(G[:, :, HALO + LAT:], 0.0)
            take_lo(dve, OD0)
            for s in range(N_ODZ):
                if s + 1 < N_ODZ:
                    take_lo(dve, OD0 + s + 1)
                b = 3 * (s % 2)
                dve.wait_ge(w_used, OD0 + s + 1)
                if s < 4:
                    dve.wait_ge(S("odz", "sg"), s + 1)
                    nc.vector.tensor_tensor(G[:, s, HALO:HALO + LAT], PS[:, b, :], sg[s % 2][:, :], ALU.mult)\
                        .then_inc(S("odz", "evac"), 1)
                elif s < 6:
                    for i in range(2):
                        last = nc.vector.tensor_copy(zq[:, 2 * i:2 * i + 2, (s - 4) * 256:(s - 3) * 256],
                                                     PS[:, b + i, :].rearrange("p (a b) -> p a b", a=2))
                    last.then_inc(S("odz", "evac"), 1)
                else:
                    for i in range(3):
                        last = nc.vector.tensor_copy(zkv[:, 2 * i:2 * i + 2, (s - 6) * 160:(s - 5) * 160],
                                                     PS[:, b + i, :].rearrange("p (a b) -> p a b", a=2)[:, :, 0:160])
                    last.then_inc(S("odz", "evac"), 1)
            barrier(dve)
            dve.wait_ge(S("odn", "ssq"), 1)
            nc.vector.tensor_scalar(rstd[:, 0:LT], ssq[:, 0:LT], 1.0 / 512, EPS, ALU.mult, ALU.add)
            nc.vector.tensor_scalar(rstd[:, LT:LT + NT], ssq[:, LT:LT + NT], 1.0 / 256, EPS, ALU.mult, ALU.add)
            dve.drain().then_inc(S("odn", "mean"), 1)
            dve.wait_ge(S("odn", "rstd"), 1)
            dve.wait_ge(consts, 16 * 16)
            for t in range(LT):
                nc.vector.tensor_scalar(nrm_t[:, t, :], zq[:, t, :], rstd[:, t:t + 1], None, ALU.mult)
                kr = zkv[:, t, 256:320].rearrange("p (i two) -> p i two", two=2)
                rotate(dve, kr[:, :, 0], kr[:, :, 1], csd[:, 0, t, :], csd[:, 1, t, :], rA[:, 0:32], rB[:, 0:32])
            for t in range(NT):
                nc.vector.tensor_scalar(nrm_k[:, t, :], zkv[:, t, 0:256], rstd[:, LT + t:LT + t + 1], None, ALU.mult)
                for half in range(2):
                    nc.vector.tensor_copy(kr2[:, t, 64 * half:64 * half + 64], zkv[:, t, 256:320])
            dve.drain().then_inc(S("odn", "xn"), 1)
            for k in range(7):
                dve.wait_ge(S("odn", "tr"), k + 1)
                src = ps2(2 * (k % 2), TOK)
                if k == 6:
                    nc.vector.tensor_copy(KRT[:, :], src)
                    continue
                if k >= 2:
                    dve.wait_ge(S("odn", "hi"), k - 1)
                w = LAT if k < 4 else TOK
                g = gq[:, k:k + 1] if k < 4 else gkv[:, k - 4:k - 3]
                nc.vector.tensor_scalar(ev_t[k % 2][:, 0:w], src[:, 0:w], g, None, ALU.mult).then_inc(S("odn", "aff"), 1)
                dve.wait_ge(S("odn", "hi"), k + 1)
                hi, lo = (cqh[:, k, :], cql[:, k, :]) if k < 4 else (ckh[:, k - 4, :], ckl[:, k - 4, :])
                nc.vector.tensor_tensor(lo, ev_t[k % 2][:, 0:w], hi.bitcast(F32), ALU.subtract)
                dve.drain()
            barrier(dve)
            for s in range(3):
                take_lo(dve, UQ0 + s)
                if s == 2:
                    break
                if s == 1:
                    for h in range(4):
                        dve.wait_ge(S("odu", "qmm"), h + 1)
                        nc.vector.tensor_copy(QTn[:, h, :], PS[:, h % 4, :]).then_inc(S("odu", "q"), 1)
            for h in range(4, HEADS):
                dve.wait_ge(S("odu", "qmm"), h + 1)
                nc.vector.tensor_copy(QTn[:, h, :], PS[:, h % 4, :]).then_inc(S("odu", "q"), 1)
            dve.wait_ge(consts, 16 * 17)
            for t in range(LT):
                dve.wait_ge(S("odu", "rmm"), t + 1)
                nc.vector.tensor_copy(QR[:, t, :], PS[:, 4 + t, :])
                dve.drain()
                zz = QR[:, t, :].rearrange("p (h i two) -> p h i two", i=32, two=2)
                rotate(dve, zz[:, :, :, 0], zz[:, :, :, 1], csd2[:, 0, t, :].unsqueeze(1).to_broadcast([P, 8, 32]),
                       csd2[:, 1, t, :].unsqueeze(1).to_broadcast([P, 8, 32]),
                       rA2[:, :].rearrange("p (h i) -> p h i", i=32), rB2[:, :].rearrange("p (h i) -> p h i", i=32))
                dve.drain().then_inc(S("odu", "rope"), 1)
            for p in range(4):
                dve.wait_ge(S("odu", "rtr"), p + 1)
                nc.vector.tensor_copy(QRT[:, p, :], PS[:, p, :])
            barrier(dve)
            for s in range(2):
                take_lo(dve, UKV0 + s)
            for s in range(2):
                for hh in range(4):
                    q = 4 * s + hh
                    dve.wait_ge(S("odk", "kmm"), q + 1)
                    nc.vector.tensor_copy(KTn[:, q, :], ps2(2 * (q % 2), TOK)).then_inc(S("odk", "k"), 1)
                for t in range(NT):
                    q = NT * s + t
                    dve.wait_ge(S("odk", "vmm"), q + 1)
                    nc.vector.tensor_copy(Vod[:, t, 512 * s:512 * s + 512], PS[:, 4 + q % 4, :])\
                        .then_inc(S("odk", "v"), 1)
            barrier(dve)

            def conv_taps(u):
                for tap in (2 * u, 2 * u + 1):
                    if tap > 30:
                        continue
                    for j in range(4):
                        g, w = G[:, j, tap:tap + LAT], ccw[:, j, tap:tap + 1]
                        if tap == 0:
                            nc.vector.tensor_scalar(cat_od[:, j, :], g, w, ccw[:, j, 31:32], ALU.mult, ALU.add)
                        else:
                            nc.vector.scalar_tensor_tensor(out=cat_od[:, j, :], in0=g, scalar=w, in1=cat_od[:, j, :],
                                                           op0=ALU.mult, op1=ALU.add)
                    dve.drain()

            attn_dve(dve, "oda", True, 192 ** -0.5, cat_od, conv_taps)
            barrier(dve)
            nc.vector.memset(nh_b[:, :], -0.5)
            dve.wait_ge(S("cln", "sum"), 1)
            nc.vector.tensor_scalar(mu[:, :], PS[:, 0, :], 1.0 / 512, None, ALU.mult)
            dve.drain()
            for j in range(4):
                nc.vector.tensor_tensor(cat_od[:, j, :], cat_od[:, j, :], mu[:, :], ALU.subtract)\
                    .then_inc(S("cln", "cent"), 1)
            dve.wait_ge(S("cln", "sum2"), 1)
            nc.vector.tensor_scalar(rs_b[:, :], PS[:, 1, :], 1.0 / 512, EPS, ALU.mult, ALU.add)\
                .then_inc(S("cln", "var"), 1)
            dve.wait_ge(S("cln", "rstd"), 1)
            for j in range(4):
                nc.vector.tensor_tensor(cat_od[:, j, :], cat_od[:, j, :], rs_b[:, :], ALU.mult)\
                    .then_inc(S("cln", "nrm"), 1)
            barrier(dve)
            out_dve(dve, "odo", ODO0, 12, LT, cat_od, 1, 0)
            barrier(dve)
            prenorm_dve(dve, "pre3", 1, 1)
            barrier(dve)
            ffn_dve(dve, "ff1", 1, F11, LAT, A_ff_lat)
            barrier(dve)
            out_dve(dve, "ffo1", F21, JF, LT, A_ff_lat, 1, 1)
            dve.drain().then_inc(S("end", "x"), 1)


def _slots_in(w, groups):
    out = []
    for cols in groups:
        s = np.zeros((P, KD, 256), w.dtype)
        s[:, :, :len(cols)] = w[:, cols].reshape(KD, P, len(cols)).transpose(1, 0, 2)
        out.append(s.reshape(P, SLOT))
    return out


def _slots_out(w):
    kt = w.shape[0] // P
    per = (kt + 3) // 4
    out = []
    for h in range(2):
        t = np.zeros((per * 4, P, 512), w.dtype)
        t[:kt] = w[:, h * 512:h * 512 + 512].reshape(kt, P, 512)
        out += [t[4 * i:4 * i + 4].transpose(1, 0, 2).reshape(P, SLOT) for i in range(per)]
    return out


def _k_cols(w, cols):
    kt = w.shape[0] // P
    return w[:, cols].reshape(kt, P, len(cols)).transpose(1, 0, 2).reshape(P, SLOT)


def _rope(d_rot):
    n = d_rot // 4
    freq = np.float32(10000.0) ** (-np.arange(n, dtype=np.float32) / np.float32(n))
    row = np.repeat(np.arange(LAT // 64, dtype=np.float32), 64)
    col = np.tile(np.arange(64, dtype=np.float32), LAT // 64)
    ang = np.concatenate([row[:, None] * freq, col[:, None] * freq], -1).astype(np.float32)
    cs = np.stack([np.cos(ang), np.sin(ang)]).astype(np.float32)
    return np.ascontiguousarray(cs.reshape(2, LT, P, d_rot // 2).transpose(2, 0, 1, 3))


def kernel(x, c, ctx, c_ctx, mod_w, mod_b, norm_g, ffn_w_in, ffn_conv_w, ffn_conv_b, ffn_w_out,
           ev_w_in, ev_a_ln, ev_w_s, ev_b_s, ev_qk_g, ev_w_out,
           od_w_in, od_conv_w, od_conv_b, od_c_ln, od_g_cq, od_g_ckv, od_w_uq, od_w_ukv, od_w_out):
    import concourse.bacc as _bacc
    from concourse.bass_utils import run_bass_kernel_spmd as _run

    def cols(a):
        a = np.asarray(a)
        return np.ascontiguousarray(np.moveaxis(a.reshape(*a.shape[:-1], -1, P), -1, 0))

    def spread(a):
        return np.ascontiguousarray(np.broadcast_to(np.asarray(a)[None], (P, *a.shape)))

    ev, od = np.asarray(ev_w_in[0]), np.asarray(od_w_in[0])
    r = np.arange
    slots = _slots_in(ev, [r(2048, 2304), r(2304, 2560)] + [r(1024 + 256 * i, 1280 + 256 * i) for i in range(4)]
                      + [r(512, 768), r(768, 1024), r(0, 256), r(256, 512)])
    slots += _slots_out(np.asarray(ev_w_out[0]))

    def ffn(layer):
        w = np.asarray(ffn_w_in[layer])
        return _slots_in(w, [np.concatenate([r(P * j, P * j + P), r(FF + P * j, FF + P * j + P)]) for j in range(JF)]) \
            + _slots_out(np.asarray(ffn_w_out[layer]))
    slots += ffn(0)
    slots += _slots_in(od, [np.concatenate([r(P * j, P * j + P), r(512 + P * j, 512 + P * j + P)]) for j in range(4)]
                       + [r(1024, 1280), r(1280, 1536), r(1536, 1696), r(1696, 1856)])
    uq, ukv = np.asarray(od_w_uq[0]), np.asarray(od_w_ukv[0])
    slots += [_k_cols(uq, np.concatenate([r(192 * h, 192 * h + P) for h in range(4 * s, 4 * s + 4)])) for s in range(2)]
    slots += [_k_cols(uq, np.concatenate([r(192 * h + P, 192 * h + 192) for h in range(HEADS)]))]
    slots += [_k_cols(ukv, np.concatenate([r(256 * h, 256 * h + P) for h in range(4 * s, 4 * s + 4)]
                                          + [r(256 * h + P, 256 * h + 256) for h in range(4 * s, 4 * s + 4)]))
              for s in range(2)]
    slots += _slots_out(np.asarray(od_w_out[0]))
    slots += ffn(1)
    while len(slots) < NSLOT:
        slots.append(np.zeros((P, SLOT), np.float32))
    mw = np.asarray(mod_w).reshape(2, KD, P, MODT, P).transpose(0, 3, 2, 1, 4).reshape(2 * MODT, P, KD, P)
    cvec = np.stack([np.asarray(c)[0], np.asarray(c_ctx)]).reshape(2, KD, P).transpose(2, 1, 0)
    ffc = np.concatenate([np.asarray(ffn_conv_w), np.asarray(ffn_conv_b)[:, None]], 1)
    occ = np.concatenate([np.asarray(od_conv_w)[0], np.asarray(od_conv_b)], 0)
    arrays = dict(
        x=np.asarray(x)[0], ctx=np.asarray(ctx)[0], cvec=cvec, wpack=np.stack(slots), modw=mw,
        modb=cols(mod_b), normg=cols(norm_g),
        ffcw=cols(ffc).transpose(0, 1, 3, 2), rope_ev=_rope(128), rope_od=_rope(64),
        qkg=spread(np.asarray(ev_qk_g)[0]), aln=spread(np.asarray(ev_a_ln)[0]),
        wsT=np.asarray(ev_w_s)[0].transpose(2, 0, 1).reshape(P, 512),
        bs=spread(np.asarray(ev_b_s)[0].reshape(512)),
        odcw=cols(occ).transpose(0, 2, 1), odcln=cols(np.asarray(od_c_ln)[0]).transpose(0, 2, 1),
        gcq=cols(np.asarray(od_g_cq)[0]), gckv=cols(np.asarray(od_g_ckv)[0]),
    )
    arrays = {k: np.ascontiguousarray(v) for k, v in arrays.items()}
    nc = _bacc.Bacc("TRN2", target_bir_lowering=False, num_devices=1)
    args = [nc.dram_tensor(k, v.shape, mybir.dt.from_np(v.dtype), kind="ExternalInput").ap() for k, v in arrays.items()]
    args.append(nc.dram_tensor("out", (LAT, D), F32, kind="ExternalOutput").ap())
    build(nc, *args)
    got = _run(nc, [arrays], core_ids=[0])
    return got.results[0]["out"].reshape(1, LAT, D)
```

```python
from contextlib import ExitStack

import numpy as np

import concourse.bass as bass
from concourse import mybir

P = 128
F32 = mybir.dt.float32
F32R = mybir.dt.float32r
ALU = mybir.AluOpType
ACT = mybir.ActivationFunctionType
AX_X = mybir.AxisListType.X

D = 1024
KD = D // P
LAT, CTX = 512, 256
TOK = LAT + CTX
LT, NT = LAT // P, TOK // P
FF = 2816
JF = FF // P
HEADS = 8
SLOT = 2048
EPS = 1e-6
KIB = 1024

N_EVZ, N_OUT, N_FF1, N_FF2, N_ODZ, N_UQ, N_UKV = 10, 6, JF, 12, 8, 3, 2
N_MOD0 = 8
EV0 = N_MOD0
EVO0 = EV0 + N_EVZ
F10 = EVO0 + N_OUT
F20 = F10 + N_FF1
OD0 = F20 + N_FF2
UQ0 = OD0 + N_ODZ
UKV0 = UQ0 + N_UQ
ODO0 = UKV0 + N_UKV
F11 = ODO0 + N_OUT
F21 = F11 + N_FF1
NSLOT = F21 + N_FF2 + ((F21 + N_FF2) % 2)
MODG = 6 * D // 512
MODT = 4 * MODG
S4W = 68
NGRAN = (2 * MODG - 4) * KD


def build(nc, x, ctx, cvec, wpack, modw, modb, normg, ffcw, rope_ev, rope_od, qkg, aln, wsT, bs,
          odcw, odcln, gcq, gckv, out):
    es = ExitStack()
    with es:
        base = [16 * KIB + 128]
        uid = [0]

        def at(name, off, shape, dt=F32):
            return nc.alloc_sbuf_tensor_at(name, shape, dt, offset=base[0] + off)

        def sem(name):
            return es.enter_context(nc.semaphore(name))

        R_X, R_HT, R_A = 0, 24 * KIB, 72 * KIB
        R_RAW, R_WH, R_WL, R_MOD, R_GM, R_C = (138 * KIB, 154 * KIB, 170 * KIB, 186 * KIB, 194 * KIB, 202 * KIB)
        X = at("X", R_X, [P, NT, D])
        HTh = at("HTh", R_HT, [P, KD, TOK], F32R)
        HTl = at("HTl", R_HT + 24 * KIB, [P, KD, TOK], F32R)
        w_raw = [at(f"w_raw{i}", R_RAW + i * 8 * KIB, [P, SLOT]) for i in range(2)]
        w_hi = [at(f"w_hi{i}", R_WH + i * 8 * KIB, [P, SLOT], F32R) for i in range(2)]
        w_lo = [at(f"w_lo{i}", R_WL + i * 8 * KIB, [P, SLOT], F32R) for i in range(2)]
        m_raw = [at(f"m_raw{i}", R_MOD + 2 * i * KIB, [P, 512]) for i in range(2)]
        m_lo = [at(f"m_lo{i}", R_MOD + 2 * i * KIB, [P, 512], F32R) for i in range(2)]
        m_hi = [at(f"m_hi{i}", R_MOD + (4 + 2 * i) * KIB, [P, 512], F32R) for i in range(2)]
        m_row = at("m_row", R_GM + 6 * KIB, [P, 512])
        gmB = at("gmB", R_GM, [P, 2, D])
        c_off = [R_C]

        def const(name, shape, dt=F32):
            n = 4
            for s in shape[1:]:
                n *= s
            t = at(name, c_off[0], shape, dt)
            c_off[0] += (n + 31) // 32 * 32
            assert base[0] + c_off[0] <= nc.sbuf_usable_end, name
            return t

        ident = const("ident", [P, P])
        ones = const("ones", [P, P])
        modc = const("modc", [P, 2, MODT, 2])
        modb_sb = const("modb_sb", [P, 2, MODT])
        ng = const("ng", [P, 2, 4, KD])
        cw = const("cw", [P, 2, JF, 4])
        sT = const("sT", [P, KD, 2])
        s4 = const("s4", [P, 4 * (KD - 1) + S4W], F32R)
        s4v = s4[:, 0:4 * KD].rearrange("p (k c) -> p k c", c=4)
        sel = const("sel", [P, 2])
        prescale = const("prescale", [P, KD, 2])
        gmcol = const("gmcol", [P, KD, 2])
        ssq = const("ssq", [P, 64])
        rstd = const("rstd", [P, 64])
        halfneg = const("halfneg", [P, 64])
        cws = [const(f"cws{i}", [P, 4]) for i in range(2)]
        lnst = at("lnst", R_HT + 44 * KIB, [P, NT, 6])
        lnmv = at("lnmv", R_HT + 45 * KIB, [P, NT, 2])
        rmax = const("rmax", [P, 2])
        rsum = const("rsum", [P, 2])

        xn = at("xn", R_A, [P, NT, D])
        pre_tmp = [at(f"pre_tmp{i}", R_A + (24 + 3 * i) * KIB, [P, TOK]) for i in range(2)]
        junk = at("junk", R_A + 32 * KIB, [P, D])
        A_ff = at("A_ff", R_A, [P, JF, TOK])
        A_ff_lat = at("A_ff_lat", R_A, [P, JF, LAT])
        cat_ev = at("cat_ev", R_A, [P, 12, TOK])
        cat_od = at("cat_od", R_A, [P, 12, LAT])
        a_hi = [at(f"a_hi{i}", R_HT + 3 * i * KIB, [P, TOK], F32R) for i in range(2)]
        a_lo = [at(f"a_lo{i}", R_HT + (6 + 3 * i) * KIB, [P, TOK], F32R) for i in range(2)]
        O = at("O", R_HT + 12 * KIB, [P, NT, D])
        diag = at("diag", R_HT + 36 * KIB, [P, 4, P])
        junk2 = at("junk2", R_HT + 40 * KIB, [P, D])
        yb = [at(f"yb{i}", R_GM + 3 * i * KIB, [P, TOK]) for i in range(2)]
        Zv = at("Zv", R_A + 12 * KIB, [P, NT, 512])
        V32 = at("V32", R_A + 24 * KIB, [P, NT, 256])
        sA = at("sA", R_A + 30 * KIB, [P, 512])
        sB = at("sB", R_A + 32 * KIB, [P, 512])
        csn = at("csn", R_A + 34 * KIB, [P, 2, LT, 64])
        Zq = at("Zq", R_A + 36 * KIB, [P, NT, D])
        Kt = at("Kt", R_A + 60 * KIB, [P, NT, 256])
        qkgb = at("qkgb", R_GM, [P, 2, P])
        bsb = at("bsb", R_GM + 2 * KIB, [P, 512])
        alnb = at("alnb", R_HT + 24 * KIB, [P, 2, 512])
        ws_sb = at("ws_sb", R_HT + 28 * KIB, [P, 512])
        KT = at("KT", R_HT, [P, 2, TOK])
        Vev = at("Vev", R_HT + 6 * KIB, [P, NT, 256])
        PTe = [at(f"PTe{i}", R_HT + (12 + 3 * i) * KIB, [P, TOK]) for i in range(2)]
        Pe = [at(f"Pe{i}", R_HT + (24 + 3 * i) * KIB, [P, TOK]) for i in range(3)]
        qTe = [at(f"qTe{i}", R_HT + (36 + i) * KIB, [P, P]) for i in range(2)]
        sptmp = [at(f"sptmp{i}", R_HT + (40 + 2 * i) * KIB, [P, 4, P]) for i in range(2)]
        HALO = 15
        G = at("G", R_A + 24 * KIB, [P, 4, LAT + 2 * HALO])
        sg = [at(f"sg{i}", R_A + (57 + 2 * i) * KIB, [P, LAT]) for i in range(2)]
        cqh = at("cqh", R_A + 33 * KIB, [P, 4, LAT], F32R)
        cql = at("cql", R_A + 41 * KIB, [P, 4, LAT], F32R)
        zq = at("zq", R_GM, [P, LT, 512])
        zkv = at("zkv", R_MOD, [P, NT, 320])
        ckh = at("ckh", R_GM, [P, 2, TOK], F32R)
        ckl = at("ckl", R_A + 57 * KIB, [P, 2, TOK], F32R)
        KRT = at("KRT", R_A + 63 * KIB, [P, TOK])
        Vod = at("Vod", R_A + 33 * KIB, [P, NT, 1024])
        QTn = at("QTn", R_HT, [P, HEADS, LAT])
        QRT = at("QRT", R_HT + 16 * KIB, [P, 4, LAT])
        KTn = at("KTn", R_HT + 24 * KIB, [P, HEADS, TOK])
        QR = at("QR", R_MOD, [P, LT, 512])
        Pod = [at(f"Pod{i}", R_MOD + 3 * i * KIB, [P, TOK]) for i in range(2)]
        PTo = [at(f"PTo{i}", R_GM + 3 * i * KIB, [P, TOK]) for i in range(2)]
        ccw = const("ccw", [P, 4, 32])
        ccln = const("ccln", [P, 4, 2])
        gq = const("gq", [P, 4])
        gkv = const("gkv", [P, 2])
        nrm_t = at("nrm_t", R_HT, [P, LT, 512])
        nrm_k = at("nrm_k", R_HT + 8 * KIB, [P, NT, 256])
        kr2 = at("kr2", R_HT + 16 * KIB, [P, NT, P])
        ev_t = [at(f"ev_t{i}", R_HT + (20 + 3 * i) * KIB, [P, TOK]) for i in range(2)]
        csd = at("csd", R_HT + 28 * KIB, [P, 2, LT, 32])
        rA = at("rA", R_HT + 30 * KIB, [P, 256])
        rB = at("rB", R_HT + 31 * KIB, [P, 256])
        csd2 = at("csd2", R_HT + 40 * KIB, [P, 2, LT, 32])
        rA2 = at("rA2", R_HT + 42 * KIB, [P, 256])
        rB2 = at("rB2", R_HT + 43 * KIB, [P, 256])
        mu = at("mu", R_HT + 0, [P, LAT])
        sqs = at("sqs", R_HT + 4 * KIB, [P, 4, LAT])
        rs_b = at("rs_b", R_HT + 2 * KIB, [P, LAT])
        nh_b = at("nh_b", R_HT + 12 * KIB, [P, LAT])

        PS = es.enter_context(nc.psum_tensor("PS", [P, 8, 512], F32))
        MODBANK, SELBANK = 6, 7

        def ps2(b, n):
            return PS[:, b:b + 2, :].rearrange("p a b -> p (a b)")[:, 0:n]

        landed = [sem(f"landed{i}") for i in range(2)]
        wh_ready, wl_ready, w_used = sem("wh_ready"), sem("wl_ready"), sem("w_used")
        m_landed = [sem(f"m_landed{i}") for i in range(2)]
        m_hi_ready, m_lo_ready, m_used = sem("m_hi_ready"), sem("m_lo_ready"), sem("m_used")
        m_row_ready, m_sel_ready, m_evac = sem("m_row_ready"), sem("m_sel_ready"), sem("m_evac")
        m_started = sem("m_started")
        arrived = sem("arrived")
        consts, stored = sem("consts"), sem("stored")
        const_count = [0]
        phase = {}
        sems = {}

        def S(stage, what):
            return sems.setdefault((stage, what), sem(f"{stage}_{what}")) if (stage, what) not in sems else sems[(stage, what)]

        def barrier(eng, drains=True):
            k = phase.get(id(eng), 0) + 1
            phase[id(eng)] = k
            eng.drain().then_inc(arrived, 1)
            eng.wait_ge(arrived, 4 * k)

        def load_const(eng, dst, src):
            const_count[0] += 16
            eng.dma_start(dst, src).then_inc(consts, 16)

        def round_hi(act, n, u=0, i=None):
            r, more = n % 2, (0 if i is None else i)
            act.wait_ge(landed[r], (more + (n // 2 + 1)) * 16)
            if n >= 2:
                act.wait_ge(w_used, more * 2 + (n - 1))
            nc.scalar.activation(w_hi[r][:, :], w_raw[r][:, :], ACT.Copy).then_inc(wh_ready, 1)

        def take_lo(dve, n, i=None):
            r, more = n % 2, (0 if i is None else i)
            dve.wait_ge(wh_ready, more * 2 + (n + 1))
            nc.vector.tensor_tensor(w_lo[r][:, :], w_raw[r][:, :], w_hi[r][:, :].bitcast(F32),
                                    ALU.subtract).then_inc(wl_ready, 1)

        def weights(pe, n, i=None):
            pe.wait_ge(wl_ready, (0 if i is None else i) * 2 + (n + 1))

        def split_mm(outs, wh, wl, xs, start, stop):
            last = None
            for o, (xh, _) in zip(outs, xs):
                nc.tensor.matmul(o, wh, xh, start=start, stop=False)
            for o, (_, xl) in zip(outs, xs):
                nc.tensor.matmul(o, wh, xl, start=False, stop=False)
            for o, (xh, _) in zip(outs, xs):
                last = nc.tensor.matmul(o, wl, xh, start=False, stop=stop)
            return last

        def feature_slot(ns, n, tok, between=lambda step: None, pair=2):
            b, r = 3 * (ns % 2), n % 2
            last = None
            for mt in range(pair):
                for k in range(KD):
                    cols = slice(k * 256 + mt * P, k * 256 + mt * P + P)
                    outs = [PS[:, b + mt, :]]
                    xs = [(HTh[:, k, 0:LAT], HTl[:, k, 0:LAT])]
                    if tok > LAT:
                        outs.append(PS[:, b + 2, mt * 256:mt * 256 + 256])
                        xs.append((HTh[:, k, LAT:TOK], HTl[:, k, LAT:TOK]))
                    between(mt * KD + k)
                    last = split_mm(outs, w_hi[r][:, cols], w_lo[r][:, cols], xs, k == 0, k == KD - 1)
            return last

        def token_slot(ns, n, tiles, width, between=lambda step: None):
            b, r = 3 * (ns % 2), n % 2
            last = None
            for t in range(tiles):
                o = PS[:, b + t // 2, (t % 2) * 256:(t % 2) * 256 + width]
                for k in range(KD):
                    between(t * KD + k)
                    wc = slice(k * 256, k * 256 + width)
                    xh, xl = HTh[:, k, t * P:(t + 1) * P], HTl[:, k, t * P:(t + 1) * P]
                    nc.tensor.matmul(o, xh, w_hi[r][:, wc], start=k == 0, stop=False)
                    nc.tensor.matmul(o, xh, w_lo[r][:, wc], start=False, stop=False)
                    last = nc.tensor.matmul(o, xl, w_hi[r][:, wc], start=False, stop=k == KD - 1)
            return last

        def s4_wide(k):
            return s4[:, 4 * k:4 * k + S4W]

        def w_load(sp, n, i=None):
            r, more = n % 2, (0 if i is None else i)
            if n >= 2:
                sp.wait_ge(wl_ready, more * 2 + (n - 1))
            src = wpack[n] if i is None else wpack[bass.ds(i * 2 + n, 1)].rearrange("a p c -> (a p) c")
            sp.dma_start(w_raw[r][:, :], src).then_inc(landed[r], 16)

        def m_load(sp, q, i=None, step=0):
            r, more = q % 2, (0 if i is None else i)
            if q >= 2:
                sp.wait_ge(m_used, more * step + (q - 1))
            src = modw[q] if i is None else modw[bass.ds(i * step + q, 1)].rearrange("a p c -> (a p) c")
            sp.dma_start(m_raw[r][:, :], src).then_inc(m_landed[r], 16)

        def m_round(act, q, i=None):
            r, more = q % 2, (0 if i is None else i)
            act.wait_ge(m_landed[r], more * 64 + 16 * (q // 2 + 1))
            if q >= 2:
                act.wait_ge(m_used, more * 8 + (q - 1))
            nc.scalar.activation(m_hi[r][:, :], m_raw[r][:, :], ACT.Copy).then_inc(m_hi_ready, 1)

        def m_split(dve, q, i=None):
            r, more = q % 2, (0 if i is None else i)
            dve.wait_ge(m_hi_ready, more * 8 + (q + 1))
            nc.vector.tensor_tensor(m_lo[r][:, :], m_raw[r][:, :], m_hi[r][:, :].bitcast(F32), ALU.subtract)\
                .then_inc(m_lo_ready, 1)

        def m_product(pe, q, i=None):
            r, k, more = q % 2, q % KD, (0 if i is None else i)
            pe.wait_ge(m_lo_ready, more * 8 + (q + 1))
            if k == 0:
                pe.wait_ge(m_row_ready, more + (q // KD + 4))
            nc.tensor.matmul(PS[0:S4W, MODBANK, :], s4_wide(k), m_hi[r][:, :], start=k == 0, stop=False)
            nc.tensor.matmul(PS[0:S4W, MODBANK, :], s4_wide(k), m_lo[r][:, :], start=False, stop=k == KD - 1)\
                .then_inc(m_used, 1)

        def m_turn(pe, g, i=None):
            more = 0 if i is None else i
            pe.wait_ge(m_row_ready, more + (g + 1))
            if g > 0:
                pe.wait_ge(m_evac, more + g)
            for j in range(4):
                last = nc.tensor.matmul(PS[:, SELBANK, 2 * j:2 * j + 2], m_row[0:4, j * P:(j + 1) * P], sel[0:4, :],
                                        start=True, stop=True)
            last.then_inc(m_sel_ready, 1)

        def m_rows(dve, g, i=None):
            more = 0 if i is None else i
            if g >= 4:
                dve.wait_ge(m_used, more * 8 + (g - 3) * KD)
            if g > 0:
                dve.wait_ge(m_sel_ready, more + g)
            nc.vector.tensor_copy(m_row[0:4, :], PS[0:4, MODBANK, :]).then_inc(m_row_ready, 1)

        def m_columns(dve, g, i=None):
            more = 0 if i is None else i
            dve.wait_ge(m_sel_ready, more + (g + 1))
            layer, c0 = g // MODG, 4 * (g % MODG)
            cs = slice(c0, c0 + 4) if i is None else bass.ds(i * 4 + c0, 4)
            nc.vector.tensor_tensor(modc[:, layer, cs, :], PS[:, SELBANK, 0:8].rearrange("p (m s) -> p m s", s=2),
                                    modb_sb[:, layer, cs].unsqueeze(2).to_broadcast([P, 4, 2]), ALU.add).then_inc(m_evac, 1)

        def prenorm_dve(dve, st, layer, which):
            o = 3 * which
            nc.vector.scalar_tensor_tensor(
                out=prescale[:, :, :], in0=modc[:, layer, (o + 1) * KD:(o + 2) * KD, :], scalar=1.0,
                in1=ng[:, layer, 2 * which, :].unsqueeze(2).to_broadcast([P, KD, 2]), op0=ALU.add, op1=ALU.mult)
            dve.wait_ge(S(st, "ssq"), NT)
            nc.vector.tensor_scalar(rstd[:, 0:NT], ssq[:, 0:NT], 1.0 / D, EPS, ALU.mult, ALU.add)\
                .then_inc(S(st, "mean"), 1)
            dve.wait_ge(S(st, "rstd"), 1)
            for t in range(NT):
                nc.vector.tensor_scalar(xn[:, t, :], X[:, t, :], rstd[:, t:t + 1], None, ALU.mult)\
                    .then_inc(S(st, "xn"), 1)
            for k in range(KD):
                dve.wait_ge(S(st, "tr"), k + 1)
                if k >= 2:
                    dve.wait_ge(S(st, "hi"), k - 1)
                src, tmp = ps2(2 * (k % 2), TOK), pre_tmp[k % 2]
                for s, (a, b) in enumerate(((0, LAT), (LAT, TOK))):
                    last = nc.vector.tensor_scalar(tmp[:, a:b], src[:, a:b], prescale[:, k, s:s + 1],
                                                   modc[:, layer, o * KD + k, s:s + 1], ALU.mult, ALU.add)
                last.then_inc(S(st, "aff"), 1)
                dve.wait_ge(S(st, "hi"), k + 1)
                nc.vector.tensor_tensor(HTl[:, k, :], tmp[:, :], HTh[:, k, :].bitcast(F32), ALU.subtract)
                dve.drain()

        def prenorm_act(act, st):
            for t in range(NT):
                nc.scalar.activation(junk[:, :], X[:, t, :], ACT.Square, accum_out=ssq[:, t:t + 1])\
                    .then_inc(S(st, "ssq"), 1)
                act.drain()
            for k in range(KD):
                act.wait_ge(S(st, "aff"), k + 1)
                nc.scalar.activation(HTh[:, k, :], pre_tmp[k % 2][:, :], ACT.Copy).then_inc(S(st, "hi"), 1)

        def power(pool, st, n, what="mean", done="rstd", count=1):
            pool.wait_ge(S(st, what), count)
            nc.gpsimd.tensor_tensor(rstd[:, 0:n], rstd[:, 0:n], halfneg[:, 0:n], ALU.pow)\
                .then_inc(S(st, done), 1)

        def prenorm_pe(pe, st):
            pe.wait_ge(S(st, "xn"), NT)
            for k in range(KD):
                if k >= 2:
                    pe.wait_ge(S(st, "aff"), k - 1)
                for t in range(NT):
                    last = nc.tensor.transpose(ps2(2 * (k % 2), TOK)[:, t * P:(t + 1) * P],
                                               xn[:, t, k * P:(k + 1) * P], ident[:, :])
                last.then_inc(S(st, "tr"), 1)

        def out_ktiles(kt):
            per = (kt + 3) // 4
            return [(h * per + k // 4, k % 4, h, k) for h in range(2) for k in range(kt)]

        def out_pe(pe, st, n0, kt, tiles):
            for c in range(2 * 2):
                pe.wait_ge(S(st, "diag"), c + 1)
                nc.tensor.matmul(PS[:, 6 + c % 2, :], ones[:, :], diag[:, :, :].rearrange("p a b -> p (a b)"),
                                 start=True, stop=True).then_inc(S(st, "row"), 1)
            for q, (s, j, h, k) in enumerate(out_ktiles(kt)):
                n = n0 + s
                if j == 0:
                    weights(pe, n)
                pe.wait_ge(S(st, "a_lo"), q + 1)
                for t in range(tiles):
                    if h == 1 and k == 0:
                        pe.wait_ge(S(st, "o_copy"), t + 1)
                    tc = slice(t * P, (t + 1) * P)
                    wc = slice(j * 512, j * 512 + 512)
                    ah, al = a_hi[q % 2][:, tc], a_lo[q % 2][:, tc]
                    nc.tensor.matmul(PS[:, t, :], ah, w_hi[n % 2][:, wc], start=k == 0, stop=False)
                    nc.tensor.matmul(PS[:, t, :], ah, w_lo[n % 2][:, wc], start=False, stop=False)
                    last = nc.tensor.matmul(PS[:, t, :], al, w_hi[n % 2][:, wc], start=False, stop=k == kt - 1)
                last.then_inc(S(st, "a_used"), 1)
                if j == 3 or k == kt - 1:
                    pe.drain().then_inc(w_used, 1)

        def out_act(act, st, n0, kt, tiles, A):
            w = tiles * P
            for q, (s, j, h, k) in enumerate(out_ktiles(kt)):
                if j == 0:
                    if h == 0 and k == 0:
                        round_hi(act, n0)
                    if n0 + s + 1 < n0 + 2 * ((kt + 3) // 4):
                        round_hi(act, n0 + s + 1) if False else None
                if q >= 2:
                    act.wait_ge(S(st, "a_used"), q - 1)
                nc.scalar.activation(a_hi[q % 2][:, 0:w], A[:, k, :], ACT.Copy).then_inc(S(st, "a_hi"), 1)
                if (j == 2 or (k == kt - 1 and j < 2)) and s + 1 < 2 * ((kt + 3) // 4):
                    round_hi(act, n0 + s + 1)
            for h in range(2):
                for t in range(tiles):
                    act.wait_ge(S(st, "o_copy"), h * tiles + t + 1)
                    nc.scalar.activation(junk2[:, 0:512], O[:, t, h * 512:h * 512 + 512], ACT.Square,
                                         accum_out=ssq[:, 2 * t + h:2 * t + h + 1]).then_inc(S(st, "ssq"), 1)
                    act.drain()

        def out_dve(dve, st, n0, kt, tiles, A, layer, which):
            w = tiles * P
            gate = 3 * which + 2
            nc.vector.tensor_tensor(gmcol[:, :, :], modc[:, layer, gate * KD:(gate + 1) * KD, :],
                                    ng[:, layer, 2 * which + 1, :].unsqueeze(2).to_broadcast([P, KD, 2]), ALU.mult)
            for c in range(4):
                s, half = divmod(c, 2)
                dve.drain()
                nc.vector.tensor_tensor(
                    diag[:, :, :], ident[:, :].unsqueeze(1).to_broadcast([P, 4, P]),
                    gmcol[:, 4 * half:4 * half + 4, s:s + 1].to_broadcast([P, 4, P]), ALU.mult)\
                    .then_inc(S(st, "diag"), 1)
                dve.wait_ge(S(st, "row"), c + 1)
                nc.vector.tensor_copy(gmB[:, s, half * 512:half * 512 + 512], PS[:, 6 + c % 2, :])
            order = out_ktiles(kt)
            for q, (s, j, h, k) in enumerate(order):
                if h == 0 and k == 0:
                    take_lo(dve, n0)
                dve.wait_ge(S(st, "a_hi"), q + 1)
                nc.vector.tensor_tensor(a_lo[q % 2][:, 0:w], A[:, k, :], a_hi[q % 2][:, 0:w].bitcast(F32),
                                        ALU.subtract).then_inc(S(st, "a_lo"), 1)
                if (j == 2 or (k == kt - 1 and j < 2)) and s + 1 < 2 * ((kt + 3) // 4):
                    take_lo(dve, n0 + s + 1)
                if h == 1 and k == 0 or k == kt - 1 and h == 1:
                    pass
                if k == kt - 1:
                    dve.wait_ge(S(st, "a_used"), q + 1)
                    for t in range(tiles):
                        nc.vector.tensor_copy(O[:, t, h * 512:h * 512 + 512], PS[:, t, :])\
                            .then_inc(S(st, "o_copy"), 1)
            dve.wait_ge(S(st, "ssq"), 2 * tiles)
            pairs = ssq[:, 0:2 * tiles].rearrange("p (t h) -> p t h", h=2)
            nc.vector.tensor_tensor(rstd[:, 0:tiles], pairs[:, :, 0], pairs[:, :, 1], ALU.add)
            dve.drain()
            nc.vector.tensor_scalar(rstd[:, 0:tiles], rstd[:, 0:tiles], 1.0 / D, EPS, ALU.mult, ALU.add)\
                .then_inc(S(st, "mean"), 1)
            dve.wait_ge(S(st, "rstd"), 1)
            for t in range(tiles):
                s = 0 if t < LT else 1
                nc.vector.scalar_tensor_tensor(out=O[:, t, :], in0=O[:, t, :], scalar=rstd[:, t:t + 1],
                                               in1=gmB[:, s, :], op0=ALU.mult, op1=ALU.mult)
            dve.drain()
            for t in range(tiles):
                nc.vector.tensor_tensor(X[:, t, :], X[:, t, :], O[:, t, :], ALU.add)

        def ffn_grans(ns, q0):
            if q0 is None:
                return []
            return list(range(q0 + 8 * ns, q0 + 8 * ns + 8)) if ns < 2 else \
                list(range(q0 + 16 + 4 * (ns - 2), q0 + 16 + 4 * (ns - 2) + 4))

        def ffn_pe(pe, st, n0, tok, q0, g0):
            def slot(ns, i=None):
                n = n0 + ns
                weights(pe, n, i)
                if ns >= 2:
                    pe.wait_ge(S(st, "evac"), (0 if i is None else i * 2) + (ns - 1))
                grans = ffn_grans(ns, q0)
                places = (3, 4, 7, 8, 11, 12, 14, 15) if ns < 2 else (5, 7, 11, 13)

                def between(step):
                    if grans and step in places:
                        m_product(pe, grans[places.index(step)], i)
                    if q0 is not None and step == 10 and (ns == 1 or ns == 2):
                        m_turn(pe, g0 + ns - 1, i)
                feature_slot(ns, n, tok, between).then_inc(w_used, 1)
            slot(0)
            slot(1)
            with pe.Fori(0, JF // 2 - 1) as i:
                slot(2, i)
                slot(3, i)
            if q0 is not None:
                m_turn(pe, g0 + 11)

        def ffn_act(act, st, layer, n0, tok, q0):
            def slot(u, i, more):
                y, b = yb[u % 2], 3 * (u % 2)
                u2 = u % 2
                if more:
                    round_hi(act, n0 + u + 1, i=i)
                for q in ffn_grans(u, q0)[2 if u else 0:]:
                    m_round(act, q, i)
                ii = 0 if i is None else i
                act.wait_ge(S(st, "tap"), ii * 2 + (u + 1))
                act.wait_ge(w_used, ii * 2 + (n0 + u + 1))
                nc.scalar.activation(y[:, 0:LAT], PS[:, b, :], ACT.Identity, bias=cws[u2][:, 3:4], scale=cws[u2][:, 1:2])
                if tok > LAT:
                    nc.scalar.activation(y[:, LAT:TOK], PS[:, b + 2, 0:256], ACT.Identity, bias=cws[u2][:, 3:4],
                                         scale=cws[u2][:, 1:2])
                act.drain().then_inc(S(st, "mid"), 1)
                if more:
                    for q in ffn_grans(u + 1, q0)[:2]:
                        m_round(act, q, i)
                act.wait_ge(S(st, "conv"), ii * 2 + (u + 1))
                nc.scalar.activation(y[:, 0:tok], y[:, 0:tok], ACT.Silu).then_inc(S(st, "silu"), 1)
            round_hi(act, n0)
            slot(0, None, True)
            slot(1, None, True)
            with act.Fori(0, JF // 2 - 2) as i:
                slot(2, i, True)
                slot(3, i, True)
            slot(2, JF // 2 - 2, True)
            slot(3, JF // 2 - 2, False)

        def ffn_dve(dve, st, layer, n0, tok, A, q0, g0):
            def slot(u, i, more):
                y, b, u2 = yb[u % 2], 3 * (u % 2), u % 2
                ii = 0 if i is None else i
                if more:
                    take_lo(dve, n0 + u + 1, i)
                for q in ffn_grans(u, q0)[2 if u else 0:]:
                    m_split(dve, q, i)
                if q0 is not None and u in (1, 2):
                    m_columns(dve, g0 + u - 1, i)
                nc.vector.tensor_copy(cws[u2][:, :], cw[:, layer, bass.ds(ii * 2 + u, 1), :].rearrange("p a b -> p (a b)"))\
                    .then_inc(S(st, "tap"), 1)
                dve.wait_ge(S(st, "mid"), ii * 2 + (u + 1))
                streams = ((0, LAT, PS[:, b, :]),) + (((LAT, TOK, PS[:, b + 2, 0:256]),) if tok > LAT else ())
                for w, dst, src in ((0, 1, 0), (2, 0, 1)):
                    for a, e, g in streams:
                        n = e - a - 1
                        last = nc.vector.scalar_tensor_tensor(
                            out=y[:, a + dst:a + dst + n], in0=g[:, src:src + n], scalar=cws[u2][:, w:w + 1],
                            in1=y[:, a + dst:a + dst + n], op0=ALU.mult, op1=ALU.add)
                    if w == 0:
                        dve.drain()
                last.then_inc(S(st, "conv"), 1)
                if q0 is not None and u in (0, 1, 3):
                    m_rows(dve, g0 + (u if u < 2 else 2), i)
                if more:
                    for q in ffn_grans(u + 1, q0)[:2]:
                        m_split(dve, q, i)
                dve.wait_ge(S(st, "silu"), ii * 2 + (u + 1))
                parts = ((0, LAT, PS[:, b + 1, :]),) + (((LAT, TOK, PS[:, b + 2, 256:512]),) if tok > LAT else ())
                for a, e, z in parts:
                    last = nc.vector.tensor_tensor(
                        A[:, bass.ds(ii * 2 + u, 1), a:e].rearrange("p a b -> p (a b)"), y[:, a:e], z, ALU.mult)
                last.then_inc(S(st, "evac"), 1)
            take_lo(dve, n0)
            slot(0, None, True)
            slot(1, None, True)
            with dve.Fori(0, JF // 2 - 2) as i:
                slot(2, i, True)
                slot(3, i, True)
            slot(2, JF // 2 - 2, True)
            slot(3, JF // 2 - 2, False)
            if q0 is not None:
                m_columns(dve, g0 + 11)

        def units(odd):
            lat = [(h, t, NT, 0) for h in range(HEADS) for t in range(LT)]
            return lat if odd else lat + [(h, t, 2, LT) for h in range(HEADS) for t in range(LT, NT)]

        def attn_pe(pe, st, odd):
            U = units(odd)
            PT, Pb, V = (PTo, Pod, Vod) if odd else (PTe, Pe, Vev)

            def q_transpose(u):
                h, t, nk, k0 = U[u]
                if u >= 1:
                    pe.wait_ge(S(st, "qT"), u)
                nc.tensor.transpose(PS[:, 6, 0:P], Zq[:, t, h * P:(h + 1) * P], ident[:, :]).then_inc(S(st, "qtr"), 1)

            def scores(u):
                h, t, nk, k0 = U[u]
                if not odd:
                    pe.wait_ge(S(st, "qT"), u + 1)
                if u >= 2:
                    pe.wait_ge(S(st, "exp"), u - 1)
                for a, e in (((0, 512), (512, 768)) if nk == NT else ((0, 256),)):
                    ks = slice(k0 * P + a, k0 * P + e)
                    o = PS[:, 2 * (u % 2) + a // 512, 0:e - a]
                    if odd:
                        qs = slice(t * P, (t + 1) * P)
                        r = slice(64 * (h % 2), 64 * (h % 2) + 64)
                        nc.tensor.matmul(o, QTn[:, h, qs], KTn[:, h, ks], start=True, stop=False)
                        last = nc.tensor.matmul(o, QRT[r, h // 2, qs], KRT[r, ks], start=False, stop=True)
                    else:
                        last = nc.tensor.matmul(o, qTe[u % 2][:, :], KT[:, h // 4, ks], start=True, stop=True)
                last.then_inc(S(st, "s"), 1)

            for u in range(2):
                if not odd:
                    q_transpose(u)
                scores(u)
            if not odd:
                q_transpose(2)
            for u, (h, t, nk, k0) in enumerate(U):
                pe.wait_ge(S(st, "p"), u + 1)
                if u >= 1:
                    pe.wait_ge(S(st, "pT"), u)
                for j in range(nk):
                    last = nc.tensor.transpose(ps2(4, TOK)[:, j * P:(j + 1) * P], Pb[u % len(Pb)][:, j * P:(j + 1) * P],
                                               ident[:, :])
                last.then_inc(S(st, "ptr"), 1)
                if u + 2 < len(U):
                    scores(u + 2)
                if u + 3 < len(U) and not odd:
                    q_transpose(u + 3)
                pe.wait_ge(S(st, "pT"), u + 1)
                if u >= 1:
                    pe.wait_ge(S(st, "ocopy"), u)
                for j in range(nk):
                    c = h * P if odd else (h // 4) * P
                    last = nc.tensor.matmul(PS[:, 7, 0:P], V[:, k0 + j, c:c + P], PT[u % 2][:, j * P:(j + 1) * P],
                                            start=j == 0, stop=j == nk - 1)
                last.then_inc(S(st, "o"), 1)

        def attn_act(act, st, odd, scale):
            U = units(odd)
            PT, Pb = (PTo, Pod) if odd else (PTe, Pe)

            def q_copy(u):
                act.wait_ge(S(st, "qtr"), u + 1)
                if u >= 2:
                    act.wait_ge(S(st, "s"), u - 1)
                nc.scalar.activation(qTe[u % 2][:, :], PS[:, 6, 0:P], ACT.Copy).then_inc(S(st, "qT"), 1)

            def exps(u):
                nk = U[u][2]
                if u >= len(Pb):
                    act.wait_ge(S(st, "ptr"), u - len(Pb) + 1)
                act.wait_ge(S(st, "max"), u + 1)
                nc.scalar.activation(Pb[u % len(Pb)][:, 0:nk * P], ps2(2 * (u % 2), nk * P), ACT.Exp,
                                     bias=rmax[:, u % 2:u % 2 + 1], scale=scale,
                                     accum_out=rsum[:, u % 2:u % 2 + 1]).then_inc(S(st, "exp"), 1)
            if not odd:
                for u in range(3):
                    q_copy(u)
            exps(0)
            for u, (h, t, nk, k0) in enumerate(U):
                if u + 1 < len(U):
                    exps(u + 1)
                act.wait_ge(S(st, "ptr"), u + 1)
                if u >= 2:
                    act.wait_ge(S(st, "o"), u - 1)
                nc.scalar.activation(PT[u % 2][:, 0:nk * P], ps2(4, nk * P), ACT.Copy).then_inc(S(st, "pT"), 1)
                if u + 3 < len(U) and not odd:
                    q_copy(u + 3)

        def attn_dve(dve, st, odd, scale, cat, extra):
            U = units(odd)
            Pb = Pod if odd else Pe

            def maxima(u):
                dve.wait_ge(S(st, "s"), u + 1)
                if u >= 2:
                    dve.wait_ge(S(st, "exp"), u - 1)
                m = rmax[:, u % 2:u % 2 + 1]
                nc.vector.reduce_max(m, ps2(2 * (u % 2), U[u][2] * P), AX_X)
                dve.drain()
                nc.vector.tensor_scalar(m, m, -scale, None, ALU.mult).then_inc(S(st, "max"), 1)

            def normalise(u):
                dve.wait_ge(S(st, "exp"), u + 1)
                sm, pr = rsum[:, u % 2:u % 2 + 1], Pb[u % len(Pb)][:, 0:U[u][2] * P]
                nc.vector.reciprocal(sm, sm)
                dve.drain()
                nc.vector.tensor_scalar(pr, pr, sm, None, ALU.mult).then_inc(S(st, "p"), 1)

            maxima(0)
            maxima(1)
            normalise(0)
            for u, (h, t, nk, k0) in enumerate(U):
                if u + 1 < len(U):
                    normalise(u + 1)
                if u + 2 < len(U):
                    maxima(u + 2)
                extra(u)
                dve.wait_ge(S(st, "o"), u + 1)
                nc.vector.tensor_copy(cat[:, 4 + h, t * P:(t + 1) * P], PS[:, 7, 0:P]).then_inc(S(st, "ocopy"), 1)

        def rotate(dve, x0, x1, cs, sn, tA, tB):
            nc.vector.tensor_tensor(tA, x1, sn, ALU.mult)
            nc.vector.tensor_tensor(tB, x0, sn, ALU.mult)
            nc.vector.tensor_tensor(x0, x0, cs, ALU.mult)
            nc.vector.tensor_tensor(x1, x1, cs, ALU.mult)
            dve.drain()
            nc.vector.tensor_tensor(x0, x0, tA, ALU.subtract)
            nc.vector.tensor_tensor(x1, x1, tB, ALU.add)
            dve.drain()

        block = es.enter_context(nc.Block())

        @block.sync
        def _(sp):
            w_load(sp, 0)
            w_load(sp, 1)
            with sp.Fori(0, N_MOD0 // 2) as i:
                for u in range(2):
                    w_load(sp, 2 + u, i)
            m_load(sp, 0)
            m_load(sp, 1)
            with sp.Fori(0, 4) as i:
                for u in range(2):
                    w_load(sp, EV0 + 2 + u, i)
                    for r in range(8):
                        m_load(sp, 2 + 8 * u + r, i, 16)
            n = EV0 + 2 + 8
            with sp.Fori(0, (F10 + 2 - n) // 2) as i:
                for u in range(2):
                    w_load(sp, n + u, i)
            q = 8 * KD + 2
            for u in range(2):
                w_load(sp, F10 + 2 + u)
                for r in range(8):
                    m_load(sp, q + 8 * u + r)
            q += 16
            with sp.Fori(0, JF // 2 - 2) as i:
                for u in range(2):
                    w_load(sp, F10 + 4 + u, i)
                    for r in range(4):
                        m_load(sp, q + 4 * u + r, i, 8)
            n, q = F10 + JF, q + 8 * (JF // 2 - 2)
            for u in range(2):
                w_load(sp, n + u)
            while q < NGRAN:
                m_load(sp, q)
                q += 1
            n += 2
            with sp.Fori(0, (NSLOT - n) // 2) as i:
                for u in range(2):
                    w_load(sp, n + u, i)
            sp.wait_ge(S("end", "x"), 1)
            sp.dma_start(out.rearrange("(t p) d -> p t d", p=P), X[:, 0:LT, :]).then_inc(stored, 16)
            sp.wait_ge(stored, 16)

        @block.gpsimd
        def _(pool):
            nc.gpsimd.memset(ident[:, :], 0.0)
            nc.gpsimd.memset(ones[:, :], 1.0)
            nc.gpsimd.memset(halfneg[:, :], -0.5)
            pool.drain()
            nc.gpsimd.affine_select(out=ident[:, :], in_=ident[:, :], compare_op=ALU.not_equal, fill=1.0,
                                    base=0, pattern=[[-1, P]], channel_multiplier=1).then_inc(S("init", "ident"), 1)
            barrier(pool)
            power(pool, "pre0", NT)
            barrier(pool)
            power(pool, "evz", 60)
            barrier(pool)
            power(pool, "gate", NT)
            barrier(pool)
            barrier(pool)
            power(pool, "evo", NT)
            barrier(pool)
            power(pool, "pre1", NT)
            barrier(pool)
            barrier(pool)
            power(pool, "ffo0", NT)
            barrier(pool)
            power(pool, "pre2", NT)
            barrier(pool)
            barrier(pool)
            power(pool, "odn", LT + NT)
            barrier(pool)
            barrier(pool)
            barrier(pool)
            barrier(pool)
            barrier(pool)
            power(pool, "odo", LT)
            barrier(pool)
            power(pool, "pre3", NT)
            barrier(pool)
            barrier(pool)
            power(pool, "ffo1", LT)

        @block.scalar
        def _(act):
            load_const(act, sT[:, :, :], cvec)
            load_const(act, modb_sb[:, :, :], modb)
            load_const(act, ng[:, :, :, :], normg)
            load_const(act, cw[:, :, :, :], ffcw)
            load_const(act, ccw[:, :, :], odcw)
            load_const(act, ccln[:, :, :], odcln)
            load_const(act, gq[:, :], gcq)
            load_const(act, gkv[:, :], gckv)
            load_const(act, X[:, 0:LT, :], x.rearrange("(t p) d -> p t d", p=P))
            load_const(act, X[:, LT:NT, :], ctx.rearrange("(t p) d -> p t d", p=P))
            act.wait_ge(consts, const_count[0])
            nc.scalar.activation(sT[:, :, :], sT[:, :, :], ACT.Silu)
            act.drain()
            nc.scalar.activation(s4v[:, :, 0:2], sT[:, :, :], ACT.Copy).then_inc(S("init", "silu"), 1)
            for n in range(N_MOD0):
                round_hi(act, n)
            barrier(act)
            prenorm_act(act, "pre0")
            barrier(act)
            load_const(act, csn[:, :, :, :], rope_ev)
            load_const(act, qkgb[:, :, :], qkg)
            load_const(act, bsb[:, :], bs)
            round_hi(act, EV0)
            for s in range(N_EVZ):
                if s + 1 < N_EVZ:
                    round_hi(act, EV0 + s + 1)
                if s < 8:
                    for q in range(8 * s, 8 * s + 8):
                        m_round(act, q)
                b = 3 * (s % 2)
                if s in (0, 2, 3, 4, 5):
                    act.wait_ge(S("evz", "copy"), s + 1)
                    for t in range(NT):
                        for hh in range(2):
                            src = Kt[:, t, hh * P:hh * P + P] if s == 0 else \
                                Zq[:, t, (s - 2) * 256 + hh * P:(s - 2) * 256 + hh * P + P]
                            c = t * 10 + (8 + hh if s == 0 else 2 * (s - 2) + hh)
                            j4 = (2 * t + hh) % 4
                            nc.scalar.activation(sA[:, j4 * P:(j4 + 1) * P], src, ACT.Square, accum_out=ssq[:, c:c + 1])
                        if t % 2:
                            act.drain()
                    act.drain().then_inc(S("evz", "ssq"), 1)
                if s in (6, 7):
                    act.wait_ge(w_used, EV0 + s + 1)
                    for i in range(3):
                        nc.scalar.activation(Zv[:, 2 * i:2 * i + 2, (s - 6) * 256:(s - 6) * 256 + 256],
                                             PS[:, b + i, :].rearrange("p (a b) -> p a b", a=2), ACT.Gelu_apprx_tanh)
                    act.drain().then_inc(S("evz", "gelu"), 1)
                if s in (8, 9):
                    act.wait_ge(w_used, EV0 + s + 1)
                    for mt in range(2):
                        g = 2 * (s - 8) + mt
                        nc.scalar.activation(cat_ev[:, g, 0:LAT], PS[:, b + mt, :], ACT.Gelu_apprx_tanh)
                        nc.scalar.activation(cat_ev[:, g, LAT:TOK], PS[:, b + 2, mt * 256:mt * 256 + 256],
                                             ACT.Gelu_apprx_tanh)
            barrier(act)
            load_const(act, alnb[:, :, :], aln)
            load_const(act, ws_sb[:, :], wsT)
            for g in range(2):
                act.wait_ge(S("gate", "ktr"), g + 1)
                nc.scalar.activation(KT[:, g, :], ps2(6, TOK), ACT.Copy).then_inc(S("gate", "kT"), 1)
            barrier(act)
            attn_act(act, "eva", False, P ** -0.5)
            barrier(act)
            out_act(act, "evo", EVO0, 12, NT, cat_ev)
            barrier(act)
            prenorm_act(act, "pre1")
            barrier(act)
            ffn_act(act, "ff0", 0, F10, TOK, 8 * KD)
            barrier(act)
            out_act(act, "ffo0", F20, JF, NT, A_ff)
            barrier(act)
            prenorm_act(act, "pre2")
            barrier(act)
            round_hi(act, OD0)
            for s in range(N_ODZ):
                if s + 1 < N_ODZ:
                    round_hi(act, OD0 + s + 1)
                if s < 4:
                    act.wait_ge(w_used, OD0 + s + 1)
                    if s >= 2:
                        act.wait_ge(S("odz", "evac"), s - 1)
                    nc.scalar.activation(sg[s % 2][:, :], PS[:, 3 * (s % 2) + 1, :], ACT.Sigmoid)\
                        .then_inc(S("odz", "sg"), 1)
            barrier(act)
            load_const(act, csd[:, :, :, :], rope_od)
            for t in range(LT):
                nc.scalar.activation(ev_t[0][:, 0:512], zq[:, t, :], ACT.Square, accum_out=ssq[:, t:t + 1])
                act.drain()
            for t in range(NT):
                nc.scalar.activation(ev_t[0][:, 0:256], zkv[:, t, 0:256], ACT.Square,
                                     accum_out=ssq[:, LT + t:LT + t + 1])
                act.drain()
            act.drain().then_inc(S("odn", "ssq"), 1)
            for k in range(6):
                act.wait_ge(S("odn", "aff"), k + 1)
                if k < 4:
                    nc.scalar.activation(cqh[:, k, :], ev_t[k % 2][:, 0:LAT], ACT.Copy).then_inc(S("odn", "hi"), 1)
                else:
                    nc.scalar.activation(ckh[:, k - 4, :], ev_t[k % 2][:, :], ACT.Copy).then_inc(S("odn", "hi"), 1)
            barrier(act)
            load_const(act, csd2[:, :, :, :], rope_od)
            for n in range(UQ0, UQ0 + 3):
                round_hi(act, n)
            barrier(act)
            for n in range(UKV0, UKV0 + 2):
                round_hi(act, n)
            barrier(act)
            attn_act(act, "oda", True, 192 ** -0.5)
            barrier(act)
            for j in range(4):
                act.wait_ge(S("cln", "cent"), j + 1)
                nc.scalar.activation(sqs[:, j, :], cat_od[:, j, :], ACT.Square).then_inc(S("cln", "sq"), 1)
            for j in range(4):
                if j == 0:
                    act.wait_ge(S("cln", "var"), 1)
                    nc.scalar.activation(nh_b[:, :], rs_b[:, :], ACT.Sqrt).then_inc(S("cln", "rstd"), 1)
                act.wait_ge(S("cln", "nrm"), j + 1)
                nc.scalar.activation(cat_od[:, j, :], cat_od[:, j, :], ACT.Silu, bias=ccln[:, j, 1:2],
                                     scale=ccln[:, j, 0:1])
            barrier(act)
            out_act(act, "odo", ODO0, 12, LT, cat_od)
            barrier(act)
            prenorm_act(act, "pre3")
            barrier(act)
            ffn_act(act, "ff1", 1, F11, LAT, None)
            barrier(act)
            out_act(act, "ffo1", F21, JF, LT, A_ff_lat)



        @block.tensor
        def _(pe):
            pe.wait_ge(S("init", "s4"), 1)
            for n in range(N_MOD0):
                g, r = n // 2, n % 2
                weights(pe, n)
                if r == 0 and g > 0:
                    pe.wait_ge(m_row_ready, g)
                for kk in range(4):
                    k, cols = 4 * r + kk, slice(kk * 512, kk * 512 + 512)
                    nc.tensor.matmul(PS[0:S4W, MODBANK, :], s4_wide(k), w_hi[r][:, cols], start=k == 0, stop=False)
                    last = nc.tensor.matmul(PS[0:S4W, MODBANK, :], s4_wide(k), w_lo[r][:, cols], start=False,
                                            stop=k == KD - 1)
                last.then_inc(w_used, 1)
                if r == 1:
                    m_turn(pe, g)
            barrier(pe)
            prenorm_pe(pe, "pre0")
            barrier(pe)
            for s in range(N_EVZ):
                n = EV0 + s
                weights(pe, n)
                if s >= 2:
                    if s - 2 < 6:
                        pe.wait_ge(S("evz", "copy"), s - 1)
                    else:
                        pe.wait_ge(S("evz", "gelu"), s - 7)
                def between(step):
                    if s < 8 and step % 6 == 5:
                        m_product(pe, 8 * s + step // 6)
                    if 1 <= s <= 8 and step == 2:
                        m_turn(pe, 3 + s)
                (feature_slot(s, n, TOK, between) if s >= 8 else token_slot(s, n, NT, 256, between)).then_inc(w_used, 1)
            barrier(pe)
            for g in range(2):
                if g:
                    pe.wait_ge(S("gate", "kT"), g)
                for t in range(NT):
                    last = nc.tensor.transpose(ps2(6, TOK)[:, t * P:(t + 1) * P], Kt[:, t, g * P:(g + 1) * P],
                                               ident[:, :])
                last.then_inc(S("gate", "ktr"), 1)
            pe.wait_ge(S("gate", "ws"), 1)
            for c in range(NT):
                pe.wait_ge(S("gate", "vn"), c + 1)
                for g in range(4):
                    last = nc.tensor.matmul(PS[:, c, g * P:(g + 1) * P], Zv[:, c, g * P:(g + 1) * P],
                                            ws_sb[:, g * P:(g + 1) * P], start=True, stop=True)
                last.then_inc(S("gate", "sp"), 1)
            barrier(pe)
            attn_pe(pe, "eva", False)
            barrier(pe)
            out_pe(pe, "evo", EVO0, 12, NT)
            barrier(pe)
            prenorm_pe(pe, "pre1")
            barrier(pe)
            ffn_pe(pe, "ff0", F10, TOK, 8 * KD, MODG)
            barrier(pe)
            out_pe(pe, "ffo0", F20, JF, NT)
            barrier(pe)
            prenorm_pe(pe, "pre2")
            barrier(pe)
            for s in range(N_ODZ):
                n = OD0 + s
                weights(pe, n)
                if s >= 2:
                    pe.wait_ge(S("odz", "evac"), s - 1)
                if s < 4:
                    last = feature_slot(s, n, LAT)
                elif s < 6:
                    last = token_slot(s, n, LT, 256)
                else:
                    last = token_slot(s, n, NT, 160)
                last.then_inc(w_used, 1)
            barrier(pe)
            pe.wait_ge(S("odn", "xn"), 1)
            for k in range(7):
                if k >= 2:
                    pe.wait_ge(S("odn", "aff"), k - 1)
                b = 2 * (k % 2)
                for t in range(LT if k < 4 else NT):
                    src = nrm_t[:, t, k * P:(k + 1) * P] if k < 4 else \
                        (nrm_k[:, t, (k - 4) * P:(k - 3) * P] if k < 6 else kr2[:, t, :])
                    last = nc.tensor.transpose(ps2(b, TOK)[:, t * P:(t + 1) * P], src, ident[:, :])
                last.then_inc(S("odn", "tr"), 1)
            barrier(pe)
            for s in range(2):
                n = UQ0 + s
                weights(pe, n)
                for hh in range(4):
                    h = 4 * s + hh
                    if h >= 4:
                        pe.wait_ge(S("odu", "q"), h - 3)
                    for k in range(4):
                        cols = slice(k * 512 + hh * P, k * 512 + (hh + 1) * P)
                        last = split_mm([PS[:, h % 4, :]], w_hi[n % 2][:, cols], w_lo[n % 2][:, cols],
                                        [(cqh[:, k, :], cql[:, k, :])], k == 0, k == 3)
                    last.then_inc(S("odu", "qmm"), 1)
                pe.drain().then_inc(w_used, 1)
            n = UQ0 + 2
            weights(pe, n)
            for t in range(LT):
                for k in range(4):
                    wc, tc = slice(k * 512, k * 512 + 512), slice(t * P, (t + 1) * P)
                    nc.tensor.matmul(PS[:, 4 + t, :], cqh[:, k, tc], w_hi[n % 2][:, wc], start=k == 0, stop=False)
                    nc.tensor.matmul(PS[:, 4 + t, :], cqh[:, k, tc], w_lo[n % 2][:, wc], start=False, stop=False)
                    last = nc.tensor.matmul(PS[:, 4 + t, :], cql[:, k, tc], w_hi[n % 2][:, wc], start=False, stop=k == 3)
                last.then_inc(S("odu", "rmm"), 1)
            pe.drain().then_inc(w_used, 1)
            pe.wait_ge(S("odu", "rope"), LT)
            for p in range(4):
                if p >= 0:
                    pe.wait_ge(S("odu", "q"), 8 if p < 4 else 8)
                for t in range(LT):
                    last = nc.tensor.transpose(PS[:, p, t * P:(t + 1) * P], QR[:, t, p * P:(p + 1) * P], ident[:, :])
                last.then_inc(S("odu", "rtr"), 1)
            barrier(pe)
            for s in range(2):
                n = UKV0 + s
                weights(pe, n)
                for hh in range(4):
                    q = 4 * s + hh
                    if q >= 2:
                        pe.wait_ge(S("odk", "k"), q - 1)
                    b = 2 * (q % 2)
                    for k in range(2):
                        cols = slice(k * 1024 + hh * P, k * 1024 + (hh + 1) * P)
                        last = split_mm([PS[:, b, :], PS[:, b + 1, 0:256]], w_hi[n % 2][:, cols], w_lo[n % 2][:, cols],
                                        [(ckh[:, k, 0:LAT], ckl[:, k, 0:LAT]), (ckh[:, k, LAT:TOK], ckl[:, k, LAT:TOK])],
                                        k == 0, k == 1)
                    last.then_inc(S("odk", "kmm"), 1)
                for t in range(NT):
                    q = NT * s + t
                    if q >= 4:
                        pe.wait_ge(S("odk", "v"), q - 3)
                    o = PS[:, 4 + q % 4, :]
                    for k in range(2):
                        wc, tc = slice(k * 1024 + 512, k * 1024 + 1024), slice(t * P, (t + 1) * P)
                        nc.tensor.matmul(o, ckh[:, k, tc], w_hi[n % 2][:, wc], start=k == 0, stop=False)
                        nc.tensor.matmul(o, ckh[:, k, tc], w_lo[n % 2][:, wc], start=False, stop=False)
                        last = nc.tensor.matmul(o, ckl[:, k, tc], w_hi[n % 2][:, wc], start=False, stop=k == 1)
                    last.then_inc(S("odk", "vmm"), 1)
                pe.drain().then_inc(w_used, 1)
            barrier(pe)
            attn_pe(pe, "oda", True)
            barrier(pe)
            for j in range(4):
                last = nc.tensor.matmul(PS[:, 0, :], ones[:, :], cat_od[:, j, :], start=j == 0, stop=j == 3)
            last.then_inc(S("cln", "sum"), 1)
            for j in range(4):
                pe.wait_ge(S("cln", "sq"), j + 1)
                last = nc.tensor.matmul(PS[:, 1, :], ones[:, :], sqs[:, j, :], start=j == 0, stop=j == 3)
            last.then_inc(S("cln", "sum2"), 1)
            barrier(pe)
            out_pe(pe, "odo", ODO0, 12, LT)
            barrier(pe)
            prenorm_pe(pe, "pre3")
            barrier(pe)
            ffn_pe(pe, "ff1", F11, LAT, None, None)
            barrier(pe)
            out_pe(pe, "ffo1", F21, JF, LT)

        @block.vector
        def _(dve):
            dve.wait_ge(consts, 16 * 10)
            dve.wait_ge(S("init", "silu"), 1)
            nc.vector.memset(s4[:, 4 * KD:].bitcast(F32), 0.0)
            nc.vector.tensor_tensor(s4v[:, :, 2:4], sT[:, :, :], s4v[:, :, 0:2].bitcast(F32), ALU.subtract)
            dve.wait_ge(S("init", "ident"), 1)
            nc.vector.tensor_tensor(sel[0:4, :], ident[0:4, 0:2], ident[0:4, 2:4], ALU.add)
            dve.drain().then_inc(S("init", "s4"), 1)
            for n in range(N_MOD0):
                take_lo(dve, n)
                if n % 2:
                    dve.wait_ge(w_used, n + 1)
                    m_rows(dve, n // 2)
                    m_columns(dve, n // 2)
            barrier(dve)
            prenorm_dve(dve, "pre0", 0, 0)
            barrier(dve)
            take_lo(dve, EV0)
            for s in range(N_EVZ):
                if s + 1 < N_EVZ:
                    take_lo(dve, EV0 + s + 1)
                if s < 8:
                    for q in range(8 * s, 8 * s + 8):
                        m_split(dve, q)
                        if q % 8 == 1 and s >= 1:
                            m_columns(dve, 3 + s)
                    m_rows(dve, 4 + s)
                if s == 8:
                    m_columns(dve, 11)
                b = 3 * (s % 2)
                if s < 6:
                    dve.wait_ge(w_used, EV0 + s + 1)
                    for i in range(3):
                        dst = (Kt if s == 0 else V32)[:, 2 * i:2 * i + 2, :] if s < 2 else \
                            Zq[:, 2 * i:2 * i + 2, (s - 2) * 256:(s - 1) * 256]
                        last = nc.vector.tensor_copy(dst, PS[:, b + i, :].rearrange("p (a b) -> p a b", a=2))
                    last.then_inc(S("evz", "copy"), 1)
                if s == 7:
                    dve.wait_ge(S("evz", "ssq"), 5)
                    nc.vector.tensor_scalar(rstd[:, 0:60], ssq[:, 0:60], 1.0 / P, EPS, ALU.mult, ALU.add)\
                        .then_inc(S("evz", "mean"), 1)
            dve.wait_ge(S("evz", "rstd"), 1)
            dve.wait_ge(consts, 16 * 13)
            for t in range(NT):
                q3 = Zq[:, t, :].rearrange("p (h d) -> p h d", d=P)
                k3 = Kt[:, t, :].rearrange("p (h d) -> p h d", d=P)
                nc.vector.tensor_tensor(q3, q3, rstd[:, 10 * t:10 * t + 8].unsqueeze(2).to_broadcast([P, 8, P]), ALU.mult)
                nc.vector.tensor_tensor(k3, k3, rstd[:, 10 * t + 8:10 * t + 10].unsqueeze(2).to_broadcast([P, 2, P]),
                                        ALU.mult)
                dve.drain()
                nc.vector.tensor_tensor(q3, q3, qkgb[:, 0, :].unsqueeze(1).to_broadcast([P, 8, P]), ALU.mult)
                nc.vector.tensor_tensor(k3, k3, qkgb[:, 1, :].unsqueeze(1).to_broadcast([P, 2, P]), ALU.mult)
                dve.drain()
                if t < LT:
                    for z, nh in ((Zq, 8), (Kt, 2)):
                        zz = z[:, t, :].rearrange("p (h i two) -> p h i two", i=64, two=2)
                        cs = csn[:, 0, t, :].unsqueeze(1).to_broadcast([P, nh, 64])
                        sn = csn[:, 1, t, :].unsqueeze(1).to_broadcast([P, nh, 64])
                        tA = sA[:, 0:nh * 64].rearrange("p (h i) -> p h i", i=64)
                        tB = sB[:, 0:nh * 64].rearrange("p (h i) -> p h i", i=64)
                        rotate(dve, zz[:, :, :, 0], zz[:, :, :, 1], cs, sn, tA, tB)
            barrier(dve)
            nc.vector.tensor_copy(Vev[:, :, :], V32[:, :, :])
            dve.wait_ge(consts, 16 * 15)
            nc.vector.tensor_copy(ws_sb[:, 0:1], ws_sb[:, 0:1]).then_inc(S("gate", "ws"), 1)
            for t in range(NT):
                nc.vector.bn_stats(lnst[:, t, :], Zv[:, t, :])
            dve.drain()
            for t in range(NT):
                nc.vector.bn_aggr(lnmv[:, t, :], lnst[:, t, :])
            dve.drain()
            nc.vector.tensor_scalar(rstd[:, 0:NT], lnmv[:, :, 1], 1.0, EPS, ALU.mult, ALU.add)\
                .then_inc(S("gate", "mean"), 1)
            dve.wait_ge(S("gate", "rstd"), 1)
            for t in range(NT):
                nc.vector.tensor_scalar(Zv[:, t, :], Zv[:, t, :], lnmv[:, t, 0:1], rstd[:, t:t + 1],
                                        ALU.subtract, ALU.mult)
                dve.drain()
                nc.vector.tensor_tensor(Zv[:, t, :], Zv[:, t, :], alnb[:, 0, :], ALU.mult)
                dve.drain()
                nc.vector.tensor_tensor(Zv[:, t, :], Zv[:, t, :], alnb[:, 1, :], ALU.add).then_inc(S("gate", "vn"), 1)
            for c in range(NT):
                dve.wait_ge(S("gate", "sp"), c + 1)
                tmp = sptmp[c % 2]
                nc.vector.tensor_tensor(tmp[:, :, :], PS[:, c, :].rearrange("p (g q) -> p g q", q=P),
                                        bsb[:, :].rearrange("p (g q) -> p g q", q=P), ALU.add)
                dve.drain()
                cc = cat_ev[:, 0:4, c * P:(c + 1) * P]
                nc.vector.tensor_tensor(cc, cc, tmp[:, :, :], ALU.mult)
            barrier(dve)
            attn_dve(dve, "eva", False, P ** -0.5, cat_ev, lambda u: None)
            barrier(dve)
            out_dve(dve, "evo", EVO0, 12, NT, cat_ev, 0, 0)
            barrier(dve)
            prenorm_dve(dve, "pre1", 0, 1)
            barrier(dve)
            ffn_dve(dve, "ff0", 0, F10, TOK, A_ff, 8 * KD, MODG)
            barrier(dve)
            out_dve(dve, "ffo0", F20, JF, NT, A_ff, 0, 1)
            barrier(dve)
            prenorm_dve(dve, "pre2", 1, 0)
            barrier(dve)
            nc.vector.memset(G[:, :, 0:HALO], 0.0)
            nc.vector.memset(G[:, :, HALO + LAT:], 0.0)
            take_lo(dve, OD0)
            for s in range(N_ODZ):
                if s + 1 < N_ODZ:
                    take_lo(dve, OD0 + s + 1)
                b = 3 * (s % 2)
                dve.wait_ge(w_used, OD0 + s + 1)
                if s < 4:
                    dve.wait_ge(S("odz", "sg"), s + 1)
                    nc.vector.tensor_tensor(G[:, s, HALO:HALO + LAT], PS[:, b, :], sg[s % 2][:, :], ALU.mult)\
                        .then_inc(S("odz", "evac"), 1)
                elif s < 6:
                    for i in range(2):
                        last = nc.vector.tensor_copy(zq[:, 2 * i:2 * i + 2, (s - 4) * 256:(s - 3) * 256],
                                                     PS[:, b + i, :].rearrange("p (a b) -> p a b", a=2))
                    last.then_inc(S("odz", "evac"), 1)
                else:
                    for i in range(3):
                        last = nc.vector.tensor_copy(zkv[:, 2 * i:2 * i + 2, (s - 6) * 160:(s - 5) * 160],
                                                     PS[:, b + i, :].rearrange("p (a b) -> p a b", a=2)[:, :, 0:160])
                    last.then_inc(S("odz", "evac"), 1)
            barrier(dve)
            dve.wait_ge(S("odn", "ssq"), 1)
            nc.vector.tensor_scalar(rstd[:, 0:LT], ssq[:, 0:LT], 1.0 / 512, EPS, ALU.mult, ALU.add)
            nc.vector.tensor_scalar(rstd[:, LT:LT + NT], ssq[:, LT:LT + NT], 1.0 / 256, EPS, ALU.mult, ALU.add)
            dve.drain().then_inc(S("odn", "mean"), 1)
            dve.wait_ge(S("odn", "rstd"), 1)
            dve.wait_ge(consts, 16 * 16)
            for t in range(LT):
                nc.vector.tensor_scalar(nrm_t[:, t, :], zq[:, t, :], rstd[:, t:t + 1], None, ALU.mult)
                kr = zkv[:, t, 256:320].rearrange("p (i two) -> p i two", two=2)
                rotate(dve, kr[:, :, 0], kr[:, :, 1], csd[:, 0, t, :], csd[:, 1, t, :], rA[:, 0:32], rB[:, 0:32])
            for t in range(NT):
                nc.vector.tensor_scalar(nrm_k[:, t, :], zkv[:, t, 0:256], rstd[:, LT + t:LT + t + 1], None, ALU.mult)
                for half in range(2):
                    nc.vector.tensor_copy(kr2[:, t, 64 * half:64 * half + 64], zkv[:, t, 256:320])
            dve.drain().then_inc(S("odn", "xn"), 1)
            for k in range(7):
                dve.wait_ge(S("odn", "tr"), k + 1)
                src = ps2(2 * (k % 2), TOK)
                if k == 6:
                    nc.vector.tensor_copy(KRT[:, :], src)
                    continue
                if k >= 2:
                    dve.wait_ge(S("odn", "hi"), k - 1)
                w = LAT if k < 4 else TOK
                g = gq[:, k:k + 1] if k < 4 else gkv[:, k - 4:k - 3]
                nc.vector.tensor_scalar(ev_t[k % 2][:, 0:w], src[:, 0:w], g, None, ALU.mult).then_inc(S("odn", "aff"), 1)
                dve.wait_ge(S("odn", "hi"), k + 1)
                hi, lo = (cqh[:, k, :], cql[:, k, :]) if k < 4 else (ckh[:, k - 4, :], ckl[:, k - 4, :])
                nc.vector.tensor_tensor(lo, ev_t[k % 2][:, 0:w], hi.bitcast(F32), ALU.subtract)
                dve.drain()
            barrier(dve)
            for s in range(3):
                take_lo(dve, UQ0 + s)
                if s == 2:
                    break
                if s == 1:
                    for h in range(4):
                        dve.wait_ge(S("odu", "qmm"), h + 1)
                        nc.vector.tensor_copy(QTn[:, h, :], PS[:, h % 4, :]).then_inc(S("odu", "q"), 1)
            for h in range(4, HEADS):
                dve.wait_ge(S("odu", "qmm"), h + 1)
                nc.vector.tensor_copy(QTn[:, h, :], PS[:, h % 4, :]).then_inc(S("odu", "q"), 1)
            dve.wait_ge(consts, 16 * 17)
            for t in range(LT):
                dve.wait_ge(S("odu", "rmm"), t + 1)
                nc.vector.tensor_copy(QR[:, t, :], PS[:, 4 + t, :])
                dve.drain()
                zz = QR[:, t, :].rearrange("p (h i two) -> p h i two", i=32, two=2)
                rotate(dve, zz[:, :, :, 0], zz[:, :, :, 1], csd2[:, 0, t, :].unsqueeze(1).to_broadcast([P, 8, 32]),
                       csd2[:, 1, t, :].unsqueeze(1).to_broadcast([P, 8, 32]),
                       rA2[:, :].rearrange("p (h i) -> p h i", i=32), rB2[:, :].rearrange("p (h i) -> p h i", i=32))
                dve.drain().then_inc(S("odu", "rope"), 1)
            for p in range(4):
                dve.wait_ge(S("odu", "rtr"), p + 1)
                nc.vector.tensor_copy(QRT[:, p, :], PS[:, p, :])
            barrier(dve)
            for s in range(2):
                take_lo(dve, UKV0 + s)
            for s in range(2):
                for hh in range(4):
                    q = 4 * s + hh
                    dve.wait_ge(S("odk", "kmm"), q + 1)
                    nc.vector.tensor_copy(KTn[:, q, :], ps2(2 * (q % 2), TOK)).then_inc(S("odk", "k"), 1)
                for t in range(NT):
                    q = NT * s + t
                    dve.wait_ge(S("odk", "vmm"), q + 1)
                    nc.vector.tensor_copy(Vod[:, t, 512 * s:512 * s + 512], PS[:, 4 + q % 4, :])\
                        .then_inc(S("odk", "v"), 1)
            barrier(dve)

            def conv_taps(u):
                for tap in range(u, min(u + 1, 31)):
                    for j in range(4):
                        g, w = G[:, j, tap:tap + LAT], ccw[:, j, tap:tap + 1]
                        if tap == 0:
                            nc.vector.tensor_scalar(cat_od[:, j, :], g, w, ccw[:, j, 31:32], ALU.mult, ALU.add)
                        else:
                            nc.vector.scalar_tensor_tensor(out=cat_od[:, j, :], in0=g, scalar=w, in1=cat_od[:, j, :],
                                                           op0=ALU.mult, op1=ALU.add)
                    dve.drain()

            attn_dve(dve, "oda", True, 192 ** -0.5, cat_od, conv_taps)
            barrier(dve)
            dve.wait_ge(S("cln", "sum"), 1)
            nc.vector.tensor_scalar(mu[:, :], PS[:, 0, :], 1.0 / 512, None, ALU.mult)
            dve.drain()
            for j in range(4):
                nc.vector.tensor_tensor(cat_od[:, j, :], cat_od[:, j, :], mu[:, :], ALU.subtract)\
                    .then_inc(S("cln", "cent"), 1)
            dve.wait_ge(S("cln", "sum2"), 1)
            nc.vector.tensor_scalar(mu[:, :], PS[:, 1, :], 1.0 / 512, EPS, ALU.mult, ALU.add)
            dve.drain()
            nc.vector.reciprocal(rs_b[:, :], mu[:, :]).then_inc(S("cln", "var"), 1)
            dve.wait_ge(S("cln", "rstd"), 1)
            nc.vector.tensor_tensor(rs_b[:, :], nh_b[:, :], nh_b[:, :], ALU.mult)
            dve.drain()
            nc.vector.tensor_tensor(rs_b[:, :], rs_b[:, :], mu[:, :], ALU.mult)
            dve.drain()
            nc.vector.tensor_scalar(rs_b[:, :], rs_b[:, :], -0.5, 1.5, ALU.mult, ALU.add)
            dve.drain()
            nc.vector.tensor_tensor(rs_b[:, :], rs_b[:, :], nh_b[:, :], ALU.mult)
            dve.drain()
            for j in range(4):
                nc.vector.tensor_tensor(cat_od[:, j, :], cat_od[:, j, :], rs_b[:, :], ALU.mult)\
                    .then_inc(S("cln", "nrm"), 1)
            barrier(dve)
            out_dve(dve, "odo", ODO0, 12, LT, cat_od, 1, 0)
            barrier(dve)
            prenorm_dve(dve, "pre3", 1, 1)
            barrier(dve)
            ffn_dve(dve, "ff1", 1, F11, LAT, A_ff_lat, None, None)
            barrier(dve)
            out_dve(dve, "ffo1", F21, JF, LT, A_ff_lat, 1, 1)
            dve.drain().then_inc(S("end", "x"), 1)


def _slots_in(w, groups):
    out = []
    for cols in groups:
        s = np.zeros((P, KD, 256), w.dtype)
        s[:, :, :len(cols)] = w[:, cols].reshape(KD, P, len(cols)).transpose(1, 0, 2)
        out.append(s.reshape(P, SLOT))
    return out


def _slots_out(w):
    kt = w.shape[0] // P
    per = (kt + 3) // 4
    out = []
    for h in range(2):
        t = np.zeros((per * 4, P, 512), w.dtype)
        t[:kt] = w[:, h * 512:h * 512 + 512].reshape(kt, P, 512)
        out += [t[4 * i:4 * i + 4].transpose(1, 0, 2).reshape(P, SLOT) for i in range(per)]
    return out


def _k_cols(w, cols):
    kt = w.shape[0] // P
    return w[:, cols].reshape(kt, P, len(cols)).transpose(1, 0, 2).reshape(P, SLOT)


def _rope(d_rot):
    n = d_rot // 4
    freq = np.float32(10000.0) ** (-np.arange(n, dtype=np.float32) / np.float32(n))
    row = np.repeat(np.arange(LAT // 64, dtype=np.float32), 64)
    col = np.tile(np.arange(64, dtype=np.float32), LAT // 64)
    ang = np.concatenate([row[:, None] * freq, col[:, None] * freq], -1).astype(np.float32)
    cs = np.stack([np.cos(ang), np.sin(ang)]).astype(np.float32)
    return np.ascontiguousarray(cs.reshape(2, LT, P, d_rot // 2).transpose(2, 0, 1, 3))


def kernel(x, c, ctx, c_ctx, mod_w, mod_b, norm_g, ffn_w_in, ffn_conv_w, ffn_conv_b, ffn_w_out,
           ev_w_in, ev_a_ln, ev_w_s, ev_b_s, ev_qk_g, ev_w_out,
           od_w_in, od_conv_w, od_conv_b, od_c_ln, od_g_cq, od_g_ckv, od_w_uq, od_w_ukv, od_w_out):
    import concourse.bacc as _bacc
    from concourse.bass_utils import run_bass_kernel_spmd as _run

    def cols(a):
        a = np.asarray(a)
        return np.ascontiguousarray(np.moveaxis(a.reshape(*a.shape[:-1], -1, P), -1, 0))

    def spread(a):
        return np.ascontiguousarray(np.broadcast_to(np.asarray(a)[None], (P, *a.shape)))

    ev, od = np.asarray(ev_w_in[0]), np.asarray(od_w_in[0])
    r = np.arange
    mw = np.asarray(mod_w).reshape(2, KD, P, MODG, 512).transpose(0, 3, 1, 2, 4).reshape(2 * MODG, KD, P, 512)
    slots = [mw[g, 4 * i:4 * i + 4].transpose(1, 0, 2).reshape(P, SLOT) for g in range(4) for i in range(2)]
    slots += _slots_in(ev, [r(2048, 2304), r(2304, 2560)] + [r(1024 + 256 * i, 1280 + 256 * i) for i in range(4)]
                      + [r(512, 768), r(768, 1024), r(0, 256), r(256, 512)])
    slots += _slots_out(np.asarray(ev_w_out[0]))

    def ffn(layer):
        w = np.asarray(ffn_w_in[layer])
        return _slots_in(w, [np.concatenate([r(P * j, P * j + P), r(FF + P * j, FF + P * j + P)]) for j in range(JF)]) \
            + _slots_out(np.asarray(ffn_w_out[layer]))
    slots += ffn(0)
    slots += _slots_in(od, [np.concatenate([r(P * j, P * j + P), r(512 + P * j, 512 + P * j + P)]) for j in range(4)]
                       + [r(1024, 1280), r(1280, 1536), r(1536, 1696), r(1696, 1856)])
    uq, ukv = np.asarray(od_w_uq[0]), np.asarray(od_w_ukv[0])
    slots += [_k_cols(uq, np.concatenate([r(192 * h, 192 * h + P) for h in range(4 * s, 4 * s + 4)])) for s in range(2)]
    slots += [_k_cols(uq, np.concatenate([r(192 * h + P, 192 * h + 192) for h in range(HEADS)]))]
    slots += [_k_cols(ukv, np.concatenate([r(256 * h, 256 * h + P) for h in range(4 * s, 4 * s + 4)]
                                          + [r(256 * h + P, 256 * h + 256) for h in range(4 * s, 4 * s + 4)]))
              for s in range(2)]
    slots += _slots_out(np.asarray(od_w_out[0]))
    slots += ffn(1)
    while len(slots) < NSLOT:
        slots.append(np.zeros((P, SLOT), np.float32))
    cvec = np.stack([np.asarray(c)[0], np.asarray(c_ctx)]).reshape(2, KD, P).transpose(2, 1, 0)
    ffc = np.concatenate([np.asarray(ffn_conv_w), np.asarray(ffn_conv_b)[:, None]], 1)
    occ = np.concatenate([np.asarray(od_conv_w)[0], np.asarray(od_conv_b)], 0)
    arrays = dict(
        x=np.asarray(x)[0], ctx=np.asarray(ctx)[0], cvec=cvec, wpack=np.stack(slots), modw=mw[4:].reshape(NGRAN, P, 512),
        modb=cols(mod_b), normg=cols(norm_g),
        ffcw=cols(ffc).transpose(0, 1, 3, 2), rope_ev=_rope(128), rope_od=_rope(64),
        qkg=spread(np.asarray(ev_qk_g)[0]), aln=spread(np.asarray(ev_a_ln)[0]),
        wsT=np.asarray(ev_w_s)[0].transpose(2, 0, 1).reshape(P, 512),
        bs=spread(np.asarray(ev_b_s)[0].reshape(512)),
        odcw=cols(occ).transpose(0, 2, 1), odcln=cols(np.asarray(od_c_ln)[0]).transpose(0, 2, 1),
        gcq=cols(np.asarray(od_g_cq)[0]), gckv=cols(np.asarray(od_g_ckv)[0]),
    )
    arrays = {k: np.ascontiguousarray(v) for k, v in arrays.items()}
    nc = _bacc.Bacc("TRN2", target_bir_lowering=False, num_devices=1)
    args = [nc.dram_tensor(k, v.shape, mybir.dt.from_np(v.dtype), kind="ExternalInput").ap() for k, v in arrays.items()]
    args.append(nc.dram_tensor("out", (LAT, D), F32, kind="ExternalOutput").ap())
    build(nc, *args)
    got = _run(nc, [arrays], core_ids=[0])
    return got.results[0]["out"].reshape(1, LAT, D)
```

```python
from contextlib import ExitStack

import numpy as np

import concourse.bass as bass
from concourse import mybir

P = 128
F32 = mybir.dt.float32
F32R = mybir.dt.float32r
ALU = mybir.AluOpType
ACT = mybir.ActivationFunctionType
AX_X = mybir.AxisListType.X

D = 1024
KD = D // P
LAT, CTX = 512, 256
TOK = LAT + CTX
LT, NT = LAT // P, TOK // P
FF = 2816
JF = FF // P
HEADS = 8
SLOT = 2048
EPS = 1e-6
KIB = 1024

N_EVZ, N_OUT, N_FF1, N_FF2, N_ODZ, N_UQ, N_UKV = 10, 6, JF, 12, 8, 3, 2
N_MOD0 = 8
EV0 = N_MOD0
EVO0 = EV0 + N_EVZ
F10 = EVO0 + N_OUT
F20 = F10 + N_FF1
OD0 = F20 + N_FF2
UQ0 = OD0 + N_ODZ
UKV0 = UQ0 + N_UQ
ODO0 = UKV0 + N_UKV
F11 = ODO0 + N_OUT
F21 = F11 + N_FF1
NSLOT = F21 + N_FF2
MODG = 6 * D // 512
MODT = 4 * MODG
S4W = 68
NGRAN = (2 * MODG - 4) * KD


def build(nc, x, ctx, cvec, wpack, modw, modb, normg, ffcw, rope_ev, rope_od, qkg, aln, wsT, bs,
          odcw, odcln, gcq, gckv, out):
    es = ExitStack()
    with es:
        BASE = 16 * KIB + 128

        def at(name, off, shape, dt=F32):
            return nc.alloc_sbuf_tensor_at(name, shape, dt, offset=BASE + off)

        def sem(name):
            return es.enter_context(nc.semaphore(name))

        R_X, R_HT, R_A = 0, 24 * KIB, 72 * KIB
        R_RAW, R_WH, R_WL, R_MOD, R_GM, R_C = (138 * KIB, 154 * KIB, 170 * KIB, 186 * KIB, 194 * KIB, 202 * KIB)
        X = at("X", R_X, [P, NT, D])
        HTh = at("HTh", R_HT, [P, KD, TOK], F32R)
        HTl = at("HTl", R_HT + 24 * KIB, [P, KD, TOK], F32R)
        w_raw = [at(f"w_raw{i}", R_RAW + i * 8 * KIB, [P, SLOT]) for i in range(2)]
        w_hi = [at(f"w_hi{i}", R_WH + i * 8 * KIB, [P, SLOT], F32R) for i in range(2)]
        w_lo = [at(f"w_lo{i}", R_WL + i * 8 * KIB, [P, SLOT], F32R) for i in range(2)]
        m_raw = [at(f"m_raw{i}", R_MOD + 2 * i * KIB, [P, 512]) for i in range(2)]
        m_lo = [at(f"m_lo{i}", R_MOD + 2 * i * KIB, [P, 512], F32R) for i in range(2)]
        m_hi = [at(f"m_hi{i}", R_MOD + (4 + 2 * i) * KIB, [P, 512], F32R) for i in range(2)]
        m_row = at("m_row", R_GM + 6 * KIB, [P, 512])
        gmB = at("gmB", R_GM, [P, 2, D])
        c_off = [R_C]

        def const(name, shape, dt=F32):
            n = 4
            for s in shape[1:]:
                n *= s
            t = at(name, c_off[0], shape, dt)
            c_off[0] += (n + 31) // 32 * 32
            assert BASE + c_off[0] <= nc.sbuf_usable_end, name
            return t

        ident = const("ident", [P, P])
        ones = const("ones", [P, P])
        modc = const("modc", [P, 2, MODT, 2])
        modb_sb = const("modb_sb", [P, 2, MODT])
        ng = const("ng", [P, 2, 4, KD])
        cw = const("cw", [P, 2, JF, 4])
        sT = const("sT", [P, KD, 2])
        s4 = const("s4", [P, 4 * (KD - 1) + S4W], F32R)
        s4v = s4[:, 0:4 * KD].rearrange("p (k c) -> p k c", c=4)
        sel = const("sel", [P, 2])
        prescale = const("prescale", [P, KD, 2])
        gmcol = const("gmcol", [P, KD, 2])
        ssq = const("ssq", [P, 64])
        rstd = const("rstd", [P, 64])
        halfneg = const("halfneg", [P, 64])
        cws = [const(f"cws{i}", [P, 4]) for i in range(2)]
        lnst = at("lnst", R_GM + KIB, [P, NT, 6])
        lnmv = at("lnmv", R_GM + KIB + 512, [P, NT, 2])
        rmax = const("rmax", [P, 2])
        rsum = const("rsum", [P, 2])

        xn = at("xn", R_A, [P, NT, D])
        pre_tmp = [at(f"pre_tmp{i}", R_A + (24 + 3 * i) * KIB, [P, TOK]) for i in range(4)]
        junk = at("junk", R_A + 32 * KIB, [P, D])
        mod_raw = [at(f"mod_raw{i}", R_HT + 8 * i * KIB if i < 6 else R_A + (40 + 8 * (i - 6)) * KIB, [P, SLOT])
                   for i in range(N_MOD0)]
        A_ff = at("A_ff", R_A, [P, JF, TOK])
        A_ff_lat = at("A_ff_lat", R_A, [P, JF, LAT])
        cat_ev = at("cat_ev", R_A, [P, 12, TOK])
        cat_od = at("cat_od", R_A, [P, 12, LAT])
        a_hi = [at(f"a_hi{i}", R_HT + 3 * i * KIB, [P, TOK], F32R) for i in range(2)]
        a_lo = [at(f"a_lo{i}", R_HT + (6 + 3 * i) * KIB, [P, TOK], F32R) for i in range(2)]
        O = at("O", R_HT + 12 * KIB, [P, NT, D])
        diag = at("diag", R_HT + 36 * KIB, [P, 4, P])
        junk3 = at("junk3", R_HT + 44 * KIB, [P, D])
        junk2 = at("junk2", R_HT + 40 * KIB, [P, D])
        yb = [at(f"yb{i}", R_GM + 3 * i * KIB, [P, TOK]) for i in range(2)]
        Zv = at("Zv", R_A + 12 * KIB, [P, NT, 512])
        V32 = at("V32", R_A + 24 * KIB, [P, NT, 256])
        sA = at("sA", R_A + 30 * KIB, [P, 512])
        sB = at("sB", R_A + 32 * KIB, [P, 512])
        csn = at("csn", R_A + 34 * KIB, [P, 2, LT, 64])
        Zq = at("Zq", R_A + 36 * KIB, [P, NT, D])
        Kt = at("Kt", R_A + 60 * KIB, [P, NT, 256])
        qkgb = at("qkgb", R_GM, [P, 2, P])
        bsb = at("bsb", R_GM + 2 * KIB, [P, 512])
        alnb = at("alnb", R_A + 30 * KIB, [P, 2, 512])
        ws_sb = at("ws_sb", R_GM + 4 * KIB, [P, 512])
        KTh = at("KTh", R_HT, [P, 2, TOK], F32R)
        KTl = at("KTl", R_HT + 18 * KIB, [P, 2, TOK], F32R)
        Vev = at("Vev", R_HT + 6 * KIB, [P, NT, 256])
        PTe = [at(f"PTe{i}", R_HT + (12 + 3 * i) * KIB, [P, TOK]) for i in range(2)]
        Pe = [at(f"Pe{i}", R_HT + (24 + 3 * i) * KIB, [P, TOK]) for i in range(3)]
        qTh = [at(f"qTh{i}", R_HT + (36 + i) * KIB, [P, P], F32R) for i in range(2)]
        qTl = [at(f"qTl{i}", R_HT + (38 + i) * KIB, [P, P], F32R) for i in range(2)]
        sptmp = [at(f"sptmp{i}", R_HT + (40 + 2 * i) * KIB, [P, 4, P]) for i in range(2)]
        HALO = 15
        G = at("G", R_A + 24 * KIB, [P, 4, LAT + 2 * HALO])
        sg = [at(f"sg{i}", R_A + (57 + 2 * i) * KIB, [P, LAT]) for i in range(2)]
        cqh = at("cqh", R_A + 33 * KIB, [P, 4, LAT], F32R)
        cql = at("cql", R_A + 41 * KIB, [P, 4, LAT], F32R)
        zq = at("zq", R_GM, [P, LT, 512])
        zkv = at("zkv", R_MOD, [P, NT, 320])
        ckh = at("ckh", R_GM, [P, 2, TOK], F32R)
        ckl = at("ckl", R_A + 57 * KIB, [P, 2, TOK], F32R)
        KRT = at("KRT", R_A + 63 * KIB, [P, TOK])
        Vod = at("Vod", R_A + 33 * KIB, [P, NT, 1024])
        QTn = at("QTn", R_HT, [P, HEADS, LAT])
        QRT = at("QRT", R_HT + 16 * KIB, [P, 4, LAT])
        KTn = at("KTn", R_HT + 24 * KIB, [P, HEADS, TOK])
        QR = at("QR", R_MOD, [P, LT, 512])
        Pod = [at(f"Pod{i}", R_MOD + 3 * i * KIB, [P, TOK]) for i in range(2)]
        PTo = [at(f"PTo{i}", R_GM + 3 * i * KIB, [P, TOK]) for i in range(2)]
        ccw = const("ccw", [P, 4, 32])
        ccln = const("ccln", [P, 4, 2])
        gq = const("gq", [P, 4])
        gkv = const("gkv", [P, 2])
        kr2 = at("kr2", R_A + 52 * KIB, [P, NT, P])
        ev_t = [at(f"ev_t{i}", R_A + (8 + 3 * i) * KIB, [P, TOK]) for i in range(2)]
        csd = at("csd", R_A + 49 * KIB, [P, 2, LT, 32])
        rA = at("rA", R_A + 50 * KIB, [P, 256])
        rB = at("rB", R_A + 51 * KIB, [P, 256])
        mu = at("mu", R_A + 24 * KIB, [P, LAT])
        rs_b = at("rs_b", R_A + 26 * KIB, [P, LAT])
        nh_b = at("nh_b", R_A + 28 * KIB, [P, LAT])
        sqs = [at(f"sqs{j}", R_A + (57 + 2 * j if j < 3 else 30) * KIB, [P, LAT]) for j in range(4)]

        PS = es.enter_context(nc.psum_tensor("PS", [P, 8, 512], F32))
        MODBANK, SELBANK = 6, 7

        def ps2(b, n):
            return PS[:, b:b + 2, :].rearrange("p a b -> p (a b)")[:, 0:n]

        landed = [sem(f"landed{i}") for i in range(2)]
        wh_ready, wl_ready, w_used = sem("wh_ready"), sem("wl_ready"), sem("w_used")
        m_landed = [sem(f"m_landed{i}") for i in range(2)]
        m_hi_ready, m_lo_ready, m_used = sem("m_hi_ready"), sem("m_lo_ready"), sem("m_used")
        m_row_ready, m_sel_ready, m_evac = sem("m_row_ready"), sem("m_sel_ready"), sem("m_evac")
        arrived = sem("arrived")
        mod_landed = [sem(f"mod_landed{i}") for i in range(N_MOD0)]
        stored = sem("stored")
        phase = {}
        sems = {}

        def gate_chunks(tiles):
            return [(s, half) for s in range(1 if tiles == LT else 2) for half in range(2)]

        NORMS = {"pre0": NT, "pre1": NT, "pre2": NT, "pre3": LT}
        OUTS = {"evo": (12, NT), "ffo0": (JF, NT), "odo": (12, LT), "ffo1": (JF, LT)}

        def adds(stage, what):
            if stage in NORMS:
                return {"tr": KD, "hi": KD, "aff": KD, "lo_odd": KD // 2, "lo_even": KD // 2}.get(what, NORMS[stage])
            kt, tiles = OUTS[stage]
            return {"diag": len(gate_chunks(tiles)), "row": len(gate_chunks(tiles)),
                    "a_hi": 2 * kt, "a_lo": 2 * kt, "a_used": 2 * kt, "acc": 2 * tiles, "ssq": 2 * tiles,
                    "o_copy": 2 * tiles}.get(what, tiles)

        def family(stage):
            return NORMS if stage in NORMS else (OUTS if stage in OUTS else None)

        def S(stage, what):
            name = {id(NORMS): "pre", id(OUTS): "out"}.get(id(family(stage)), stage)
            if (name, what) not in sems:
                sems[(name, what)] = sem(f"{name}_{what}")
            return sems[(name, what)]

        def since(stage, what):
            stages = family(stage)
            return sum(adds(other, what) for other in list(stages)[:list(stages).index(stage)])

        def barrier(eng):
            k = phase.get(id(eng), 0) + 1
            phase[id(eng)] = k
            eng.drain().then_inc(arrived, 1)
            eng.wait_ge(arrived, 4 * k)

        def load_const(eng, group, dst, src):
            eng.dma_start(dst, src).then_inc(S("const", group), 16)

        def const_ready(eng, group, count):
            eng.wait_ge(S("const", group), 16 * count)

        def raw_slot(n):
            return mod_raw[n] if n < N_MOD0 else w_raw[n % 2]

        def round_hi(act, n, i=None):
            r, more = n % 2, (0 if i is None else i)
            if n < N_MOD0:
                act.wait_ge(mod_landed[n], 16)
            else:
                act.wait_ge(landed[r], (more + ((n - N_MOD0) // 2 + 1)) * 16)
            if n >= 2:
                act.wait_ge(w_used, more * 2 + (n - 1))
            nc.scalar.activation(w_hi[r][:, :], raw_slot(n)[:, :], ACT.Copy).then_inc(wh_ready, 1)

        def take_lo(dve, n, i=None):
            r, more = n % 2, (0 if i is None else i)
            dve.wait_ge(wh_ready, more * 2 + (n + 1))
            nc.vector.tensor_tensor(w_lo[r][:, :], raw_slot(n)[:, :], w_hi[r][:, :].bitcast(F32),
                                    ALU.subtract).then_inc(wl_ready, 1)

        def weights(pe, n, i=None):
            pe.wait_ge(wl_ready, (0 if i is None else i) * 2 + (n + 1))

        def split_mm(outs, wh, wl, xs, start, stop):
            last = None
            for o, (xh, _) in zip(outs, xs):
                nc.tensor.matmul(o, wh, xh, start=start, stop=False)
            for o, (_, xl) in zip(outs, xs):
                nc.tensor.matmul(o, wh, xl, start=False, stop=False)
            for o, (xh, _) in zip(outs, xs):
                last = nc.tensor.matmul(o, wl, xh, start=False, stop=stop)
            return last

        def feature_slot(ns, n, tok, between=lambda step: None, pair=2):
            b, r = 3 * (ns % 2), n % 2
            last = None
            for mt in range(pair):
                for k in range(KD):
                    cols = slice(k * 256 + mt * P, k * 256 + mt * P + P)
                    outs = [PS[:, b + mt, :]]
                    xs = [(HTh[:, k, 0:LAT], HTl[:, k, 0:LAT])]
                    if tok > LAT:
                        outs.append(PS[:, b + 2, mt * 256:mt * 256 + 256])
                        xs.append((HTh[:, k, LAT:TOK], HTl[:, k, LAT:TOK]))
                    between(mt * KD + k)
                    last = split_mm(outs, w_hi[r][:, cols], w_lo[r][:, cols], xs, k == 0, k == KD - 1)
            return last

        def token_slot(ns, n, tiles, width, between=lambda step: None):
            b, r = 3 * (ns % 2), n % 2
            last = None
            for t in range(tiles):
                o = PS[:, b + t // 2, (t % 2) * 256:(t % 2) * 256 + width]
                for k in range(KD):
                    between(t * KD + k)
                    wc = slice(k * 256, k * 256 + width)
                    xh, xl = HTh[:, k, t * P:(t + 1) * P], HTl[:, k, t * P:(t + 1) * P]
                    nc.tensor.matmul(o, xh, w_hi[r][:, wc], start=k == 0, stop=False)
                    nc.tensor.matmul(o, xh, w_lo[r][:, wc], start=False, stop=False)
                    last = nc.tensor.matmul(o, xl, w_hi[r][:, wc], start=False, stop=k == KD - 1)
            return last

        def s4_wide(k):
            return s4[:, 4 * k:4 * k + S4W]

        def w_load(sp, n, i=None):
            r, more = n % 2, (0 if i is None else i)
            if n >= N_MOD0 + 2:
                sp.wait_ge(wl_ready, more * 2 + (n - 1))
            src = wpack[n] if i is None else wpack[bass.ds(i * 2 + n, 1)].rearrange("a p c -> (a p) c")
            sp.dma_start(w_raw[r][:, :], src).then_inc(landed[r], 16)

        def m_load(sp, q, i=None, step=0):
            r, more = q % 2, (0 if i is None else i)
            if q >= 2:
                sp.wait_ge(m_used, more * step + (q - 1))
            src = modw[q] if i is None else modw[bass.ds(i * step + q, 1)].rearrange("a p c -> (a p) c")
            sp.dma_start(m_raw[r][:, :], src).then_inc(m_landed[r], 16)

        def m_round(act, q, i=None):
            r, more = q % 2, (0 if i is None else i)
            act.wait_ge(m_landed[r], more * 64 + 16 * (q // 2 + 1))
            if q >= 2:
                act.wait_ge(m_used, more * 8 + (q - 1))
            nc.scalar.activation(m_hi[r][:, :], m_raw[r][:, :], ACT.Copy).then_inc(m_hi_ready, 1)

        def m_split(dve, q, i=None):
            r, more = q % 2, (0 if i is None else i)
            dve.wait_ge(m_hi_ready, more * 8 + (q + 1))
            nc.vector.tensor_tensor(m_lo[r][:, :], m_raw[r][:, :], m_hi[r][:, :].bitcast(F32), ALU.subtract)\
                .then_inc(m_lo_ready, 1)

        def m_product(pe, q, i=None):
            r, k, more = q % 2, q % KD, (0 if i is None else i)
            pe.wait_ge(m_lo_ready, more * 8 + (q + 1))
            if k == 0:
                pe.wait_ge(m_row_ready, more + (q // KD + 4))
            nc.tensor.matmul(PS[0:S4W, MODBANK, :], s4_wide(k), m_hi[r][:, :], start=k == 0, stop=False)
            nc.tensor.matmul(PS[0:S4W, MODBANK, :], s4_wide(k), m_lo[r][:, :], start=False, stop=k == KD - 1)\
                .then_inc(m_used, 1)

        def m_turn(pe, g, i=None):
            more = 0 if i is None else i
            pe.wait_ge(m_row_ready, more + (g + 1))
            if g > 0:
                pe.wait_ge(m_evac, more + g)
            for j in range(4):
                last = nc.tensor.matmul(PS[:, SELBANK, 2 * j:2 * j + 2], m_row[0:4, j * P:(j + 1) * P], sel[0:4, :],
                                        start=True, stop=True)
            last.then_inc(m_sel_ready, 1)

        def first_bank(g):
            return (MODBANK, 0)[g % 2]

        def m_rows(dve, g, i=None, bank=MODBANK):
            more = 0 if i is None else i
            if g < N_MOD0 // 2:
                dve.wait_ge(w_used, 2 * g + 2)
            else:
                dve.wait_ge(m_used, more * 8 + (g - 3) * KD)
            if g > 0:
                dve.wait_ge(m_sel_ready, more + g)
            nc.vector.tensor_copy(m_row[0:4, :], PS[0:4, bank, :]).then_inc(m_row_ready, 1)

        def m_columns(dve, g, i=None):
            more = 0 if i is None else i
            dve.wait_ge(m_sel_ready, more + (g + 1))
            layer, c0 = g // MODG, 4 * (g % MODG)
            cs = slice(c0, c0 + 4) if i is None else bass.ds(i * 4 + c0, 4)
            nc.vector.tensor_tensor(modc[:, layer, cs, :], PS[:, SELBANK, 0:8].rearrange("p (m s) -> p m s", s=2),
                                    modb_sb[:, layer, cs].unsqueeze(2).to_broadcast([P, 4, 2]), ALU.add).then_inc(m_evac, 1)

        TRB = ((3, 4), (5, 7))

        def pre_bank(k, s):
            return PS[:, TRB[k % 2][s], :]

        def power(pool, st, col, done="rstd", count=1):
            pool.wait_ge(S(st, "mean"), count)
            nc.gpsimd.tensor_tensor(col, col, halfneg[:, 0:col.shape[1]], ALU.pow).then_inc(S(st, done), 1)

        def prenorm_gain(dve, layer, which):
            o = 3 * which
            nc.vector.scalar_tensor_tensor(
                out=prescale[:, :, :], in0=modc[:, layer, (o + 1) * KD:(o + 2) * KD, :], scalar=1.0,
                in1=ng[:, layer, 2 * which, :].unsqueeze(2).to_broadcast([P, KD, 2]), op0=ALU.add, op1=ALU.mult)

        def pre_mean(dve, st, t):
            dve.wait_ge(S(st, "ssq"), since(st, "ssq") + t + 1)
            nc.vector.tensor_scalar(rstd[:, 8 + t:9 + t], ssq[:, 16 + t:17 + t], 1.0 / D, EPS, ALU.mult, ALU.add)\
                .then_inc(S(st, "mean"), 1)

        def pre_xn(dve, st, t):
            dve.wait_ge(S(st, "rstd"), since(st, "rstd") + t + 1)
            nc.vector.tensor_scalar(xn[:, t, :], X[:, t, :], rstd[:, 8 + t:9 + t], None, ALU.mult)\
                .then_inc(S(st, "xn"), 1)

        def prenorm_dve(dve, st, layer, which, tiles):
            o, w = 3 * which, tiles * P
            for k in range(KD):
                dve.wait_ge(S(st, "tr"), since(st, "tr") + k + 1)
                if k >= 4:
                    dve.wait_ge(S(st, "hi"), since(st, "hi") + k - 3)
                    low = "lo_odd" if k % 2 else "lo_even"
                    dve.wait_ge(S(st, low), since(st, low) + k // 2 - 1)
                tmp = pre_tmp[k % 4]
                for s, (a, b) in enumerate(((0, LAT), (LAT, w))[:1 + (w > LAT)]):
                    last = nc.vector.tensor_scalar(tmp[:, a:b], pre_bank(k, s)[:, 0:b - a], prescale[:, k, s:s + 1],
                                                   modc[:, layer, o * KD + k, s:s + 1], ALU.mult, ALU.add)
                last.then_inc(S(st, "aff"), 1)
                if k % 2 == 1:
                    j = k - 1
                    dve.wait_ge(S(st, "hi"), since(st, "hi") + k)
                    nc.vector.tensor_tensor(HTl[:, j, 0:w], pre_tmp[j % 4][:, 0:w], HTh[:, j, 0:w].bitcast(F32),
                                            ALU.subtract).then_inc(S(st, "lo_even"), 1)

        def prenorm_pool(pool, st, tiles):
            w = tiles * P
            for t in range(tiles):
                pool.wait_ge(S(st, "mean"), since(st, "mean") + t + 1)
                nc.gpsimd.tensor_tensor(rstd[:, 8 + t:9 + t], rstd[:, 8 + t:9 + t], halfneg[:, 0:1], ALU.pow)\
                    .then_inc(S(st, "rstd"), 1)
            for k in range(1, KD, 2):
                pool.wait_ge(S(st, "hi"), since(st, "hi") + k + 1)
                nc.gpsimd.tensor_tensor(HTl[:, k, 0:w], pre_tmp[k % 4][:, 0:w], HTh[:, k, 0:w].bitcast(F32),
                                        ALU.subtract).then_inc(S(st, "lo_odd"), 1)

        def prenorm_squares(act, st, tiles, scratch):
            for t in range(tiles):
                nc.scalar.activation(scratch[:, :], X[:, t, :], ACT.Square, accum_out=ssq[:, 16 + t:17 + t])\
                    .then_inc(S(st, "ssq"), 1)
                act.drain()

        def prenorm_act(act, st, tiles):
            w = tiles * P
            for k in range(KD):
                act.wait_ge(S(st, "aff"), since(st, "aff") + k + 1)
                nc.scalar.activation(HTh[:, k, 0:w], pre_tmp[k % 4][:, 0:w], ACT.Copy).then_inc(S(st, "hi"), 1)

        def pre_transposes(pe, st, k, tiles):
            if k == 0:
                pe.wait_ge(S(st, "xn"), since(st, "xn") + tiles)
            if k >= 2:
                pe.wait_ge(S(st, "aff"), since(st, "aff") + k - 1)
            for t in range(tiles):
                last = nc.tensor.transpose(pre_bank(k, t // LT)[:, t % LT * P:t % LT * P + P],
                                           xn[:, t, k * P:(k + 1) * P], ident[:, :])
            last.then_inc(S(st, "tr"), 1)

        def pre_step(pe, st, step, tiles):
            if step == 0:
                pre_transposes(pe, st, 0, tiles)
                pre_transposes(pe, st, 1, tiles)
            if step < KD:
                if step % 2:
                    pe.wait_ge(S(st, "lo_odd"), since(st, "lo_odd") + step // 2 + 1)
                else:
                    pe.wait_ge(S(st, "lo_even"), since(st, "lo_even") + step // 2 + 1)
                if step + 2 < KD:
                    pre_transposes(pe, st, step + 2, tiles)

        def out_ktiles(kt):
            per = (kt + 3) // 4
            return [(h * per + k // 4, k % 4, h, k) for h in range(2) for k in range(kt)]

        OUTB = (0, 1, 2, 6, 7, 3)

        def out_pe(pe, st, n0, kt, tiles, before=None):
            if before is not None:
                pe.wait_ge(S(before, "evac"), JF - 1)
            for q, (s, j, h, k) in enumerate(out_ktiles(kt)):
                n = n0 + s
                if j == 0:
                    weights(pe, n)
                if 2 <= q < 2 + len(gate_chunks(tiles)):
                    if q == 2 and before is not None:
                        pe.wait_ge(S(before, "evac"), JF)
                    pe.wait_ge(S(st, "diag"), since(st, "diag") + q - 1)
                    nc.tensor.matmul(PS[:, 4 + q % 2, :], ones[:, :], diag[:, :, :].rearrange("p a b -> p (a b)"),
                                     start=True, stop=True).then_inc(S(st, "row"), 1)
                if h == 1 and k == kt - 2:
                    continue
                steps = [(q, j, k, t) for t in range(tiles)]
                if h == 1 and k == kt - 1:
                    steps = sorted([(q - 1, j - 1, k - 1, t) for t in range(tiles)] + steps,
                                   key=lambda x: (x[3] + (3 if x[0] == q else 0), -x[0]))
                waited = set()
                for qq, jj, kk, t in steps:
                    if qq not in waited:
                        pe.wait_ge(S(st, "a_lo"), since(st, "a_lo") + qq + 1)
                        waited.add(qq)
                    if h == 1 and k == 0:
                        pe.wait_ge(S(st, "o_copy"), since(st, "o_copy") + t + 1)
                    if q == 0 and before is not None and OUTB[t] == 7:
                        pe.wait_ge(m_evac, 2 * MODG)
                    if q == 0 and before is not None and OUTB[t] == 3:
                        pe.wait_ge(S(before, "evac"), JF)
                    tc, o = slice(t * P, (t + 1) * P), PS[:, OUTB[t], :]
                    wc = slice(jj * 512, jj * 512 + 512)
                    ah, al = a_hi[qq % 2][:, tc], a_lo[qq % 2][:, tc]
                    nc.tensor.matmul(o, ah, w_hi[n % 2][:, wc], start=kk == 0, stop=False)
                    nc.tensor.matmul(o, ah, w_lo[n % 2][:, wc], start=False, stop=False)
                    last = nc.tensor.matmul(o, al, w_hi[n % 2][:, wc], start=False, stop=kk == kt - 1)
                    if kk == kt - 1:
                        last.then_inc(S(st, "acc"), 1)
                if k == kt - 1:
                    pe.drain().then_inc(S(st, "a_used"), 1 + h)
                else:
                    last.then_inc(S(st, "a_used"), 1)
                if j == 3 or k == kt - 1:
                    pe.drain().then_inc(w_used, 1)

        def part_hi(act, st, q, kt, tiles, A):
            k = q % kt
            nc.scalar.activation(a_hi[q % 2][:, 0:tiles * P], A[:, k, :], ACT.Copy).then_inc(S(st, "a_hi"), 1)

        def part_lo(dve, st, q, kt, tiles, A):
            dve.wait_ge(S(st, "a_hi"), since(st, "a_hi") + q + 1)
            nc.vector.tensor_tensor(a_lo[q % 2][:, 0:tiles * P], A[:, q % kt, :], a_hi[q % 2][:, 0:tiles * P].bitcast(F32),
                                    ALU.subtract).then_inc(S(st, "a_lo"), 1)

        def out_act(act, st, n0, kt, tiles, A, n_next, before=None):

            def square(h, t):
                act.wait_ge(S(st, "acc"), since(st, "acc") + h * tiles + t + 1)
                nc.scalar.activation(junk2[:, (t % 2) * 512:(t % 2) * 512 + 512], PS[:, OUTB[t], :], ACT.Square,
                                     accum_out=ssq[:, 2 * t + h:2 * t + h + 1]).then_inc(S(st, "ssq"), 1)
                if t % 2:
                    act.drain()
            for q, (s, j, h, k) in enumerate(out_ktiles(kt)):
                if q >= 2:
                    act.wait_ge(S(st, "a_used"), since(st, "a_used") + q - 1)
                if q >= 2 or before is None:
                    if before is not None and q == 2:
                        act.wait_ge(S(before, "evac"), JF)
                    part_hi(act, st, q, kt, tiles, A)
                if h == 1 and k == 0:
                    for t in range(tiles):
                        square(0, t)
                if j == 1:
                    if s + 1 < 2 * ((kt + 3) // 4):
                        round_hi(act, n0 + s + 1)
                    elif n_next is not None:
                        round_hi(act, n_next)
            return lambda t: square(1, t)

        def out_then_norm_act(act, square, st, sp, tiles):
            for t in range(tiles + 3):
                if t < tiles:
                    square(t)
                if t >= 3:
                    act.wait_ge(S(st, "x"), since(st, "x") + t - 2)
                    nc.scalar.activation(junk3[:, :], X[:, t - 3, :], ACT.Square, accum_out=ssq[:, 13 + t:14 + t])\
                        .then_inc(S(sp, "ssq"), 1)
                if 5 <= t < 7:
                    act.wait_ge(S(sp, "rstd"), since(sp, "rstd") + t - 4)
                    nc.scalar.activation(xn[:, t - 5, :], X[:, t - 5, :], ACT.Copy, scale=rstd[:, 3 + t:4 + t])\
                        .then_inc(S(sp, "xn"), 1)
                act.drain()

        def out_dve(dve, st, n0, kt, tiles, A, layer, which, n_next, before=None):
            gate = 3 * which + 2
            nc.vector.tensor_tensor(gmcol[:, :, :], modc[:, layer, gate * KD:(gate + 1) * KD, :],
                                    ng[:, layer, 2 * which + 1, :].unsqueeze(2).to_broadcast([P, KD, 2]), ALU.mult)
            chunks = gate_chunks(tiles)

            def gate_row(c):
                if 1 <= c <= len(chunks):
                    s, half = chunks[c - 1]
                    dve.wait_ge(S(st, "row"), since(st, "row") + c)
                    nc.vector.tensor_copy(gmB[:, s, half * 512:half * 512 + 512], PS[:, 4 + (c - 1) % 2, :])
                if 0 <= c < len(chunks):
                    s, half = chunks[c]
                    dve.drain()
                    nc.vector.tensor_tensor(
                        diag[:, :, :], ident[:, :].unsqueeze(1).to_broadcast([P, 4, P]),
                        gmcol[:, 4 * half:4 * half + 4, s:s + 1].to_broadcast([P, 4, P]), ALU.mult)\
                        .then_inc(S(st, "diag"), 1)

            def gated(h, t):
                dve.wait_ge(S(st, "ssq"), since(st, "ssq") + h * tiles + t + 1)
                cols = slice(h * 512, h * 512 + 512)
                nc.vector.tensor_tensor(O[:, t, cols], PS[:, OUTB[t], :], gmB[:, 0 if t < LT else 1, cols], ALU.mult)\
                    .then_inc(S(st, "o_copy"), 1)
                if h == 1:
                    nc.vector.tensor_scalar(rstd[:, t:t + 1], ssq[:, 2 * t + 1:2 * t + 2], ssq[:, 2 * t:2 * t + 1],
                                            1.0 / D, ALU.add, ALU.mult).then_inc(S(st, "mean"), 1)

            for q, (s, j, h, k) in enumerate(out_ktiles(kt)):
                gate_row(q - 2)
                if q >= 2 or before is None:
                    part_lo(dve, st, q, kt, tiles, A)
                if h == 1 and k == 0:
                    for t in range(tiles):
                        gated(0, t)
                    part = ssq[:, 0:2 * tiles].rearrange("p (t h) -> p t h", h=2)[:, :, 0]
                    nc.vector.tensor_scalar(part, part, EPS * D, None, ALU.add)
                    dve.drain()
                if j == 1:
                    if s + 1 < 2 * ((kt + 3) // 4):
                        take_lo(dve, n0 + s + 1)
                    elif n_next is not None:
                        take_lo(dve, n_next)
            if which == 0:
                prenorm_gain(dve, layer, 1)
            elif layer == 0:
                prenorm_gain(dve, 1, 0)
            dve.drain()

            def tail(t):
                if t < tiles:
                    gated(1, t)
                if 2 <= t < tiles + 2:
                    t -= 2
                    dve.wait_ge(S(st, "rstd"), since(st, "rstd") + t + 1)
                    nc.vector.scalar_tensor_tensor(out=X[:, t, :], in0=O[:, t, :], scalar=rstd[:, t:t + 1],
                                                   in1=X[:, t, :], op0=ALU.mult, op1=ALU.add).then_inc(S(st, "x"), 1)
            return tail

        def out_pool(pool, st, tiles):
            for t in range(tiles):
                pool.wait_ge(S(st, "mean"), since(st, "mean") + t + 1)
                nc.gpsimd.tensor_tensor(rstd[:, t:t + 1], rstd[:, t:t + 1], halfneg[:, 0:1], ALU.pow)\
                    .then_inc(S(st, "rstd"), 1)

        def out_then_norm_dve(dve, tail, sp, layer, which, tiles):
            for t in range(tiles + 4):
                tail(t)
                if t >= 4:
                    pre_mean(dve, sp, t - 4)
                if t >= 7:
                    pre_xn(dve, sp, t - 5)
            pre_xn(dve, sp, tiles - 1)
            prenorm_dve(dve, sp, layer, which, tiles)

        def ffn_grans(ns, q0, i=None):
            if q0 is None or ns == 0 or (isinstance(i, int) and ns + 2 * i >= 20):
                return []
            return list(range(q0, q0 + 8)) if ns == 1 else list(range(q0 + 8 + 4 * (ns - 2), q0 + 8 + 4 * (ns - 2) + 4))

        def ffn_pe(pe, st, n0, tok, q0, g0, norm):
            def slot(ns, i=None):
                n = n0 + ns
                weights(pe, n, i)
                if ns >= 2:
                    pe.wait_ge(S(st, "evac"), (0 if i is None else i * 2) + (ns - 1))
                grans = ffn_grans(ns, q0, i)
                places = (3, 4, 7, 8, 11, 12, 14, 15) if ns == 1 else (5, 7, 11, 13)

                def between(step):
                    if ns == 0:
                        pre_step(pe, norm, step, tok // P)
                    if grans and step in places:
                        m_product(pe, grans[places.index(step)], i)
                    if q0 is not None and step == 10 and ns == 2:
                        m_turn(pe, g0, i)
                feature_slot(ns, n, tok, between).then_inc(w_used, 1)
            slot(0)
            slot(1)
            with pe.Fori(0, JF // 2 - 2) as i:
                slot(2, i)
                slot(3, i)
            slot(2, JF // 2 - 2)
            slot(3, JF // 2 - 2)

        def ffn_act(act, st, layer, n0, tok, q0, after):
            def slot(u, i, last=False):
                y, b = yb[u % 2], 3 * (u % 2)
                u2 = u % 2
                round_hi(act, n0 + u + 1, i=i)
                for q in ffn_grans(u, q0, i)[2:]:
                    m_round(act, q, i)
                ii = 0 if i is None else i
                act.wait_ge(S(st, "tap"), ii * 2 + (u + 1))
                act.wait_ge(w_used, ii * 2 + (n0 + u + 1))
                if last:
                    after()
                nc.scalar.activation(y[:, 0:LAT], PS[:, b, :], ACT.Identity, bias=cws[u2][:, 3:4], scale=cws[u2][:, 1:2])
                if tok > LAT:
                    nc.scalar.activation(y[:, LAT:TOK], PS[:, b + 2, 0:256], ACT.Identity, bias=cws[u2][:, 3:4],
                                         scale=cws[u2][:, 1:2])
                act.drain().then_inc(S(st, "mid"), 1)
                for q in ffn_grans(u + 1, q0, i)[:2]:
                    m_round(act, q, i)
                act.wait_ge(S(st, "conv"), ii * 2 + (u + 1))
                nc.scalar.activation(y[:, 0:tok], y[:, 0:tok], ACT.Silu).then_inc(S(st, "silu"), 1)
            slot(0, None)
            slot(1, None)
            with act.Fori(0, JF // 2 - 3) as i:
                slot(2, i)
                slot(3, i)
            for i in (JF // 2 - 3, JF // 2 - 2):
                slot(2, i)
                slot(3, i, i == JF // 2 - 2)

        def ffn_dve(dve, st, layer, n0, tok, A, q0, g0, after):
            def slot(u, i, last_slot=False):
                y, b, u2 = yb[u % 2], 3 * (u % 2), u % 2
                ii = 0 if i is None else i
                take_lo(dve, n0 + u + 1, i)
                for q in ffn_grans(u, q0, i)[2:]:
                    m_split(dve, q, i)
                if q0 is not None and u == 2:
                    m_columns(dve, g0, i)
                nc.vector.tensor_copy(cws[u2][:, :], cw[:, layer, bass.ds(ii * 2 + u, 1), :].rearrange("p a b -> p (a b)"))\
                    .then_inc(S(st, "tap"), 1)
                if last_slot:
                    after()
                dve.wait_ge(S(st, "mid"), ii * 2 + (u + 1))
                streams = ((0, LAT, PS[:, b, :]),) + (((LAT, TOK, PS[:, b + 2, 0:256]),) if tok > LAT else ())
                for w, dst, src in ((0, 1, 0), (2, 0, 1)):
                    for a, e, g in streams:
                        n = e - a - 1
                        last = nc.vector.scalar_tensor_tensor(
                            out=y[:, a + dst:a + dst + n], in0=g[:, src:src + n], scalar=cws[u2][:, w:w + 1],
                            in1=y[:, a + dst:a + dst + n], op0=ALU.mult, op1=ALU.add)
                    if w == 0:
                        dve.drain()
                last.then_inc(S(st, "conv"), 1)
                if u in (1, 3) and ffn_grans(u, q0, i):
                    m_rows(dve, g0 + u // 2, i)
                for q in ffn_grans(u + 1, q0, i)[:2]:
                    m_split(dve, q, i)
                dve.wait_ge(S(st, "silu"), ii * 2 + (u + 1))
                parts = ((0, LAT, PS[:, b + 1, :]),) + (((LAT, TOK, PS[:, b + 2, 256:512]),) if tok > LAT else ())
                for a, e, z in parts:
                    last = nc.vector.tensor_tensor(
                        A[:, bass.ds(ii * 2 + u, 1), a:e].rearrange("p a b -> p (a b)"), y[:, a:e], z, ALU.mult)
                last.then_inc(S(st, "evac"), 1)
            slot(0, None)
            slot(1, None)
            with dve.Fori(0, JF // 2 - 3) as i:
                slot(2, i)
                slot(3, i)
            for i in (JF // 2 - 3, JF // 2 - 2):
                slot(2, i)
                slot(3, i, i == JF // 2 - 2)

        def units(odd):
            lat = [(h, t, NT, 0) for h in range(HEADS) for t in range(LT)]
            return lat if odd else lat + [(h, t, 2, LT) for h in range(HEADS) for t in range(LT, NT)]

        def attn_pe(pe, st, odd, extra=lambda u: None):
            U = units(odd)
            PT, Pb, V = (PTo, Pod, Vod) if odd else (PTe, Pe, Vev)

            def q_transpose(u):
                h, t, nk, k0 = U[u]
                if u >= 1:
                    pe.wait_ge(S(st, "qTl"), u)
                nc.tensor.transpose(PS[:, 6, 0:P], Zq[:, t, h * P:(h + 1) * P], ident[:, :]).then_inc(S(st, "qtr"), 1)

            def scores(u):
                h, t, nk, k0 = U[u]
                if not odd:
                    pe.wait_ge(S(st, "qTl"), u + 1)
                if u >= 2:
                    pe.wait_ge(S(st, "exp"), u - 1)
                for a, e in (((0, 512), (512, 768)) if nk == NT else ((0, 256),)):
                    ks = slice(k0 * P + a, k0 * P + e)
                    o = PS[:, 2 * (u % 2) + a // 512, 0:e - a]
                    if odd:
                        qs = slice(t * P, (t + 1) * P)
                        r = slice(64 * (h % 2), 64 * (h % 2) + 64)
                        nc.tensor.matmul(o, QTn[:, h, qs], KTn[:, h, ks], start=True, stop=False)
                        last = nc.tensor.matmul(o, QRT[r, h // 2, qs], KRT[r, ks], start=False, stop=True)
                    else:
                        qh, ql = qTh[u % 2][:, :], qTl[u % 2][:, :]
                        nc.tensor.matmul(o, qh, KTh[:, h // 4, ks], start=True, stop=False)
                        nc.tensor.matmul(o, qh, KTl[:, h // 4, ks], start=False, stop=False)
                        last = nc.tensor.matmul(o, ql, KTh[:, h // 4, ks], start=False, stop=True)
                last.then_inc(S(st, "s"), 1)

            for u in range(2):
                if not odd:
                    q_transpose(u)
                scores(u)
            if not odd:
                q_transpose(2)
            for u, (h, t, nk, k0) in enumerate(U):
                pe.wait_ge(S(st, "p"), u + 1)
                if u >= 1:
                    pe.wait_ge(S(st, "pT"), u)
                for j in range(nk):
                    last = nc.tensor.transpose(ps2(4, TOK)[:, j * P:(j + 1) * P], Pb[u % len(Pb)][:, j * P:(j + 1) * P],
                                               ident[:, :])
                last.then_inc(S(st, "ptr"), 1)
                if u + 2 < len(U):
                    scores(u + 2)
                if u + 3 < len(U) and not odd:
                    q_transpose(u + 3)
                pe.wait_ge(S(st, "pT"), u + 1)
                if u >= 1:
                    pe.wait_ge(S(st, "ocopy"), u)
                for j in range(nk):
                    c = h * P if odd else (h // 4) * P
                    last = nc.tensor.matmul(PS[:, 7, 0:P], V[:, k0 + j, c:c + P], PT[u % 2][:, j * P:(j + 1) * P],
                                            start=j == 0, stop=j == nk - 1)
                last.then_inc(S(st, "o"), 1)
                extra(u)

        def attn_act(act, st, odd, scale, extra=lambda u: None):
            U = units(odd)
            PT, Pb = (PTo, Pod) if odd else (PTe, Pe)

            def q_copy(u):
                act.wait_ge(S(st, "qtr"), u + 1)
                if u >= 2:
                    act.wait_ge(S(st, "s"), u - 1)
                nc.scalar.activation(qTh[u % 2][:, :], PS[:, 6, 0:P], ACT.Copy).then_inc(S(st, "qT"), 1)

            def exps(u):
                nk = U[u][2]
                if u >= len(Pb):
                    act.wait_ge(S(st, "ptr"), u - len(Pb) + 1)
                act.wait_ge(S(st, "max"), u + 1)
                nc.scalar.activation(Pb[u % len(Pb)][:, 0:nk * P], ps2(2 * (u % 2), nk * P), ACT.Exp,
                                     bias=rmax[:, u % 2:u % 2 + 1], scale=scale,
                                     accum_out=rsum[:, u % 2:u % 2 + 1]).then_inc(S(st, "exp"), 1)
            if not odd:
                for u in range(3):
                    q_copy(u)
            exps(0)
            for u, (h, t, nk, k0) in enumerate(U):
                if u + 1 < len(U):
                    exps(u + 1)
                act.wait_ge(S(st, "ptr"), u + 1)
                if u >= 2:
                    act.wait_ge(S(st, "o"), u - 1)
                nc.scalar.activation(PT[u % 2][:, 0:nk * P], ps2(4, nk * P), ACT.Copy).then_inc(S(st, "pT"), 1)
                if u + 3 < len(U) and not odd:
                    q_copy(u + 3)
                extra(u)

        def attn_dve(dve, st, odd, scale, cat, extra):
            U = units(odd)
            Pb = Pod if odd else Pe

            def maxima(u):
                dve.wait_ge(S(st, "s"), u + 1)
                if u >= 2:
                    dve.wait_ge(S(st, "exp"), u - 1)
                m = rmax[:, u % 2:u % 2 + 1]
                nc.vector.reduce_max(m, ps2(2 * (u % 2), U[u][2] * P), AX_X)
                dve.drain()
                nc.vector.tensor_scalar(m, m, -scale, None, ALU.mult).then_inc(S(st, "max"), 1)

            def normalise(u):
                dve.wait_ge(S(st, "exp"), u + 1)
                sm, pr = rsum[:, u % 2:u % 2 + 1], Pb[u % len(Pb)][:, 0:U[u][2] * P]
                nc.vector.reciprocal(sm, sm)
                dve.drain()
                nc.vector.tensor_scalar(pr, pr, sm, None, ALU.mult).then_inc(S(st, "p"), 1)

            def q_low(u):
                if not odd and u < len(U):
                    dve.wait_ge(S(st, "qT"), u + 1)
                    nc.vector.tensor_tensor(qTl[u % 2][:, :], PS[:, 6, 0:P], qTh[u % 2][:, :].bitcast(F32), ALU.subtract)\
                        .then_inc(S(st, "qTl"), 1)
            q_low(0)
            maxima(0)
            q_low(1)
            maxima(1)
            q_low(2)
            normalise(0)
            for u, (h, t, nk, k0) in enumerate(U):
                if u + 1 < len(U):
                    normalise(u + 1)
                if u + 2 < len(U):
                    maxima(u + 2)
                extra(u)
                q_low(u + 3)
                dve.wait_ge(S(st, "o"), u + 1)
                nc.vector.tensor_copy(cat[:, 4 + h, t * P:(t + 1) * P], PS[:, 7, 0:P]).then_inc(S(st, "ocopy"), 1)

        def rotate(dve, x0, x1, cs, sn, tA, tB):
            nc.vector.tensor_tensor(tA, x1, sn, ALU.mult)
            nc.vector.tensor_tensor(tB, x0, sn, ALU.mult)
            nc.vector.tensor_tensor(x0, x0, cs, ALU.mult)
            nc.vector.tensor_tensor(x1, x1, cs, ALU.mult)
            dve.drain()
            nc.vector.tensor_tensor(x0, x0, tA, ALU.subtract)
            nc.vector.tensor_tensor(x1, x1, tB, ALU.add)
            dve.drain()

        block = es.enter_context(nc.Block())
        CLN = 24
        QK_SLOTS = (0, 2, 3, 4, 5)

        def qk_head(s, hh):
            return Kt[:, :, hh * P:hh * P + P] if s == 0 else Zq[:, :, (s - 2) * 256 + hh * P:(s - 2) * 256 + hh * P + P]

        @block.sync
        def _(sp):
            load_const(sp, "c", sT[:, :, :], cvec)
            for n in range(N_MOD0):
                if n == 4:
                    load_const(sp, "x", X[:, 0:LT, :], x.rearrange("(t p) d -> p t d", p=P))
                    load_const(sp, "x", X[:, LT:NT, :], ctx.rearrange("(t p) d -> p t d", p=P))
                sp.dma_start(mod_raw[n][:, :], wpack[n]).then_inc(mod_landed[n], 16)
            w_load(sp, EV0)
            w_load(sp, EV0 + 1)
            m_load(sp, 0)
            m_load(sp, 1)
            with sp.Fori(0, N_EVZ // 2) as i:
                for u in range(2):
                    w_load(sp, EV0 + 2 + u, i)
                    for r in range(8):
                        m_load(sp, 2 + 8 * u + r, i, 16)
            n = EV0 + 2 + N_EVZ
            with sp.Fori(0, (F10 + 2 - n) // 2) as i:
                for u in range(2):
                    w_load(sp, n + u, i)
            q = N_EVZ * KD + 2
            w_load(sp, F10 + 2)
            w_load(sp, F10 + 3)
            for r in range(8):
                m_load(sp, q + r)
            q += 8
            with sp.Fori(0, JF // 2 - 3) as i:
                for u in range(2):
                    w_load(sp, F10 + 4 + u, i)
                    for r in range(4):
                        m_load(sp, q + 4 * u + r, i, 8)
            n, q = F10 + JF - 2, q + 8 * (JF // 2 - 3)
            for u in range(2):
                w_load(sp, n + u)
                for r in range(4):
                    if q < NGRAN:
                        m_load(sp, q)
                    q += 1
            n += 2
            with sp.Fori(0, (NSLOT - n) // 2) as i:
                for u in range(2):
                    w_load(sp, n + u, i)
            if (NSLOT - n) % 2:
                w_load(sp, NSLOT - 1)
            for t in range(LT):
                sp.wait_ge(S("ffo1", "x"), since("ffo1", "x") + t + 1)
                sp.dma_start(out[t * P:(t + 1) * P, :], X[:, t, :]).then_inc(stored, 16)
            sp.wait_ge(stored, 16 * LT)

        @block.gpsimd
        def _(pool):
            nc.gpsimd.memset(ident[:, :], 0.0)
            nc.gpsimd.memset(ones[:, :], 1.0)
            nc.gpsimd.memset(halfneg[:, :], -0.5)
            pool.drain()
            nc.gpsimd.affine_select(out=ident[:, :], in_=ident[:, :], compare_op=ALU.not_equal, fill=1.0,
                                    base=0, pattern=[[-1, P]], channel_multiplier=1).then_inc(S("init", "ident"), 1)
            prenorm_pool(pool, "pre0", NT)
            barrier(pool)
            const_ready(pool, "ev", 4)
            for qk, s in enumerate(QK_SLOTS):
                power(pool, "evz", rstd[:, 12 * qk:12 * qk + 12], count=qk + 1)
                pool.wait_ge(S("evz", "xn"), qk + 1)
                pairs = [qk_head(s, hh)[:, 0:LT, :].rearrange("p t (i two) -> p t i two", two=2) for hh in range(2)]
                cs, sn = csn[:, 0, :, :], csn[:, 1, :, :]
                tA, tB = (z[:, :].rearrange("p (h t i) -> p h t i", h=2, i=64) for z in (sA, sB))
                for hh in range(2):
                    x0, x1 = pairs[hh][:, :, :, 0], pairs[hh][:, :, :, 1]
                    nc.gpsimd.tensor_tensor(tA[:, hh], x1, sn, ALU.mult)
                    nc.gpsimd.tensor_tensor(tB[:, hh], x0, sn, ALU.mult)
                    nc.gpsimd.tensor_tensor(x0, x0, cs, ALU.mult)
                    nc.gpsimd.tensor_tensor(x1, x1, cs, ALU.mult)
                pool.drain()
                for hh in range(2):
                    x0, x1 = pairs[hh][:, :, :, 0], pairs[hh][:, :, :, 1]
                    nc.gpsimd.tensor_tensor(x0, x0, tA[:, hh], ALU.subtract)
                    nc.gpsimd.tensor_tensor(x1, x1, tB[:, hh], ALU.add)
                pool.drain().then_inc(S("evz", "rope"), 1)
            power(pool, "vln", lnmv[:, :, 1])
            barrier(pool)
            for c in range(NT):
                pool.wait_ge(S("gate", "bias"), c + 1)
                cc = cat_ev[:, 0:4, c * P:(c + 1) * P]
                nc.gpsimd.tensor_tensor(cc, cc, sptmp[c % 2][:, :, :], ALU.mult).then_inc(S("gate", "gated"), 1)
            barrier(pool)
            barrier(pool)
            out_pool(pool, "evo", NT)
            prenorm_pool(pool, "pre1", NT)
            out_pool(pool, "ffo0", NT)
            prenorm_pool(pool, "pre2", NT)
            power(pool, "odq", rstd[:, 0:LT])
            power(pool, "odkv", rstd[:, 16:16 + NT])
            barrier(pool)
            barrier(pool)
            out_pool(pool, "odo", LT)
            prenorm_pool(pool, "pre3", LT)
            out_pool(pool, "ffo1", LT)

        @block.scalar
        def _(act):
            load_const(act, "mod", modb_sb[:, :, :], modb)
            load_const(act, "mod", ng[:, :, :, :], normg)
            load_const(act, "late", cw[:, :, :, :], ffcw)
            load_const(act, "late", ccw[:, :, :], odcw)
            load_const(act, "late", ccln[:, :, :], odcln)
            load_const(act, "late", gq[:, :], gcq)
            load_const(act, "late", gkv[:, :], gckv)
            const_ready(act, "c", 1)
            nc.scalar.activation(sT[:, :, :], sT[:, :, :], ACT.Silu)
            act.drain()
            nc.scalar.activation(s4v[:, :, 0:2], sT[:, :, :], ACT.Copy).then_inc(S("init", "silu"), 1)
            round_hi(act, 0)
            for n in range(1, N_MOD0):
                round_hi(act, n)
                if n == 5:
                    const_ready(act, "x", 2)
                    prenorm_squares(act, "pre0", NT, junk)
            round_hi(act, EV0)
            prenorm_act(act, "pre0", NT)
            m_round(act, 0)
            m_round(act, 1)
            barrier(act)
            load_const(act, "ev", csn[:, :, :, :], rope_ev)
            load_const(act, "ev", qkgb[:, :, :], qkg)
            load_const(act, "ev", bsb[:, :], bs)
            load_const(act, "ev", ws_sb[:, :], wsT)
            for s in range(N_EVZ):
                for q in (8 * s + 2, 8 * s + 3):
                    m_round(act, q)
                round_hi(act, EV0 + s + 1)
                for q in range(8 * s + 4, 8 * s + 8 + (2 if s + 1 < N_EVZ else 0)):
                    m_round(act, q)
                b = 3 * (s % 2)
                if s in QK_SLOTS:
                    qk = QK_SLOTS.index(s)
                    act.wait_ge(S("evz", "copy"), s + 1)
                    for t in range(NT):
                        for hh in range(2):
                            c = 12 * qk + 2 * t + hh
                            j4 = (2 * t + hh) % 4
                            nc.scalar.activation(Zv[:, 0, j4 * P:(j4 + 1) * P], qk_head(s, hh)[:, t, :], ACT.Square,
                                                 accum_out=ssq[:, c:c + 1])
                        if t % 2:
                            act.drain()
                    act.drain().then_inc(S("evz", "ssq"), 1)
                if s in (6, 7):
                    act.wait_ge(w_used, EV0 + s + 1)
                    for i in range(3):
                        nc.scalar.activation(Zv[:, 2 * i:2 * i + 2, (s - 6) * 256:(s - 6) * 256 + 256],
                                             PS[:, b + i, :].rearrange("p (a b) -> p a b", a=2), ACT.Gelu_apprx_tanh)
                    act.drain().then_inc(S("evz", "gelu"), 1)
                if s == 7:
                    act.wait_ge(S("evz", "rope"), len(QK_SLOTS))
                    load_const(act, "aln", alnb[:, :, :], aln)
                if s in (8, 9):
                    act.wait_ge(w_used, EV0 + s + 1)
                    for mt in range(2):
                        g = 2 * (s - 8) + mt
                        nc.scalar.activation(cat_ev[:, g, 0:LAT], PS[:, b + mt, :], ACT.Gelu_apprx_tanh)
                        nc.scalar.activation(cat_ev[:, g, LAT:TOK], PS[:, b + 2, mt * 256:mt * 256 + 256],
                                             ACT.Gelu_apprx_tanh)
            barrier(act)
            nc.scalar.activation(Vev[:, :, :], V32[:, :, :], ACT.Copy)
            for g in range(2):
                act.wait_ge(S("gate", "ktr"), g + 1)
                nc.scalar.activation(KTh[:, g, :], ps2(6, TOK), ACT.Copy).then_inc(S("gate", "kT"), 1)
            barrier(act)
            attn_act(act, "eva", False, P ** -0.5)
            barrier(act)
            square = out_act(act, "evo", EVO0, 12, NT, cat_ev, F10)
            out_then_norm_act(act, square, "evo", "pre1", NT)
            prenorm_act(act, "pre1", NT)

            def parts_0_1(st, stage, kt, tiles, A):
                act.wait_ge(S(stage, "evac"), 2)
                for q in range(2):
                    part_hi(act, st, q, kt, tiles, A)
            const_ready(act, "late", 5)
            ffn_act(act, "ff0", 0, F10, TOK, N_EVZ * KD, lambda: parts_0_1("ffo0", "ff0", JF, NT, A_ff))
            square = out_act(act, "ffo0", F20, JF, NT, A_ff, OD0, "ff0")
            out_then_norm_act(act, square, "ffo0", "pre2", NT)
            load_const(act, "csd", csd[:, :, :, :], rope_od)
            prenorm_act(act, "pre2", NT)
            for s in range(N_ODZ):
                round_hi(act, OD0 + s + 1)
                if s < 4:
                    act.wait_ge(w_used, OD0 + s + 1)
                    if s >= 2:
                        act.wait_ge(S("odz", "evac"), s - 1)
                    nc.scalar.activation(sg[s % 2][:, :], PS[:, 3 * (s % 2) + 1, :], ACT.Sigmoid)\
                        .then_inc(S("odz", "sg"), 1)
                if s == 6:
                    act.wait_ge(S("odz", "evac"), 6)
                    for t in range(LT):
                        nc.scalar.activation(sg[t % 2][:, :], zq[:, t, :], ACT.Square, accum_out=ssq[:, t:t + 1])
                        if t % 2:
                            act.drain()
                    act.drain().then_inc(S("odq", "ssq"), 1)
            act.wait_ge(S("odz", "evac"), 8)
            for t in range(NT):
                nc.scalar.activation(sg[t % 2][:, 0:256], zkv[:, t, 0:256], ACT.Square, accum_out=ssq[:, 16 + t:17 + t])
                if t % 2:
                    act.drain()
            act.drain().then_inc(S("odkv", "ssq"), 1)
            for k in range(6):
                act.wait_ge(S("odn", "aff"), k + 1)
                if k < 4:
                    nc.scalar.activation(cqh[:, k, :], ev_t[k % 2][:, 0:LAT], ACT.Copy).then_inc(S("odn", "hi"), 1)
                else:
                    nc.scalar.activation(ckh[:, k - 4, :], ev_t[k % 2][:, :], ACT.Copy).then_inc(S("odn", "hi"), 1)
                if k == 3:
                    round_hi(act, UQ0 + 1)
            round_hi(act, UQ0 + 2)
            for n in range(UKV0, UKV0 + 3):
                round_hi(act, n)
            barrier(act)

            def channel_norm(u):
                if u == CLN + 1:
                    for j in range(4):
                        act.wait_ge(S("cln", "cent"), j + 1)
                        nc.scalar.activation(sqs[j][:, :], cat_od[:, j, :], ACT.Square).then_inc(S("cln", "sq"), 1)
                if u == CLN + 4:
                    act.wait_ge(S("cln", "var"), 1)
                    nc.scalar.activation(nh_b[:, :], rs_b[:, :], ACT.Sqrt).then_inc(S("cln", "rstd"), 1)
                if u == CLN + 7:
                    for j in range(4):
                        act.wait_ge(S("cln", "nrm"), j + 1)
                        nc.scalar.activation(cat_od[:, j, :], cat_od[:, j, :], ACT.Silu, bias=ccln[:, j, 1:2],
                                             scale=ccln[:, j, 0:1])
            attn_act(act, "oda", True, 192 ** -0.5, channel_norm)
            barrier(act)
            square = out_act(act, "odo", ODO0, 12, LT, cat_od, F11)
            out_then_norm_act(act, square, "odo", "pre3", LT)
            prenorm_act(act, "pre3", LT)
            ffn_act(act, "ff1", 1, F11, LAT, None, lambda: parts_0_1("ffo1", "ff1", JF, LT, A_ff_lat))
            square = out_act(act, "ffo1", F21, JF, LT, A_ff_lat, None, "ff1")
            for t in range(LT):
                square(t)

        @block.tensor
        def _(pe):
            pe.wait_ge(S("init", "s4"), 1)
            for n in range(N_MOD0):
                g, r = n // 2, n % 2
                weights(pe, n)
                if r == 0 and g > 1:
                    pe.wait_ge(m_row_ready, g - 1)
                for kk in range(4):
                    k, cols = 4 * r + kk, slice(kk * 512, kk * 512 + 512)
                    nc.tensor.matmul(PS[0:S4W, first_bank(g), :], s4_wide(k), w_hi[r][:, cols], start=k == 0, stop=False)
                    last = nc.tensor.matmul(PS[0:S4W, first_bank(g), :], s4_wide(k), w_lo[r][:, cols], start=False,
                                            stop=k == KD - 1)
                last.then_inc(w_used, 1)
                if r == 0 and g > 0:
                    m_turn(pe, g - 1)
            m_turn(pe, N_MOD0 // 2 - 1)
            pe.wait_ge(m_evac, 4)
            for k in range(KD):
                pre_transposes(pe, "pre0", k, NT)
            pe.wait_ge(S("pre0", "lo_odd"), since("pre0", "lo_odd") + KD // 2)
            barrier(pe)
            for s in range(N_EVZ):
                n = EV0 + s
                weights(pe, n)
                if s >= 2:
                    if s - 2 < 6:
                        pe.wait_ge(S("evz", "copy"), s - 1)
                    else:
                        pe.wait_ge(S("evz", "gelu"), s - 7)
                places = (2, 8, 18, 24, 30, 36, 42, 47) if s < 8 else (1, 3, 5, 7, 9, 11, 12, 13)

                def between(step):
                    if step in places:
                        m_product(pe, 8 * s + places.index(step))
                    if 1 <= s and step == 2:
                        m_turn(pe, 3 + s)
                (feature_slot(s, n, TOK, between) if s >= 8 else token_slot(s, n, NT, 256, between)).then_inc(w_used, 1)
            m_turn(pe, 3 + N_EVZ)
            barrier(pe)
            for c in range(NT):
                for g in range(4):
                    last = nc.tensor.matmul(PS[:, c, g * P:(g + 1) * P], Zv[:, c, g * P:(g + 1) * P],
                                            ws_sb[:, g * P:(g + 1) * P], start=True, stop=True)
                last.then_inc(S("gate", "sp"), 1)
            for g in range(2):
                if g:
                    pe.wait_ge(S("gate", "kTl"), g)
                for t in range(NT):
                    last = nc.tensor.transpose(ps2(6, TOK)[:, t * P:(t + 1) * P], Kt[:, t, g * P:(g + 1) * P],
                                               ident[:, :])
                last.then_inc(S("gate", "ktr"), 1)
            barrier(pe)
            attn_pe(pe, "eva", False)
            barrier(pe)
            out_pe(pe, "evo", EVO0, 12, NT)
            ffn_pe(pe, "ff0", F10, TOK, N_EVZ * KD, 4 + N_EVZ, "pre1")
            out_pe(pe, "ffo0", F20, JF, NT, "ff0")
            for s in range(N_ODZ):
                n = OD0 + s
                weights(pe, n)
                if s >= 2:
                    pe.wait_ge(S("odz", "evac"), s - 1)
                if s < 4:
                    last = feature_slot(s, n, LAT, lambda step: pre_step(pe, "pre2", step, NT) if s == 0 else None)
                elif s < 6:
                    last = token_slot(s, n, LT, 256)
                else:
                    last = token_slot(s, n, NT, 160)
                last.then_inc(w_used, 1)
            pe.wait_ge(S("odz", "evac"), 8)
            pe.wait_ge(S("odq", "xn"), 1)
            for k in range(4):
                for t in range(LT):
                    last = nc.tensor.transpose(PS[:, 4 + k, t * P:(t + 1) * P], zq[:, t, k * P:(k + 1) * P], ident[:, :])
                last.then_inc(S("odn", "tr"), 1)
            pe.wait_ge(S("odkv", "xn"), 1)

            def key_transposes(k):
                if k == 4:
                    pe.wait_ge(S("odn", "aff"), 2)
                elif k == 5:
                    pe.wait_ge(S("odn", "aff"), 4)
                else:
                    pe.wait_ge(S("odn", "aff"), 5)
                for t in range(NT):
                    src = zkv[:, t, (k - 4) * P:(k - 3) * P] if k < 6 else kr2[:, t, :]
                    last = nc.tensor.transpose(ps2(4 + 2 * (k % 2), TOK)[:, t * P:(t + 1) * P], src, ident[:, :])
                last.then_inc(S("odn", "tr"), 1)
            key_transposes(4)
            key_transposes(5)
            pe.wait_ge(S("odn", "lo"), 4)
            for s in range(2):
                n = UQ0 + s
                weights(pe, n)
                for hh in range(4):
                    h = 4 * s + hh
                    if h >= 4:
                        pe.wait_ge(S("odu", "q"), h - 3)
                    for k in range(4):
                        cols = slice(k * 512 + hh * P, k * 512 + (hh + 1) * P)
                        last = split_mm([PS[:, h % 4, :]], w_hi[n % 2][:, cols], w_lo[n % 2][:, cols],
                                        [(cqh[:, k, :], cql[:, k, :])], k == 0, k == 3)
                    last.then_inc(S("odu", "qmm"), 1)
                    if h == 1:
                        key_transposes(6)
                pe.drain().then_inc(w_used, 1)
            n = UQ0 + 2
            weights(pe, n)
            pe.wait_ge(S("odn", "krt"), 1)
            for t in range(LT):
                for k in range(4):
                    wc, tc = slice(k * 512, k * 512 + 512), slice(t * P, (t + 1) * P)
                    nc.tensor.matmul(PS[:, 4 + t, :], cqh[:, k, tc], w_hi[n % 2][:, wc], start=k == 0, stop=False)
                    nc.tensor.matmul(PS[:, 4 + t, :], cqh[:, k, tc], w_lo[n % 2][:, wc], start=False, stop=False)
                    last = nc.tensor.matmul(PS[:, 4 + t, :], cql[:, k, tc], w_hi[n % 2][:, wc], start=False, stop=k == 3)
                last.then_inc(S("odu", "rmm"), 1)
            pe.drain().then_inc(w_used, 1)
            pe.wait_ge(S("odu", "q"), HEADS)
            for s in range(2):
                n = UKV0 + s
                weights(pe, n)
                for hh in range(4):
                    q = 4 * s + hh
                    if q >= 2:
                        pe.wait_ge(S("odk", "k"), q - 1)
                    b = 2 * (q % 2)
                    for k in range(2):
                        cols = slice(k * 1024 + hh * P, k * 1024 + (hh + 1) * P)
                        last = split_mm([PS[:, b, :], PS[:, b + 1, 0:256]], w_hi[n % 2][:, cols], w_lo[n % 2][:, cols],
                                        [(ckh[:, k, 0:LAT], ckl[:, k, 0:LAT]), (ckh[:, k, LAT:TOK], ckl[:, k, LAT:TOK])],
                                        k == 0, k == 1)
                    last.then_inc(S("odk", "kmm"), 1)
                for t in range(NT):
                    q = NT * s + t
                    if q < 4:
                        pe.wait_ge(S("odu", "qr"), q + 1)
                    if q >= 4:
                        pe.wait_ge(S("odk", "v"), q - 3)
                    o = PS[:, 4 + q % 4, :]
                    for k in range(2):
                        wc, tc = slice(k * 1024 + 512, k * 1024 + 1024), slice(t * P, (t + 1) * P)
                        nc.tensor.matmul(o, ckh[:, k, tc], w_hi[n % 2][:, wc], start=k == 0, stop=False)
                        nc.tensor.matmul(o, ckh[:, k, tc], w_lo[n % 2][:, wc], start=False, stop=False)
                        last = nc.tensor.matmul(o, ckl[:, k, tc], w_hi[n % 2][:, wc], start=False, stop=k == 1)
                    last.then_inc(S("odk", "vmm"), 1)
                pe.drain().then_inc(w_used, 1)
            pe.wait_ge(S("odu", "rope"), LT)
            pe.wait_ge(S("odk", "k"), HEADS)
            for p in range(4):
                for t in range(LT):
                    last = nc.tensor.transpose(PS[:, p, t * P:(t + 1) * P], QR[:, t, p * P:(p + 1) * P], ident[:, :])
                last.then_inc(S("odu", "rtr"), 1)
            barrier(pe)

            def channel_sums(u):
                if u == CLN:
                    pe.wait_ge(S("cln", "conv"), 1)
                    for j in range(4):
                        last = nc.tensor.matmul(PS[:, 6, :], ones[:, :], cat_od[:, j, :], start=j == 0, stop=j == 3)
                    last.then_inc(S("cln", "sum"), 1)
                if u == CLN + 2:
                    for j in range(4):
                        pe.wait_ge(S("cln", "sq"), j + 1)
                        last = nc.tensor.matmul(PS[:, 6, :], ones[:, :], sqs[j][:, :], start=j == 0, stop=j == 3)
                    last.then_inc(S("cln", "sum2"), 1)
            attn_pe(pe, "oda", True, channel_sums)
            barrier(pe)
            out_pe(pe, "odo", ODO0, 12, LT)
            ffn_pe(pe, "ff1", F11, LAT, None, None, "pre3")
            out_pe(pe, "ffo1", F21, JF, LT, "ff1")

        @block.vector
        def _(dve):
            const_ready(dve, "c", 1)
            dve.wait_ge(S("init", "silu"), 1)
            nc.vector.memset(s4[:, 4 * KD:].bitcast(F32), 0.0)
            nc.vector.tensor_tensor(s4v[:, :, 2:4], sT[:, :, :], s4v[:, :, 0:2].bitcast(F32), ALU.subtract)
            take_lo(dve, 0)
            dve.wait_ge(S("init", "ident"), 1)
            nc.vector.tensor_tensor(sel[0:4, :], ident[0:4, 0:2], ident[0:4, 2:4], ALU.add)
            dve.drain().then_inc(S("init", "s4"), 1)
            take_lo(dve, 1)
            const_ready(dve, "mod", 2)
            for g in range(N_MOD0 // 2):
                if g + 1 < N_MOD0 // 2:
                    take_lo(dve, 2 * g + 2)
                m_rows(dve, g, bank=first_bank(g))
                if g + 1 < N_MOD0 // 2:
                    take_lo(dve, 2 * g + 3)
                if g == 2:
                    const_ready(dve, "x", 2)
                    for t in range(NT + 1):
                        if t < NT:
                            pre_mean(dve, "pre0", t)
                        if t:
                            pre_xn(dve, "pre0", t - 1)
                m_columns(dve, g)
            dve.drain()
            prenorm_gain(dve, 0, 0)
            dve.drain()
            prenorm_dve(dve, "pre0", 0, 0, NT)
            take_lo(dve, EV0)
            m_split(dve, 0)
            m_split(dve, 1)
            barrier(dve)
            const_ready(dve, "ev", 4)
            def layer_norm(s, step):
                if s != N_EVZ - 1:
                    return
                for t in range(3 * (step % 2), 3 * (step % 2) + 3):
                    if step < 2:
                        nc.vector.tensor_scalar(Zv[:, t, :], Zv[:, t, :], lnmv[:, t, 0:1], lnmv[:, t, 1:2],
                                                ALU.subtract, ALU.mult)
                    else:
                        row, op = (0, ALU.mult) if step < 4 else (1, ALU.add)
                        nc.vector.tensor_tensor(Zv[:, t, :], Zv[:, t, :], alnb[:, row, :], op)
                dve.drain()
            for s in range(N_EVZ):
                m_split(dve, 8 * s + 2)
                m_split(dve, 8 * s + 3)
                layer_norm(s, 0)
                qk = QK_SLOTS.index(s - 1) if s - 1 in QK_SLOTS else None
                if qk is not None:
                    dve.wait_ge(S("evz", "ssq"), qk + 1)
                    nc.vector.tensor_scalar(rstd[:, 12 * qk:12 * qk + 12], ssq[:, 12 * qk:12 * qk + 12], 1.0 / P, EPS,
                                            ALU.mult, ALU.add).then_inc(S("evz", "mean"), 1)
                take_lo(dve, EV0 + s + 1)
                if s >= 1:
                    m_columns(dve, 3 + s)
                m_split(dve, 8 * s + 4)
                layer_norm(s, 1)
                m_split(dve, 8 * s + 5)
                layer_norm(s, 2)
                if qk is not None:
                    dve.wait_ge(S("evz", "rstd"), qk + 1)
                    for t in range(NT):
                        for hh in range(2):
                            z, c = qk_head(s - 1, hh)[:, t, :], 12 * qk + 2 * t + hh
                            last = nc.vector.scalar_tensor_tensor(out=z, in0=z, scalar=rstd[:, c:c + 1],
                                                                  in1=qkgb[:, 1 if s == 1 else 0, :], op0=ALU.mult,
                                                                  op1=ALU.mult)
                    last.then_inc(S("evz", "xn"), 1)
                m_split(dve, 8 * s + 6)
                layer_norm(s, 3)
                m_split(dve, 8 * s + 7)
                layer_norm(s, 4)
                m_rows(dve, 4 + s)
                if s + 1 < N_EVZ:
                    m_split(dve, 8 * s + 8)
                    m_split(dve, 8 * s + 9)
                b = 3 * (s % 2)
                if s < 6:
                    dve.wait_ge(w_used, EV0 + s + 1)
                    for i in range(3):
                        dst = (Kt if s == 0 else V32)[:, 2 * i:2 * i + 2, :] if s < 2 else \
                            Zq[:, 2 * i:2 * i + 2, (s - 2) * 256:(s - 1) * 256]
                        last = nc.vector.tensor_copy(dst, PS[:, b + i, :].rearrange("p (a b) -> p a b", a=2))
                    last.then_inc(S("evz", "copy"), 1)
                if s == 8:
                    dve.wait_ge(S("evz", "gelu"), 2)
                    for t in range(NT):
                        nc.vector.bn_stats(lnst[:, t, :], Zv[:, t, :])
                    dve.drain()
                    for t in range(NT):
                        nc.vector.bn_aggr(lnmv[:, t, :], lnst[:, t, :])
                    dve.drain()
                    nc.vector.tensor_scalar(lnmv[:, :, 1], lnmv[:, :, 1], 1.0, EPS, ALU.mult, ALU.add)\
                        .then_inc(S("vln", "mean"), 1)
                    dve.wait_ge(S("vln", "rstd"), 1)
                    const_ready(dve, "aln", 1)
            layer_norm(N_EVZ - 1, 5)
            m_columns(dve, 3 + N_EVZ)
            barrier(dve)
            for c in range(NT):
                dve.wait_ge(S("gate", "sp"), c + 1)
                if c >= 2:
                    dve.wait_ge(S("gate", "gated"), c - 1)
                nc.vector.tensor_tensor(sptmp[c % 2][:, :, :], PS[:, c, :].rearrange("p (g q) -> p g q", q=P),
                                        bsb[:, :].rearrange("p (g q) -> p g q", q=P), ALU.add)\
                    .then_inc(S("gate", "bias"), 1)
            for g in range(2):
                dve.wait_ge(S("gate", "kT"), g + 1)
                nc.vector.tensor_tensor(KTl[:, g, :], ps2(6, TOK), KTh[:, g, :].bitcast(F32), ALU.subtract)\
                    .then_inc(S("gate", "kTl"), 1)
            barrier(dve)
            attn_dve(dve, "eva", False, P ** -0.5, cat_ev, lambda u: None)
            barrier(dve)
            tail = out_dve(dve, "evo", EVO0, 12, NT, cat_ev, 0, 0, F10)
            out_then_norm_dve(dve, tail, "pre1", 0, 1, NT)
            const_ready(dve, "late", 5)

            def parts_0_1(st, kt, tiles, A):
                for q in range(2):
                    part_lo(dve, st, q, kt, tiles, A)
            ffn_dve(dve, "ff0", 0, F10, TOK, A_ff, N_EVZ * KD, 4 + N_EVZ, lambda: parts_0_1("ffo0", JF, NT, A_ff))
            tail = out_dve(dve, "ffo0", F20, JF, NT, A_ff, 0, 1, OD0, "ff0")
            out_then_norm_dve(dve, tail, "pre2", 1, 0, NT)

            done = [0]

            def conv_taps(n):
                for tap in range(done[0], min(done[0] + n, 31)):
                    for j in range(4):
                        g, w = G[:, j, tap:tap + LAT], ccw[:, j, tap:tap + 1]
                        if tap == 0:
                            nc.vector.tensor_scalar(cat_od[:, j, :], g, w, ccw[:, j, 31:32], ALU.mult, ALU.add)
                        else:
                            nc.vector.scalar_tensor_tensor(out=cat_od[:, j, :], in0=g, scalar=w, in1=cat_od[:, j, :],
                                                           op0=ALU.mult, op1=ALU.add)
                    dve.drain()
                done[0] = min(done[0] + n, 31)
            for s in range(N_ODZ):
                take_lo(dve, OD0 + s + 1)
                if s >= 4:
                    conv_taps((3, 4, 2, 1)[s - 4])
                if s == 7:
                    dve.wait_ge(S("odq", "ssq"), 1)
                    nc.vector.tensor_scalar(rstd[:, 0:LT], ssq[:, 0:LT], 1.0 / 512, EPS, ALU.mult, ALU.add)\
                        .then_inc(S("odq", "mean"), 1)
                    dve.wait_ge(S("odq", "rstd"), 1)
                    for t in range(LT):
                        last = nc.vector.tensor_scalar(zq[:, t, :], zq[:, t, :], rstd[:, t:t + 1], None, ALU.mult)
                    last.then_inc(S("odq", "xn"), 1)
                b = 3 * (s % 2)
                dve.wait_ge(w_used, OD0 + s + 1)
                if s == 0:
                    nc.vector.memset(G[:, :, 0:HALO], 0.0)
                    nc.vector.memset(G[:, :, HALO + LAT:], 0.0)
                if s < 4:
                    dve.wait_ge(S("odz", "sg"), s + 1)
                    nc.vector.tensor_tensor(G[:, s, HALO:HALO + LAT], PS[:, b, :], sg[s % 2][:, :], ALU.mult)\
                        .then_inc(S("odz", "evac"), 1)
                    if s == 3:
                        dve.drain()
                elif s < 6:
                    for i in range(2):
                        last = nc.vector.tensor_copy(zq[:, 2 * i:2 * i + 2, (s - 4) * 256:(s - 3) * 256],
                                                     PS[:, b + i, :].rearrange("p (a b) -> p a b", a=2))
                    last.then_inc(S("odz", "evac"), 1)
                else:
                    for i in range(3):
                        last = nc.vector.tensor_copy(zkv[:, 2 * i:2 * i + 2, (s - 6) * 160:(s - 5) * 160],
                                                     PS[:, b + i, :].rearrange("p (a b) -> p a b", a=2)[:, :, 0:160])
                    last.then_inc(S("odz", "evac"), 1)
            const_ready(dve, "csd", 1)
            dve.drain()
            for t in range(LT):
                kr = zkv[:, t, 256:320].rearrange("p (i two) -> p i two", two=2)
                rotate(dve, kr[:, :, 0], kr[:, :, 1], csd[:, 0, t, :], csd[:, 1, t, :], rA[:, 0:32], rB[:, 0:32])
            for half in range(2):
                nc.vector.tensor_copy(kr2[:, :, 64 * half:64 * half + 64], zkv[:, :, 256:320])
            dve.wait_ge(S("odkv", "ssq"), 1)
            nc.vector.tensor_scalar(rstd[:, 16:16 + NT], ssq[:, 16:16 + NT], 1.0 / 256, EPS, ALU.mult, ALU.add)\
                .then_inc(S("odkv", "mean"), 1)

            def scaled(k):
                dve.wait_ge(S("odn", "tr"), k + 1)
                if k >= 2:
                    dve.wait_ge(S("odn", "hi"), k - 1)
                w = LAT if k < 4 else TOK
                g = gq[:, k:k + 1] if k < 4 else gkv[:, k - 4:k - 3]
                src = PS[:, 4 + k, :] if k < 4 else ps2(4 + 2 * (k % 2), TOK)
                nc.vector.tensor_scalar(ev_t[k % 2][:, 0:w], src, g, None, ALU.mult).then_inc(S("odn", "aff"), 1)

            def low(k):
                w = LAT if k < 4 else TOK
                dve.wait_ge(S("odn", "hi"), k + 1)
                hi, lo = (cqh[:, k, :], cql[:, k, :]) if k < 4 else (ckh[:, k - 4, :], ckl[:, k - 4, :])
                nc.vector.tensor_tensor(lo, ev_t[k % 2][:, 0:w], hi.bitcast(F32), ALU.subtract)\
                    .then_inc(S("odn", "lo"), 1)
                dve.wait_ge(S("odn", "lo"), k + 1)
            scaled(0)
            dve.wait_ge(S("odkv", "rstd"), 1)
            for t in range(NT):
                last = nc.vector.tensor_scalar(zkv[:, t, 0:256], zkv[:, t, 0:256], rstd[:, 16 + t:17 + t], None, ALU.mult)
            last.then_inc(S("odkv", "xn"), 1)
            scaled(1)
            for k in range(2, 5):
                low(k - 2)
                scaled(k)
            low(3)
            take_lo(dve, UQ0 + 1)
            scaled(5)
            low(4)
            low(5)
            for h in range(2):
                dve.wait_ge(S("odu", "qmm"), h + 1)
                nc.vector.tensor_copy(QTn[:, h, :], PS[:, h % 4, :]).then_inc(S("odu", "q"), 1)
            dve.wait_ge(S("odn", "tr"), 7)
            nc.vector.tensor_copy(KRT[:, :], ps2(4, TOK)).then_inc(S("odn", "krt"), 1)
            for h in range(2, HEADS):
                conv_taps(1)
                if h == 4:
                    take_lo(dve, UQ0 + 2)
                dve.wait_ge(S("odu", "qmm"), h + 1)
                nc.vector.tensor_copy(QTn[:, h, :], PS[:, h % 4, :]).then_inc(S("odu", "q"), 1)
            take_lo(dve, UKV0)
            for t in range(LT):
                dve.wait_ge(S("odu", "rmm"), t + 1)
                nc.vector.tensor_copy(QR[:, t, :], PS[:, 4 + t, :]).then_inc(S("odu", "qr"), 1)
            dve.drain()
            for s in range(2):
                take_lo(dve, UKV0 + s + 1)
                for hh in range(4):
                    q = 4 * s + hh
                    dve.wait_ge(S("odk", "kmm"), q + 1)
                    nc.vector.tensor_copy(KTn[:, q, :], ps2(2 * (q % 2), TOK)).then_inc(S("odk", "k"), 1)
                    if q in (0, 1, 2, 3):
                        zz = QR[:, q, :].rearrange("p (h i two) -> p h i two", i=32, two=2)
                        rotate(dve, zz[:, :, :, 0], zz[:, :, :, 1], csd[:, 0, q, :].unsqueeze(1).to_broadcast([P, 8, 32]),
                               csd[:, 1, q, :].unsqueeze(1).to_broadcast([P, 8, 32]),
                               rA[:, :].rearrange("p (h i) -> p h i", i=32), rB[:, :].rearrange("p (h i) -> p h i", i=32))
                        dve.drain().then_inc(S("odu", "rope"), 1)
                    elif q == 6:
                        conv_taps(1)
                for t in range(NT):
                    q = NT * s + t
                    dve.wait_ge(S("odk", "vmm"), q + 1)
                    nc.vector.tensor_copy(Vod[:, t, 512 * s:512 * s + 512], PS[:, 4 + q % 4, :])\
                        .then_inc(S("odk", "v"), 1)
            for p in range(4):
                dve.wait_ge(S("odu", "rtr"), p + 1)
                nc.vector.tensor_copy(QRT[:, p, :], PS[:, p, :])
            barrier(dve)

            def conv_and_norm(u):
                if u < CLN and u * 3 % 5 < 3:
                    conv_taps(1)
                if u == CLN:
                    assert done[0] == 31
                    dve.drain().then_inc(S("cln", "conv"), 1)
                if u == CLN + 1:
                    dve.wait_ge(S("cln", "sum"), 1)
                    nc.vector.tensor_scalar(mu[:, :], PS[:, 6, :], 1.0 / 512, None, ALU.mult)
                    dve.drain()
                    for j in range(4):
                        nc.vector.tensor_tensor(cat_od[:, j, :], cat_od[:, j, :], mu[:, :], ALU.subtract)\
                            .then_inc(S("cln", "cent"), 1)
                if u == CLN + 3:
                    dve.wait_ge(S("cln", "sum2"), 1)
                    nc.vector.tensor_scalar(mu[:, :], PS[:, 6, :], 1.0 / 512, EPS, ALU.mult, ALU.add)
                    dve.drain()
                    nc.vector.reciprocal(rs_b[:, :], mu[:, :]).then_inc(S("cln", "var"), 1)
                if u == CLN + 5:
                    dve.wait_ge(S("cln", "rstd"), 1)
                    nc.vector.tensor_tensor(rs_b[:, :], nh_b[:, :], nh_b[:, :], ALU.mult)
                    dve.drain()
                    nc.vector.tensor_tensor(rs_b[:, :], rs_b[:, :], mu[:, :], ALU.mult)
                    dve.drain()
                    nc.vector.tensor_scalar(rs_b[:, :], rs_b[:, :], -0.5, 1.5, ALU.mult, ALU.add)
                    dve.drain()
                    nc.vector.tensor_tensor(rs_b[:, :], rs_b[:, :], nh_b[:, :], ALU.mult)
                    dve.drain()
                if u == CLN + 6:
                    for j in range(4):
                        nc.vector.tensor_tensor(cat_od[:, j, :], cat_od[:, j, :], rs_b[:, :], ALU.mult)\
                            .then_inc(S("cln", "nrm"), 1)
            attn_dve(dve, "oda", True, 192 ** -0.5, cat_od, conv_and_norm)
            barrier(dve)
            tail = out_dve(dve, "odo", ODO0, 12, LT, cat_od, 1, 0, F11)
            out_then_norm_dve(dve, tail, "pre3", 1, 1, LT)
            ffn_dve(dve, "ff1", 1, F11, LAT, A_ff_lat, None, None, lambda: parts_0_1("ffo1", JF, LT, A_ff_lat))
            tail = out_dve(dve, "ffo1", F21, JF, LT, A_ff_lat, 1, 1, None, "ff1")
            for t in range(LT + 2):
                tail(t)


def _slots_in(w, groups):
    out = []
    for cols in groups:
        s = np.zeros((P, KD, 256), w.dtype)
        s[:, :, :len(cols)] = w[:, cols].reshape(KD, P, len(cols)).transpose(1, 0, 2)
        out.append(s.reshape(P, SLOT))
    return out


def _slots_out(w):
    kt = w.shape[0] // P
    per = (kt + 3) // 4
    out = []
    for h in range(2):
        t = np.zeros((per * 4, P, 512), w.dtype)
        t[:kt] = w[:, h * 512:h * 512 + 512].reshape(kt, P, 512)
        out += [t[4 * i:4 * i + 4].transpose(1, 0, 2).reshape(P, SLOT) for i in range(per)]
    return out


def _k_cols(w, cols):
    kt = w.shape[0] // P
    return w[:, cols].reshape(kt, P, len(cols)).transpose(1, 0, 2).reshape(P, SLOT)


def _rope(d_rot):
    n = d_rot // 4
    freq = np.float32(10000.0) ** (-np.arange(n, dtype=np.float32) / np.float32(n))
    row = np.repeat(np.arange(LAT // 64, dtype=np.float32), 64)
    col = np.tile(np.arange(64, dtype=np.float32), LAT // 64)
    ang = np.concatenate([row[:, None] * freq, col[:, None] * freq], -1).astype(np.float32)
    cs = np.stack([np.cos(ang), np.sin(ang)]).astype(np.float32)
    return np.ascontiguousarray(cs.reshape(2, LT, P, d_rot // 2).transpose(2, 0, 1, 3))


def kernel(x, c, ctx, c_ctx, mod_w, mod_b, norm_g, ffn_w_in, ffn_conv_w, ffn_conv_b, ffn_w_out,
           ev_w_in, ev_a_ln, ev_w_s, ev_b_s, ev_qk_g, ev_w_out,
           od_w_in, od_conv_w, od_conv_b, od_c_ln, od_g_cq, od_g_ckv, od_w_uq, od_w_ukv, od_w_out):
    import concourse.bacc as _bacc
    from concourse.bass_utils import run_bass_kernel_spmd as _run

    def cols(a):
        a = np.asarray(a)
        return np.ascontiguousarray(np.moveaxis(a.reshape(*a.shape[:-1], -1, P), -1, 0))

    def spread(a):
        return np.ascontiguousarray(np.broadcast_to(np.asarray(a)[None], (P, *a.shape)))

    ev, od = np.asarray(ev_w_in[0]), np.asarray(od_w_in[0])
    r = np.arange
    mw = np.asarray(mod_w).reshape(2, KD, P, MODG, 512).transpose(0, 3, 1, 2, 4).reshape(2 * MODG, KD, P, 512)
    slots = [mw[g, 4 * i:4 * i + 4].transpose(1, 0, 2).reshape(P, SLOT) for g in range(4) for i in range(2)]
    slots += _slots_in(ev, [r(2048, 2304), r(2304, 2560)] + [r(1024 + 256 * i, 1280 + 256 * i) for i in range(4)]
                      + [r(512, 768), r(768, 1024), r(0, 256), r(256, 512)])
    slots += _slots_out(np.asarray(ev_w_out[0]))

    def ffn(layer):
        w = np.asarray(ffn_w_in[layer])
        return _slots_in(w, [np.concatenate([r(P * j, P * j + P), r(FF + P * j, FF + P * j + P)]) for j in range(JF)]) \
            + _slots_out(np.asarray(ffn_w_out[layer]))
    slots += ffn(0)
    slots += _slots_in(od, [np.concatenate([r(P * j, P * j + P), r(512 + P * j, 512 + P * j + P)]) for j in range(4)]
                       + [r(1024, 1280), r(1280, 1536), r(1536, 1696), r(1696, 1856)])
    uq, ukv = np.asarray(od_w_uq[0]), np.asarray(od_w_ukv[0])
    slots += [_k_cols(uq, np.concatenate([r(192 * h, 192 * h + P) for h in range(4 * s, 4 * s + 4)])) for s in range(2)]
    slots += [_k_cols(uq, np.concatenate([r(192 * h + P, 192 * h + 192) for h in range(HEADS)]))]
    slots += [_k_cols(ukv, np.concatenate([r(256 * h, 256 * h + P) for h in range(4 * s, 4 * s + 4)]
                                          + [r(256 * h + P, 256 * h + 256) for h in range(4 * s, 4 * s + 4)]))
              for s in range(2)]
    slots += _slots_out(np.asarray(od_w_out[0]))
    slots += ffn(1)
    cvec = np.stack([np.asarray(c)[0], np.asarray(c_ctx)]).reshape(2, KD, P).transpose(2, 1, 0)
    ffc = np.concatenate([np.asarray(ffn_conv_w), np.asarray(ffn_conv_b)[:, None]], 1)
    occ = np.concatenate([np.asarray(od_conv_w)[0], np.asarray(od_conv_b)], 0)
    arrays = dict(
        x=np.asarray(x)[0], ctx=np.asarray(ctx)[0], cvec=cvec, wpack=np.stack(slots), modw=mw[4:].reshape(NGRAN, P, 512),
        modb=cols(mod_b), normg=cols(norm_g),
        ffcw=cols(ffc).transpose(0, 1, 3, 2), rope_ev=_rope(128), rope_od=_rope(64),
        qkg=spread(np.asarray(ev_qk_g)[0]), aln=spread(np.asarray(ev_a_ln)[0]),
        wsT=np.asarray(ev_w_s)[0].transpose(2, 0, 1).reshape(P, 512),
        bs=spread(np.asarray(ev_b_s)[0].reshape(512)),
        odcw=cols(occ).transpose(0, 2, 1), odcln=cols(np.asarray(od_c_ln)[0]).transpose(0, 2, 1),
        gcq=cols(np.asarray(od_g_cq)[0]), gckv=cols(np.asarray(od_g_ckv)[0]),
    )
    arrays = {k: np.ascontiguousarray(v) for k, v in arrays.items()}
    nc = _bacc.Bacc("TRN2", target_bir_lowering=False, num_devices=1)
    args = [nc.dram_tensor(k, v.shape, mybir.dt.from_np(v.dtype), kind="ExternalInput").ap() for k, v in arrays.items()]
    args.append(nc.dram_tensor("out", (LAT, D), F32, kind="ExternalOutput").ap())
    build(nc, *args)
    got = _run(nc, [arrays], core_ids=[0])
    return got.results[0]["out"].reshape(1, LAT, D)
```
